# Optimizing a Trainium2 kernel written in Bass

```python
import jax
import jax.numpy as jnp
from jax import lax
import numpy as np

D_MODEL = 1024
BATCH = 1
SEQ = 1024
DEPTH = 2

GRID_W = 64
CTX_LEN = 256
N_MIXERS = 4
EPS = 1e-6
POOL_WINDOWS = (2, 4, 8, 16)
POOL_GROUPS = 4
POOL_GW = D_MODEL // POOL_GROUPS
LRU_WIDTH = D_MODEL
LRU_BLOCKS = 8
LRU_BW = LRU_WIDTH // LRU_BLOCKS
CONV_W = 4
LRU_C = 8.0
HEAD_DIM = 64
N_Q_HEADS = D_MODEL // HEAD_DIM
N_KV_HEADS = 4
Q_BLOCK = 128
ROPE_THETA = 10000.0
GMLP_HALF = 3 * D_MODEL
GMLP_GROUPS = 4
GMLP_GW = GMLP_HALF // GMLP_GROUPS
GMLP_CHUNK = 128
N_EXPERTS = 16
EXPERT_FF = D_MODEL
CAPACITY_FACTOR = 2

kernel_name = 'hybrid_interleaved_diffusion_block'

def _n_slots(m):
    return (DEPTH - m + N_MIXERS - 1) // N_MIXERS

def rms_norm(x, gain=None):
    xf = x.astype(jnp.float32)
    y = xf * lax.rsqrt(jnp.mean(xf * xf, axis=-1, keepdims=True) + EPS)
    if gain is not None:
        y = y * gain.astype(jnp.float32)
    return y.astype(x.dtype)

def layer_norm(x, g, b):
    xf = x.astype(jnp.float32)
    mu = jnp.mean(xf, axis=-1, keepdims=True)
    xc = xf - mu
    var = jnp.mean(xc * xc, axis=-1, keepdims=True)
    return (xc * lax.rsqrt(var + EPS) * g.astype(jnp.float32) + b.astype(jnp.float32)).astype(x.dtype)

def modulate(x, shift, scale):
    return rms_norm(x) * (1 + scale) + shift

def centred_window_mean(h, w):
    n = h.shape[1]
    cs = jnp.pad(jnp.cumsum(h.astype(jnp.float32), axis=1), ((0, 0), (1, 0), (0, 0)))
    t = jnp.arange(n)
    lo = jnp.clip(t - w // 2, 0, n)
    hi = jnp.clip(t + w - w // 2, 0, n)
    mean = (cs[:, hi] - cs[:, lo]) / (hi - lo).astype(jnp.float32)[None, :, None]
    return mean.astype(h.dtype)

def pool_mixer(h, w_pool, scale):
    b, n, d = h.shape
    hg = h.reshape(b, n, POOL_GROUPS, POOL_GW)
    pooled = jnp.stack([centred_window_mean(hg[:, :, g], w) for g, w in enumerate(POOL_WINDOWS)], axis=2) - hg
    y = jnp.einsum('bngc,gcd->bngd', pooled, w_pool).reshape(b, n, d)
    return y * scale

def centred_depthwise_conv(x, w, bias):
    n = x.shape[1]
    left = CONV_W // 2
    right = CONV_W - 1 - left
    xp = jnp.pad(x, ((0, 0), (left, right), (0, 0)))
    return sum(xp[:, k:k + n] * w[k] for k in range(CONV_W)) + bias

def _lin_combine(left, right):
    a1, b1 = left
    a2, b2 = right
    return a1 * a2, a2 * b1 + b2

def linear_scan(a, u, h0):
    a_cum, h = lax.associative_scan(_lin_combine, (a, u), axis=1)
    return h + a_cum * h0[:, None, :]

def rglru_gates(x, wa, ba, wx, bx, lam):
    b, n, w = x.shape
    xb = x.reshape(b, n, LRU_BLOCKS, LRU_BW)
    r = jax.nn.sigmoid((jnp.einsum('bnhi,hij->bnhj', xb, wa).reshape(b, n, w) + ba).astype(jnp.float32))
    i = jax.nn.sigmoid((jnp.einsum('bnhi,hij->bnhj', xb, wx).reshape(b, n, w) + bx).astype(jnp.float32))
    log_a = -LRU_C * r * jax.nn.softplus(-lam.astype(jnp.float32))
    a = jnp.exp(log_a)
    mult = jnp.sqrt(-jnp.expm1(2.0 * log_a))
    u = x.astype(jnp.float32) * i * mult
    return a, u

def rglru_mixer(h_lat, h_ctx, w_in, conv_w, conv_b, wa, ba, wx, bx, lam, w_out):
    def branches(h):
        z = h @ w_in
        y = jax.nn.gelu(z[..., :LRU_WIDTH])
        xr = centred_depthwise_conv(z[..., LRU_WIDTH:], conv_w, conv_b)
        return y, xr
    y_l, x_l = branches(h_lat)
    y_c, x_c = branches(h_ctx)
    zero = jnp.zeros((h_lat.shape[0], LRU_WIDTH), jnp.float32)
    out_l = 0.0
    out_c = 0.0
    for d in range(2):
        a_c, u_c = rglru_gates(x_c, wa[d], ba[d], wx[d], bx[d], lam[d])
        a_l, u_l = rglru_gates(x_l, wa[d], ba[d], wx[d], bx[d], lam[d])
        if d == 1:
            a_c, u_c, a_l, u_l = (jnp.flip(t, axis=1) for t in (a_c, u_c, a_l, u_l))
        hc = linear_scan(a_c, u_c, zero)
        hl = linear_scan(a_l, u_l, hc[:, -1])
        if d == 1:
            hc, hl = jnp.flip(hc, axis=1), jnp.flip(hl, axis=1)
        out_c = out_c + hc
        out_l = out_l + hl
    o_l = (out_l.astype(h_lat.dtype) * y_l) @ w_out
    o_c = (out_c.astype(h_ctx.dtype) * y_c) @ w_out
    return o_l, o_c

def rope_2d_tables(n):
    rows = n // GRID_W
    row = jnp.repeat(jnp.arange(rows), GRID_W).astype(jnp.float32)
    col = jnp.tile(jnp.arange(GRID_W), rows).astype(jnp.float32)
    n_freq = HEAD_DIM // 4
    inv = ROPE_THETA ** (-jnp.arange(n_freq, dtype=jnp.float32) / n_freq)
    ang = jnp.concatenate([row[:, None] * inv, col[:, None] * inv], axis=-1)
    return jnp.cos(ang), jnp.sin(ang)

def apply_rope(x, cos, sin):
    b, n, h, d = x.shape
    xp = x.astype(jnp.float32).reshape(b, n, h, d // 2, 2)
    x1, x2 = xp[..., 0], xp[..., 1]
    cs = cos[None, :, None, :]
    sn = sin[None, :, None, :]
    out = jnp.stack([x1 * cs - x2 * sn, x1 * sn + x2 * cs], axis=-1)
    return out.reshape(b, n, h, d).astype(x.dtype)

def attend(q, k, v):
    s = jnp.einsum('bqkgd,bskd->bkgqs', q, k, preferred_element_type=jnp.float32) * (HEAD_DIM ** -0.5)
    p = jax.nn.softmax(s, axis=-1).astype(v.dtype)
    return jnp.einsum('bkgqs,bskd->bqkgd', p, v)

def gqa_mixer(h_lat, h_ctx, w_qkv, q_gain, k_gain, w_o):
    b, n, _ = h_lat.shape
    n_ctx = h_ctx.shape[1]
    grp = N_Q_HEADS // N_KV_HEADS
    qd = N_Q_HEADS * HEAD_DIM
    kd = N_KV_HEADS * HEAD_DIM

    def project(h):
        t = h.shape[1]
        qkv = h @ w_qkv
        q = qkv[..., :qd].reshape(b, t, N_Q_HEADS, HEAD_DIM)
        k = qkv[..., qd:qd + kd].reshape(b, t, N_KV_HEADS, HEAD_DIM)
        v = qkv[..., qd + kd:].reshape(b, t, N_KV_HEADS, HEAD_DIM)
        return rms_norm(q, q_gain), rms_norm(k, k_gain), v

    q_l, k_l, v_l = project(h_lat)
    q_c, k_c, v_c = project(h_ctx)
    cos, sin = rope_2d_tables(n)
    q_l = apply_rope(q_l, cos, sin)
    k_l = apply_rope(k_l, cos, sin)
    k_all = jnp.concatenate([k_c, k_l], axis=1)
    v_all = jnp.concatenate([v_c, v_l], axis=1)
    q_blocks = q_l.reshape(b, n // Q_BLOCK, Q_BLOCK, N_KV_HEADS, grp, HEAD_DIM).transpose(1, 0, 2, 3, 4, 5)
    o_l = lax.map(lambda qb: attend(qb, k_all, v_all), q_blocks)
    o_l = o_l.transpose(1, 0, 2, 3, 4, 5).reshape(b, n, qd)
    o_c = attend(q_c.reshape(b, n_ctx, N_KV_HEADS, grp, HEAD_DIM), k_c, v_c).reshape(b, n_ctx, qd)
    return o_l @ w_o, o_c @ w_o

def gmlp_mixer(h, w_in, ln_g, ln_b, w_s, b_s, w_out):
    b, n, _ = h.shape
    z = jax.nn.gelu(h @ w_in)
    u, v = z[..., :GMLP_HALF], z[..., GMLP_HALF:]
    v = layer_norm(v, ln_g, ln_b).reshape(b, n // GMLP_CHUNK, GMLP_CHUNK, GMLP_GROUPS, GMLP_GW)
    v = jnp.einsum('gpq,bcqgf->bcpgf', w_s, v) + b_s.T[None, None, :, :, None]
    return (u * v.reshape(b, n, GMLP_HALF)) @ w_out

def expert_choice_ffn(h, w_router, w_gate, w_up, w_down):
    b, n, d = h.shape
    cap = CAPACITY_FACTOR * n // N_EXPERTS
    aff = jax.nn.softmax((h @ w_router).astype(jnp.float32), axis=-1)
    gates, idx = lax.top_k(jnp.swapaxes(aff, 1, 2), cap)
    xs = jax.vmap(lambda hb, ib: hb[ib])(h, idx)
    a = jnp.einsum('becd,edf->becf', xs, w_gate)
    up = jnp.einsum('becd,edf->becf', xs, w_up)
    y = jnp.einsum('becf,efd->becd', jax.nn.silu(a) * up, w_down) * gates.astype(h.dtype)[..., None]
    return jax.vmap(lambda ib, yb: jnp.zeros((n, d), yb.dtype).at[ib.reshape(-1)].add(yb.reshape(-1, d)))(idx, y)

def setup_inputs(seed: int = 0) -> dict:
    key = jax.random.key(seed)
    ks = iter(jax.random.split(key, 40))
    f32 = jnp.float32
    D = D_MODEL

    def nrm(shape, scale):
        return jax.random.normal(next(ks), shape, f32) * scale

    L0, L1, L2, L3 = (_n_slots(m) for m in range(N_MIXERS))
    u = jax.random.uniform(next(ks), (L1, 2, LRU_WIDTH), f32, 0.9, 0.999)
    a0 = u ** (1.0 / LRU_C)
    lru_lam = jnp.log(a0) - jnp.log1p(-a0)
    qkv_out = (N_Q_HEADS + 2 * N_KV_HEADS) * HEAD_DIM
    return {
        'x': nrm((BATCH, SEQ, D), 1.0),
        'c': nrm((BATCH, D), 1.0),
        'ctx': nrm((BATCH, CTX_LEN, D), 1.0),
        'c_ctx': nrm((D,), 1.0),
        'mod_w': nrm((DEPTH, D, 6 * D), 0.5 * D ** -0.5),
        'mod_b': nrm((DEPTH, 6 * D), 0.02),
        'pool_w': nrm((L0, POOL_GROUPS, POOL_GW, POOL_GW), POOL_GW ** -0.5),
        'pool_scale': 1.0 + nrm((L0, D), 0.02),
        'lru_w_in': nrm((L1, D, 2 * LRU_WIDTH), D ** -0.5),
        'lru_conv_w': nrm((L1, CONV_W, LRU_WIDTH), CONV_W ** -0.5),
        'lru_conv_b': nrm((L1, LRU_WIDTH), 0.02),
        'lru_wa': nrm((L1, 2, LRU_BLOCKS, LRU_BW, LRU_BW), LRU_BW ** -0.5),
        'lru_ba': nrm((L1, 2, LRU_WIDTH), 0.02),
        'lru_wx': nrm((L1, 2, LRU_BLOCKS, LRU_BW, LRU_BW), LRU_BW ** -0.5),
        'lru_bx': nrm((L1, 2, LRU_WIDTH), 0.02),
        'lru_lam': lru_lam,
        'lru_w_out': nrm((L1, LRU_WIDTH, D), LRU_WIDTH ** -0.5),
        'attn_w_qkv': nrm((L2, D, qkv_out), D ** -0.5),
        'attn_q_gain': 1.0 + nrm((L2, HEAD_DIM), 0.02),
        'attn_k_gain': 1.0 + nrm((L2, HEAD_DIM), 0.02),
        'attn_w_o': nrm((L2, N_Q_HEADS * HEAD_DIM, D), (N_Q_HEADS * HEAD_DIM) ** -0.5),
        'gmlp_w_in': nrm((L3, D, 2 * GMLP_HALF), D ** -0.5),
        'gmlp_ln_g': 1.0 + nrm((L3, GMLP_HALF), 0.02),
        'gmlp_ln_b': nrm((L3, GMLP_HALF), 0.02),
        'gmlp_w_s': nrm((L3, GMLP_GROUPS, GMLP_CHUNK, GMLP_CHUNK), GMLP_CHUNK ** -0.5),
        'gmlp_b_s': 1.0 + nrm((L3, GMLP_GROUPS, GMLP_CHUNK), 0.02),
        'gmlp_w_out': nrm((L3, GMLP_HALF, D), GMLP_HALF ** -0.5),
        'moe_router': nrm((DEPTH, D, N_EXPERTS), D ** -0.5),
        'moe_w_gate': nrm((DEPTH, N_EXPERTS, D, EXPERT_FF), D ** -0.5),
        'moe_w_up': nrm((DEPTH, N_EXPERTS, D, EXPERT_FF), D ** -0.5),
        'moe_w_down': nrm((DEPTH, N_EXPERTS, EXPERT_FF, D), EXPERT_FF ** -0.5),
        'final_gain': 1.0 + nrm((D,), 0.02),
    }

def reference(x, c, ctx, c_ctx, mod_w, mod_b, pool_w, pool_scale, lru_w_in, lru_conv_w, lru_conv_b,
              lru_wa, lru_ba, lru_wx, lru_bx, lru_lam, lru_w_out, attn_w_qkv, attn_q_gain, attn_k_gain,
              attn_w_o, gmlp_w_in, gmlp_ln_g, gmlp_ln_b, gmlp_w_s, gmlp_b_s, gmlp_w_out,
              moe_router, moe_w_gate, moe_w_up, moe_w_down, final_gain):
    xc = ctx
    silu_c = jax.nn.silu(c)
    silu_cc = jax.nn.silu(c_ctx)
    for i in range(DEPTH):
        m, j = i % N_MIXERS, i // N_MIXERS
        last = i == DEPTH - 1
        mod_l = (silu_c @ mod_w[i] + mod_b[i])[:, None, :]
        mod_c = (silu_cc @ mod_w[i] + mod_b[i])[None, None, :]
        sh1_l, sc1_l, g1_l, sh2_l, sc2_l, g2_l = jnp.split(mod_l, 6, axis=-1)
        sh1_c, sc1_c, g1_c, sh2_c, sc2_c, g2_c = jnp.split(mod_c, 6, axis=-1)
        h_l = modulate(x, sh1_l, sc1_l)
        need_ctx = (not last) or m in (1, 2)
        h_c = modulate(xc, sh1_c, sc1_c) if need_ctx else None
        o_c = None
        if m == 0:
            o_l = pool_mixer(h_l, pool_w[j], pool_scale[j])
            if not last:
                o_c = pool_mixer(h_c, pool_w[j], pool_scale[j])
        elif m == 1:
            o_l, o_c = rglru_mixer(h_l, h_c, lru_w_in[j], lru_conv_w[j], lru_conv_b[j], lru_wa[j], lru_ba[j],
                                   lru_wx[j], lru_bx[j], lru_lam[j], lru_w_out[j])
        elif m == 2:
            o_l, o_c = gqa_mixer(h_l, h_c, attn_w_qkv[j], attn_q_gain[j], attn_k_gain[j], attn_w_o[j])
        else:
            o_l = gmlp_mixer(h_l, gmlp_w_in[j], gmlp_ln_g[j], gmlp_ln_b[j], gmlp_w_s[j], gmlp_b_s[j], gmlp_w_out[j])
            if not last:
                o_c = gmlp_mixer(h_c, gmlp_w_in[j], gmlp_ln_g[j], gmlp_ln_b[j], gmlp_w_s[j], gmlp_b_s[j], gmlp_w_out[j])
        x = x + g1_l * o_l
        x = x + g2_l * expert_choice_ffn(modulate(x, sh2_l, sc2_l), moe_router[i], moe_w_gate[i], moe_w_up[i], moe_w_down[i])
        if not last:
            xc = xc + g1_c * o_c
            xc = xc + g2_c * expert_choice_ffn(modulate(xc, sh2_c, sc2_c), moe_router[i], moe_w_gate[i], moe_w_up[i], moe_w_down[i])
    return rms_norm(x, final_gain)


_drawn_inputs = setup_inputs


def setup_inputs(seed=0):
    import zlib

    import numpy as np

    out = dict(_drawn_inputs(seed))
    spreads = {}
    factors = {'pool_scale': 74.78,
     'lru_ba': 200.0,
     'lru_bx': 100.166,
     'final_gain': 22.761,
     'ctx': 56.464,
     'lru_conv_b': 8.092,
     'c_ctx': 3.74,
     'lru_wa': 4.515,
     'lru_wx': 2.982,
     'moe_router': 4.421,
     'moe_w_gate': 4.421,
     'moe_w_up': 4.124,
     'moe_w_down': 4.119}
    for name, (base, spread) in spreads.items():
        noise = np.random.default_rng([zlib.crc32(name.encode()), seed]).standard_normal(out[name].shape)
        drawn = base * np.exp(spread * noise) if base else spread * noise
        out[name] = jnp.asarray(drawn.astype(out[name].dtype))
    for name, factor in factors.items():
        out[name] = (out[name] * factor).astype(out[name].dtype)
    return out
```

```python
from contextlib import ExitStack, contextmanager

import concourse.bass as bass
from concourse import mybir

P = 128
D = 1024
KC = D // P
N_LAT, N_CTX = 1024, 256
T_LAT, T_CTX = N_LAT // P, N_CTX // P
TOK = N_LAT + N_CTX
EXPERTS = 16
SLOTS_LAT = 2 * N_LAT // EXPERTS
SLOTS_CTX = 2 * N_CTX // EXPERTS
WINDOWS = (2, 4, 8, 16)
EPS = 1e-6
RING = 4
CHUNK = 2048
MOD_CHUNKS = 6 * D // 256
EXP_CHUNKS = 12
LRU_COLS = 11
BANK = 512

PAD = 8
OFF_LAT = PAD
OFF_CTX = OFF_LAT + N_LAT + 2 * PAD
PADDED = OFF_CTX + N_CTX + PAD

F32 = mybir.dt.float32
F32R = mybir.dt.float32r
U32 = mybir.dt.uint32
ACT = mybir.ActivationFunctionType
ALU = mybir.AluOpType
AX = mybir.AxisListType.X
ds = bass.ds

V_C, V_CC, V_PS, V_FG, V_LRU = 0, 8, 16, 24, 32
N_VECS = V_LRU + LRU_COLS * KC


class Core:

    def __init__(self, nc, io, stack):
        self.nc, self.io, self.stack = nc, io, stack
        self.stage_sems, self.stale_sems = [], []
        self.chunks = 0
        def sb(name, shape, dt=F32):
            return stack.enter_context(nc.sbuf_tensor(name, shape, dt))

        def lasting(name):
            return stack.enter_context(nc.semaphore(name))

        self.h_lat = nc.dram_tensor("h_lat", [N_LAT, D], F32).ap()
        self.h_ctx = nc.dram_tensor("h_ctx", [N_CTX, D], F32).ap()
        self.x_lat = nc.dram_tensor("x_lat", [N_LAT, D], F32).ap()
        self.x_ctx = nc.dram_tensor("x_ctx", [N_CTX, D], F32).ap()
        self.x_fin = nc.dram_tensor("x_fin", [N_LAT, D], F32).ap()
        self.o_lru = nc.dram_tensor("o_lru", [D, N_LAT], F32).ap()
        self.raw = [sb(f"raw{i}", [P, CHUNK]) for i in range(RING)]
        self.ident = sb("ident", [P, P])
        self.ones = sb("ones", [P, P])
        self.vec = sb("vec", [P, N_VECS])
        self.mod_bias = sb("mod_bias", [P, 96])
        self.silu_c = sb("silu_c", [P, KC, 2])
        self.mod = [sb(f"mod{i}", [P, 96]) for i in range(2)]
        self.gate_t = sb("gate_t", [P, 48])
        self.index_t = sb("index_t", [P, 48], U32)
        self.unused = sb("unused", [P, 1])
        self.raw_landed = [lasting(f"raw_landed{i}") for i in range(RING)]
        self.rows_made = 0
        self.diag_ready, self.spread_ready, self.row_ready = (lasting(n) for n in ("diag_ready", "spread_ready", "row_ready"))
        self.placed = lasting("placed")
        self.chunk_done = lasting("chunk_done")

    def sem(self, name):
        self.stage_sems.append(self.nc.alloc_semaphore(name=name))
        return self.stage_sems[-1]

    @contextmanager
    def block(self):
        with self.nc.Block() as block:
            @block.gpsimd
            def _(pool):
                for sem in self.stale_sems:
                    pool.sem_clear(sem)
            yield block
        for sem in self.stale_sems:
            self.nc.release_semaphore(sem)
        self.stale_sems, self.stage_sems = self.stage_sems, []

    def mod_col(self, block, part, stream):
        return self.mod[block][:, 16 * part:16 * part + 16].rearrange("p (k s) -> p k s", s=2)[:, :, stream]


def wait(eng, sem, value):
    if isinstance(value, int) and value <= 0:
        return
    eng.wait_ge(sem, value)


def landed(core, eng, first, e=0, per=0):
    eng.wait_ge(core.raw_landed[first % RING], e * (16 * per // RING) + 16 * (first // RING + 1))


def load_chunk(core, sp, first, src, dst=None, e=0, per=0):
    sp.wait_ge(core.chunk_done, e * per + (first + 1))
    place = core.raw[first % RING]
    sp.dma_start(place[:] if dst is None else dst(place), src).then_inc(core.raw_landed[first % RING], 16)


def chunk_done(core, eng, first, e=0, per=0):
    eng.wait_ge(core.chunk_done, e * per + (RING + first + 1))


def pairs(engine, streams):
    yield 0, 0
    with engine.Fori(1, T_LAT // 2) as e:
        yield e, 0
    if streams == 2:
        yield T_LAT // 2, 1


def expert_chunk(io, block, s, e):
    if s < 8:
        w = io["moe_w_up" if s % 2 else "moe_w_gate"][block]
        return w.rearrange("e (k p) f -> p e k f", p=P)[:, ds(e, 1), :, 256 * (s // 2):256 * (s // 2) + 256]
    w = io["moe_w_down"][block]
    return w.rearrange("e (k p) f -> p e k f", p=P)[:, ds(e, 1), 2 * (s - 8):2 * (s - 8) + 2, :]



def setup(core):
    nc, io = core.nc, core.io
    with ExitStack() as st:
        rows = st.enter_context(nc.sbuf_tensor("vec_rows", [N_VECS, P], F32))
        brows = st.enter_context(nc.sbuf_tensor("modb_rows", [96, P], F32))
        turned = st.enter_context(nc.psum_tensor("turned", [P, 2, BANK], F32))
        rows_landed, made, turned_s, vec_ready, silu_ready = (
            core.sem(n) for n in ("rows_landed", "consts_made", "vecs_turned", "vec_ready", "silu_ready"))
        with core.block() as block:
            @block.sync
            def _(sp):
                sp.dma_start(rows[:], io["vecs"]).then_inc(rows_landed, 16)
                sp.dma_start(brows[:], io["mod_b"]).then_inc(rows_landed, 16)

            @block.gpsimd
            def _(pool):
                nc.gpsimd.memset(core.ident[:], 0.0).then_inc(made, 1)
                nc.gpsimd.memset(core.ones[:], 1.0).then_inc(made, 1)
                pool.wait_ge(made, 2)
                nc.gpsimd.affine_select(out=core.ident[:], in_=core.ident[:], compare_op=ALU.not_equal, fill=1.0,
                                        base=0, pattern=[[-1, P]], channel_multiplier=1).then_inc(made, 1)

            @block.tensor
            def _(pe):
                pe.wait_ge(rows_landed, 32)
                pe.wait_ge(made, 3)
                nc.tensor.transpose(turned[:, 0, 0:N_VECS], rows[:], core.ident[0:N_VECS, 0:N_VECS]).then_inc(turned_s, 1)
                nc.tensor.transpose(turned[:, 1, 0:96], brows[:], core.ident[0:96, 0:96]).then_inc(turned_s, 1)

            @block.vector
            def _(dve):
                dve.wait_ge(turned_s, 2)
                nc.vector.tensor_copy(core.vec[:], turned[:, 0, 0:N_VECS]).then_inc(vec_ready, 1)
                nc.vector.tensor_copy(core.mod_bias[:], turned[:, 1, 0:96]).then_inc(vec_ready, 1)

            @block.scalar
            def _(act):
                act.wait_ge(vec_ready, 1)
                nc.scalar.activation(core.silu_c[:, :, 0], core.vec[:, V_C:V_C + KC], ACT.Silu).then_inc(silu_ready, 1)
                nc.scalar.activation(core.silu_c[:, :, 1], core.vec[:, V_CC:V_CC + KC], ACT.Silu).then_inc(silu_ready, 1)


class Modulation:
    BODY = 2 * RING
    COLS = 4 * RING

    def __init__(self, core, block, banks):
        self.core, self.block, self.banks = core, block, banks
        self.first = core.chunks
        core.chunks += MOD_CHUNKS
        self.copied = core.sem(f"mod_copied{block}")
        self.ready = core.sem(f"mod_ready{block}")

    def bodies(self, engine):
        yield 0
        with engine.Fori(1, MOD_CHUNKS // self.BODY) as e:
            yield e

    def load(self, sp):
        w = self.core.io["mod_w"][self.block].rearrange("(k p) (c m) -> p k c m", p=P, m=256)
        for e in self.bodies(self.core.nc.sync):
            for i in range(self.BODY):
                load_chunk(self.core, sp, self.first + i, w[:, :, ds(e * self.BODY + i, 1), :],
                           lambda place: place[:].rearrange("p (k c m) -> p k c m", k=KC, c=1), e, self.BODY)

    def products(self, pe):
        core, nc = self.core, self.core.nc
        for e in self.bodies(nc.tensor):
            for i in range(self.BODY):
                half, at = divmod(i, RING)
                if at == 0:
                    wait(pe, self.copied, e * 2 + (half - 1))
                landed(core, pe, self.first + i, e, self.BODY)
                w = core.raw[(self.first + i) % RING][:].rearrange("p (k c m) -> p k c m", k=KC, c=2)
                for c in range(2):
                    col = 4 * at + 2 * c
                    for k in range(KC):
                        last = nc.tensor.matmul(self.banks[half][:, col:col + 2],
                                                w[:, k, c, :], core.silu_c[:, k, :], start=k == 0, stop=k == KC - 1)
                last.then_inc(core.chunk_done, 1)

    def copy_out(self, act):
        nc = self.core.nc
        for e in self.bodies(nc.scalar):
            for half in range(2):
                chunk_done(self.core, act, self.first + RING * (half + 1) - 1, e, self.BODY)
                nc.scalar.activation(self.core.mod[self.block][:, ds(e * (2 * self.COLS) + half * self.COLS, self.COLS)],
                                     self.banks[half][:, 0:self.COLS], ACT.Copy).then_inc(self.copied, 1)

    def finish(self, dve):
        core, nc = self.core, self.core.nc
        dve.wait_ge(self.copied, 2 * MOD_CHUNKS // self.BODY)
        out = core.mod[self.block][:].rearrange("p (c s) -> p c s", s=2)
        bias = core.mod_bias[:, 48 * self.block:48 * self.block + 48].unsqueeze(2).to_broadcast([P, 48, 2])
        nc.vector.tensor_tensor(out, out, bias, ALU.add).then_inc(self.ready, 1)
        dve.wait_ge(self.ready, 1)
        for part in (1, 4):
            cols = core.mod[self.block][:, 16 * part:16 * part + 16]
            nc.vector.tensor_scalar(cols, cols, 1.0, None, ALU.add).then_inc(self.ready, 1)


def modulation_stage(core, block):
    nc = core.nc
    with ExitStack() as st:
        mod = Modulation(core, block, [st.enter_context(nc.psum_tensor(f"mod_sums{i}", [P, BANK], F32)) for i in range(2)])
        with core.block() as blk:
            @blk.sync
            def _(sp):
                mod.load(sp)

            @blk.tensor
            def _(pe):
                mod.products(pe)

            @blk.scalar
            def _(act):
                mod.copy_out(act)

            @blk.vector
            def _(dve):
                nc.vector.memset(core.unused[:], 0.0).then_inc(core.chunk_done, RING)
                mod.finish(dve)


def broadcast_rows(core, name, wanted):
    nc = core.nc
    with ExitStack() as st:
        diag = [st.enter_context(nc.sbuf_tensor(f"{name}_diag{i}", [P, KC, P], F32)) for i in range(2)]
        spread = [st.enter_context(nc.psum_tensor(f"{name}_spread{i}", [P, 2, BANK], F32)) for i in range(2)]
        diag_ready, spread_ready, row_ready = core.diag_ready, core.spread_ready, core.row_ready
        base = core.rows_made
        core.rows_made += len(wanted)
        with core.block() as blk:
            @blk.vector
            def _(dve):
                for i, (_, col) in enumerate(wanted):
                    wait(dve, spread_ready, base + i - 1 if i > 1 else 0)
                    nc.vector.tensor_tensor(diag[i % 2][:], core.ident[:].unsqueeze(1).to_broadcast([P, KC, P]),
                                            col.unsqueeze(2).to_broadcast([P, KC, P]), ALU.mult).then_inc(diag_ready, 1)

            @blk.tensor
            def _(pe):
                for i in range(len(wanted)):
                    pe.wait_ge(diag_ready, base + i + 1)
                    wait(pe, row_ready, base + i - 1 if i > 1 else 0)
                    for n in range(2):
                        last = nc.tensor.matmul(spread[i % 2][:, n, :], core.ones[:],
                                                diag[i % 2][:, 4 * n:4 * n + 4, :].rearrange("p k m -> p (k m)"),
                                                start=True, stop=True)
                    last.then_inc(spread_ready, 1)

            @blk.scalar
            def _(act):
                for i, (row, _) in enumerate(wanted):
                    act.wait_ge(spread_ready, base + i + 1)
                    nc.scalar.activation(row, spread[i % 2][:].rearrange("p n m -> p (n m)"), ACT.Copy)\
                      .then_inc(row_ready, 1)



def norm_stage(core, name, x, rows, tiles, into=None, split=None, router=None, load=(), seed=()):
    nc = core.nc
    streams = 2 if tiles > T_LAT else 1
    with ExitStack() as st:
        junk = st.enter_context(nc.sbuf_tensor(f"{name}_squares", [P, D], F32))
        ssq = st.enter_context(nc.sbuf_tensor(f"{name}_ssq", [P, tiles], F32))
        rstd = st.enter_context(nc.sbuf_tensor(f"{name}_rstd", [P, tiles], F32))
        eps = st.enter_context(nc.sbuf_tensor(f"{name}_eps", [P, 1], F32))
        h = [st.enter_context(nc.sbuf_tensor(f"{name}_h{i}", [P, D], F32)) for i in range(2)]
        turned = [st.enter_context(nc.psum_tensor(f"{name}_turned{i}", [P, 4, P], F32)) for i in range(4)]
        if router:
            w_router, logits = router
            ht = [st.enter_context(nc.sbuf_tensor(f"{name}_ht{i}", [P, KC, P], F32)) for i in range(2)]
        (x_landed, squared, eps_set, root, rstd_ready, scaled, h_ready, turned_lo, turned_hi, out_lo, out_hi) = (
            core.sem(f"{name}_{n}") for n in (
                "x_landed", "squared", "eps_set", "root", "rstd_ready", "scaled", "h_ready", "turned_lo", "turned_hi",
                "out_lo", "out_hi"))
        stored0, stored1, seeded, routed = (
            core.sem(f"{name}_{n}") if router else None for n in ("stored0", "stored1", "seeded", "routed"))
        stored = (stored0, stored1)
        copies = 2 if split else 1

        with core.block() as blk:
            @blk.sync
            def _(sp):
                for dst, src in load:
                    sp.dma_start(dst, src).then_inc(x_landed, 16)
                if load and seed:
                    sp.wait_ge(x_landed, 16 * len(load))
                for dst, src in seed:
                    sp.dma_start(dst, src).then_inc(seeded, 16)
                if router:
                    for e, stream in pairs(nc.sync, streams):
                        out = (core.h_ctx if stream else core.h_lat).rearrange("(t p) d -> p t d", p=P)
                        for i in range(2):
                            sp.wait_ge(h_ready, e * 2 + (i + 1))
                            sp.dma_start(out[:, ds(e * 2 + (i - T_LAT * stream), 1), :], h[i][:].unsqueeze(1))\
                              .then_inc(stored[i], 16)
                    for i in range(2):
                        sp.wait_ge(stored[i], 16 * (tiles // 2))
                if seed:
                    sp.wait_ge(seeded, 16 * len(seed))

            @blk.scalar
            def _(act):
                if load:
                    act.wait_ge(x_landed, 16 * len(load))
                for t in range(tiles):
                    wait(act, squared, t)
                    nc.scalar.activation(junk[:], x[:, t, :], ACT.Square, accum_out=ssq[:, t:t + 1]).then_inc(squared, 1)
                act.wait_ge(squared, tiles)
                act.wait_ge(eps_set, 1)
                nc.scalar.activation(ssq[:], ssq[:], ACT.Sqrt, bias=eps[:], scale=1.0 / D).then_inc(root, 1)
                for e, stream in pairs(nc.scalar, streams):
                    for i in range(2):
                        t = e * 2 + i
                        act.wait_ge(turned_lo, e * 2 + (i + 1))
                        if router:
                            wait(act, routed, e * 2 + (i - 1))
                            nc.scalar.activation(ht[i][:, 0:4, :], turned[2 * i][:], ACT.Copy).then_inc(out_lo, 1)
                        elif split:
                            nc.scalar.activation(split[0][:, 0:4, ds(t * P, P)], turned[2 * i][:], ACT.Copy).then_inc(out_lo, 1)
                            act.wait_ge(turned_hi, e * 2 + (i + 1))
                            nc.scalar.activation(split[0][:, 4:8, ds(t * P, P)], turned[2 * i + 1][:], ACT.Copy)\
                              .then_inc(out_lo, 1)
                        else:
                            nc.scalar.activation(into(0, t, stream), turned[2 * i][:], ACT.Copy).then_inc(out_lo, 1)

            @blk.vector
            def _(dve):
                nc.vector.memset(eps[:], EPS).then_inc(eps_set, 1)
                dve.wait_ge(root, 1)
                nc.vector.reciprocal(rstd[:], ssq[:]).then_inc(rstd_ready, 1)
                dve.wait_ge(rstd_ready, 1)
                for e, stream in pairs(nc.vector, streams):
                    for i in range(2):
                        t = e * 2 + i
                        wait(dve, turned_hi, e * 2 + (i - 1))
                        if router:
                            wait(dve, stored[i], e * 16)
                        nc.vector.scalar_tensor_tensor(h[i][:], x[:, ds(t, 1), :].rearrange("p a d -> p (a d)"),
                                                       rstd[:, ds(t, 1)], rows[:, 2 * stream, :],
                                                       ALU.mult, ALU.mult).then_inc(scaled, 1)
                        dve.wait_ge(scaled, e * 2 + (i + 1))
                        nc.vector.tensor_tensor(h[i][:], h[i][:], rows[:, 2 * stream + 1, :], ALU.add)\
                          .then_inc(h_ready, 1)
                        dve.wait_ge(turned_hi, e * 2 + (i + 1))
                        if router:
                            wait(dve, routed, e * 2 + (i - 1))
                            nc.vector.tensor_copy(ht[i][:, 4:8, :], turned[2 * i + 1][:]).then_inc(out_hi, 1)
                        elif split:
                            for n in range(2):
                                dve.wait_ge(out_lo, e * 4 + (2 * i + n + 1))
                                nc.vector.tensor_tensor(split[1][:, 4 * n:4 * n + 4, ds(t * P, P)], turned[2 * i + n][:],
                                                        split[0][:, 4 * n:4 * n + 4, ds(t * P, P)].bitcast(F32),
                                                        ALU.subtract).then_inc(out_hi, 1)
                        else:
                            nc.vector.tensor_copy(into(4, t, stream), turned[2 * i + 1][:]).then_inc(out_hi, 1)

            @blk.tensor
            def _(pe):
                for e, stream in pairs(nc.tensor, streams):
                    for i in range(2):
                        pe.wait_ge(h_ready, e * 2 + (i + 1))
                        wait(pe, out_lo, (e * 2 + (i - 1)) * copies)
                        wait(pe, out_hi, (e * 2 + (i - 1)) * copies)
                        for k in range(KC):
                            last = nc.tensor.transpose(turned[2 * i + k // 4][:, k % 4, :], h[i][:, k * P:(k + 1) * P],
                                                       core.ident[:])
                            if k == 3:
                                last.then_inc(turned_lo, 1)
                        last.then_inc(turned_hi, 1)
                        if router:
                            pe.wait_ge(out_lo, e * 2 + (i + 1))
                            pe.wait_ge(out_hi, e * 2 + (i + 1))
                            for k in range(KC):
                                last = nc.tensor.matmul(logits[:, ds((e * 2 + i) * EXPERTS, EXPERTS)], ht[i][:, k, :],
                                                        w_router[:, k, :], start=k == 0, stop=k == KC - 1)
                            last.then_inc(routed, 1)



def choice_stage(core, name, logits, streams, beside=None):
    nc = core.nc
    tiles = T_LAT + (T_CTX if streams == 2 else 0)
    rounds = SLOTS_LAT // 8
    with ExitStack() as st:
        def sb(n, shape, dt=F32):
            return st.enter_context(nc.sbuf_tensor(f"{name}_{n}", shape, dt))

        top, total, inv = sb("top", [P, tiles]), sb("total", [P, tiles]), sb("inv", [P, tiles])
        aff = sb("aff", [P, tiles, EXPERTS])
        wide = sb("wide", [P, T_LAT, 48])
        pool_of = [sb(f"left{i}", [48, N_LAT]) for i in range(2)]
        best, where, where_f = sb("best", [48, SLOTS_LAT]), sb("where", [48, SLOTS_LAT], U32), sb("where_f", [48, SLOTS_LAT])
        turned = [st.enter_context(nc.psum_tensor(f"{name}_turned{i}", [P, 4, P], F32)) for i in range(2)]
        out = [st.enter_context(nc.psum_tensor(f"{name}_out{i}", [P, BANK], F32)) for i in range(2)]
        step, exps, turned_s, chosen, back = (core.sem(f"{name}_{n}") for n in (
            "step", "exps", "turned_s", "chosen", "back"))
        placed = core.placed
        with core.block() as blk:
            @blk.vector
            def _(dve):
                done = [0]

                def chain(ins):
                    ins.then_inc(step, 1)
                    done[0] += 1
                    dve.wait_ge(step, done[0])

                seen = logits[:, 0:tiles * EXPERTS].rearrange("p (t e) -> p t e", e=EXPERTS)
                nc.vector.memset(wide[:], -1.0)
                chain(nc.vector.tensor_reduce(top[:], seen, AX, ALU.max))
                chain(nc.vector.tensor_tensor(aff[:], seen, top[:].unsqueeze(2).to_broadcast([P, tiles, EXPERTS]),
                                              ALU.subtract))
                dve.wait_ge(exps, 1)
                chain(nc.vector.tensor_reduce(total[:], aff[:], AX, ALU.add))
                chain(nc.vector.reciprocal(inv[:], total[:]))
                ends = [(0, T_LAT, 0)] + ([(T_LAT, tiles, 32)] if streams == 2 else [])
                for a, b, col in ends:
                    chain(nc.vector.tensor_tensor(wide[:, 0:b - a, col:col + EXPERTS], aff[:, a:b, :],
                                                  inv[:, a:b].unsqueeze(2).to_broadcast([P, b - a, EXPERTS]), ALU.mult))
                for n in range(2):
                    dve.wait_ge(turned_s, n + 1)
                    chain(nc.vector.tensor_copy(pool_of[0][:, BANK * n:BANK * n + BANK],
                                                turned[n][0:48].rearrange("p k m -> p (k m)")))
                for r in range(rounds):
                    left, rest = pool_of[r % 2], pool_of[1 - r % 2]
                    eight = best[:, 8 * r:8 * r + 8]
                    chain(nc.vector.max(eight, left[:]))
                    nc.vector.max_index(where[:, 8 * r:8 * r + 8], eight, left[:]).then_inc(chosen, 1)
                    if r < rounds - 1:
                        chain(nc.vector.match_replace(rest[:], eight, left[:], -1.0))
                dve.wait_ge(chosen, rounds)
                nc.vector.tensor_copy(where_f[:], where[:]).then_inc(chosen, 1)
                dve.wait_ge(back, 1)
                nc.vector.tensor_copy(core.gate_t[:], out[0][:, 0:48]).then_inc(placed, 1)
                dve.wait_ge(back, 2)
                nc.vector.tensor_copy(core.index_t[:], out[1][:, 0:48]).then_inc(placed, 1)
                if beside:
                    beside.finish(dve)

            @blk.scalar
            def _(act):
                act.wait_ge(step, 2)
                nc.scalar.activation(aff[:], aff[:], ACT.Exp).then_inc(exps, 1)
                if beside:
                    beside.copy_out(act)

            @blk.tensor
            def _(pe):
                pe.wait_ge(step, 4 + streams)
                for t in range(T_LAT):
                    last = nc.tensor.transpose(turned[t // 4][0:48, t % 4, :], wide[:, t, :], core.ident[:])
                    if t % 4 == 3:
                        last.then_inc(turned_s, 1)
                if beside:
                    beside.products(pe)
                pe.wait_ge(chosen, rounds + 1)
                nc.tensor.transpose(out[0][:, 0:48], best[:], core.ident[0:48, 0:48]).then_inc(back, 1)
                nc.tensor.transpose(out[1][:, 0:48], where_f[:], core.ident[0:48, 0:48]).then_inc(back, 1)

            @blk.sync
            def _(sp):
                if beside:
                    beside.load(sp)



def experts_stage(core, name, block, streams, g2_rows, x_lat, x_ctx):
    nc, io = core.nc, core.io
    slots = SLOTS_LAT + (SLOTS_CTX if streams == 2 else 0)
    first = core.chunks
    core.chunks += EXPERTS * EXP_CHUNKS
    PLACES, LEAD = 6, 4
    h_cols = SLOTS_LAT + (2 * SLOTS_CTX if streams == 2 else 0) + SLOTS_LAT
    with ExitStack() as st:
        def sb(n, shape, dt=F32):
            return st.enter_context(nc.sbuf_tensor(f"{name}_{n}", shape, dt))

        def psum(n, banks=1):
            return st.enter_context(nc.psum_tensor(f"{name}_{n}", [P, banks * BANK], F32))

        w_hi = [sb(f"w_hi{i}", [P, CHUNK], F32R) for i in range(PLACES)]
        w_lo = [sb(f"w_lo{i}", [P, CHUNK], F32R) for i in range(PLACES)]
        xg, xg_ctx = sb("xg", [P, D]), sb("xg_ctx", [SLOTS_CTX, D])
        x = sb("x", [P, KC, 2, slots], F32R)
        part = [sb(f"part{i}", [P, 2, slots]) for i in range(2)]
        gate_up_s = [sb(f"gate_up{i}", [P, 2, slots]) for i in range(2)]
        silu_g = [sb(f"silu_g{i}", [P, slots]) for i in range(2)]
        prod = [sb(f"prod{i}", [P, slots]) for i in range(2)]
        h = sb("h", [P, KC, h_cols], F32R)
        y, y_ctx, ctx_part = sb("y", [P, D]), sb("y_ctx", [SLOTS_CTX, D]), sb("ctx_part", [SLOTS_CTX, D])
        gu = [psum(f"gu{i}", 2) for i in range(2)]
        y_sum = [psum(f"y_sum{i}") for i in range(2)]
        y_ctx_sum = psum("y_ctx_sum", 2) if streams == 2 else None
        (hi_done, gathered, gathered_ctx, turned_s, x_hi_done, x_ready, gu_ready, part_done, sum_done, silu_done,
         prod_done, h_hi_done, h_ready, down_done, ctx_part_done, ctx_added, y_ready, scattered, scattered_ctx) = (
            core.sem(f"{name}_{n}") for n in (
                "hi_done", "gathered", "gathered_ctx", "turned", "x_hi_done", "x_ready", "gu_ready", "part_done",
                "sum_done", "silu_done", "prod_done", "h_hi_done", "h_ready", "down_done", "ctx_part_done", "ctx_added",
                "y_ready", "scattered", "scattered_ctx"))
        turns = 2 + (streams == 2)

        def experts(engine):
            yield 0, False
            with engine.Fori(1, EXPERTS - 1) as e:
                yield e, False
            yield EXPERTS - 1, True

        def place_free(eng, s, e):
            if s < PLACES:
                before = s + EXP_CHUNKS - PLACES
                if before < 8:
                    wait(eng, gu_ready, e * KC)
                else:
                    wait(eng, down_done, e * 4 + (before - 8 + 1 - 4))
            else:
                eng.wait_ge(gu_ready, e * KC + (2 * ((s - PLACES) // 2) + 2))

        def turn_views(g):
            if g < 2:
                return (gu[0][:, BANK * g:BANK * (g + 1)].rearrange("p (k m) -> p k m", k=4),
                        (slice(4 * g, 4 * g + 4), slice(0, SLOTS_LAT)))
            return (gu[1][:, 0:KC * SLOTS_CTX].rearrange("p (k m) -> p k m", k=KC),
                    (slice(0, KC), slice(SLOTS_LAT, slots)))

        def gu_view(j, n):
            return gu[j % 2][:].rearrange("p (w m) -> p w m", w=2)[:, :, slots * n:slots * (n + 1)]

        with core.block() as blk:
            @blk.sync
            def _(sp):
                with nc.sync.Fori(0, EXPERTS) as e:
                    for s in range(EXP_CHUNKS):
                        shape = dict(e=1, k=KC if s < 8 else 2)
                        load_chunk(core, sp, first + s, expert_chunk(io, block, s, e),
                                   lambda place: place[:].rearrange("p (e k f) -> p e k f", **shape), e, EXP_CHUNKS)

            @blk.gpsimd
            def _(pool):
                rows_of = ((xg, y, core.h_lat, x_lat, gathered, scattered, SLOTS_LAT, 0),
                           (xg_ctx, y_ctx, core.h_ctx, x_ctx, gathered_ctx, scattered_ctx, SLOTS_CTX, 32))[:streams]
                for e in range(-1, EXPERTS):
                    if e + 1 < EXPERTS:
                        wait(pool, turned_s, (e + 1) * turns)
                        for got, _, rows, _, landed_s, _, n, col in rows_of:
                            index = core.index_t[0:n, e + 1 + col:e + 2 + col]
                            nc.gpsimd.indirect_dma_start(got[:], None, rows, bass.IndirectOffsetOnAxis(ap=index, axis=0))\
                              .then_inc(landed_s, 16)
                    if e >= 0:
                        pool.wait_ge(y_ready, (e + 1) * 2 * streams)
                        for _, add, _, to, _, added_s, n, col in rows_of:
                            wait(pool, added_s, e * 16)
                            index = core.index_t[0:n, e + col:e + 1 + col]
                            nc.gpsimd.indirect_dma_start(to, bass.IndirectOffsetOnAxis(ap=index, axis=0), add[:], None,
                                                         compute_op=ALU.add).then_inc(added_s, 16)
                for _, _, _, _, _, added_s, _, _ in rows_of:
                    pool.wait_ge(added_s, 16 * EXPERTS)

            @blk.tensor
            def _(pe):
                def turn(e):
                    pe.wait_ge(gathered, e * 16 + 16)
                    wait(pe, sum_done, e * KC)
                    for g in range(2):
                        if g == 1 and streams == 2:
                            pe.wait_ge(gathered_ctx, e * 16 + 16)
                        for k in range(4):
                            last = nc.tensor.transpose(gu[0][:, BANK * g + k * P:BANK * g + (k + 1) * P],
                                                       xg[:, (4 * g + k) * P:(4 * g + k + 1) * P], core.ident[:])
                        last.then_inc(turned_s, 1)
                    if streams == 2:
                        for k in range(KC):
                            last = nc.tensor.transpose(gu[1][:, k * SLOTS_CTX:(k + 1) * SLOTS_CTX],
                                                       xg_ctx[:, k * P:(k + 1) * P], core.ident[0:SLOTS_CTX, 0:SLOTS_CTX])
                        last.then_inc(turned_s, 1)

                def gate_up(e):
                    pe.wait_ge(x_ready, e * turns + turns)
                    for j in range(KC):
                        if j % 2 == 0:
                            chunk_done(core, pe, first + j + 1, e, EXP_CHUNKS)
                        wait(pe, sum_done, e * KC + (j - 1))
                        for which in range(2):
                            at = (j // 2 * 2 + which) % PLACES
                            out = gu[j % 2][:, BANK * which:BANK * which + 2 * slots]
                            for k in range(KC):
                                col = 256 * k + P * (j % 2)
                                passes = ((w_hi, 2), (w_lo, 1)) if k < KC - 1 else ((w_lo, 1), (w_hi, 2))
                                for n, (w, cols) in enumerate(passes):
                                    last = nc.tensor.matmul(out[:, 0:cols * slots], w[at][:, col:col + P],
                                                            x[:, k, 0:cols, :], start=k == 0 and n == 0,
                                                            stop=k == KC - 1 and n == 1)
                        last.then_inc(gu_ready, 1)

                def down(e, r):
                    chunk_done(core, pe, first + 8 + r, e, EXP_CHUNKS)
                    pe.wait_ge(h_ready, e * KC + (2 * r + 2))
                    w = (8 + r) % PLACES
                    for kk in range(2):
                        k = 2 * r + kk
                        lat_hi, lat_lo = h[:, k, 0:SLOTS_LAT], h[:, k, h_cols - SLOTS_LAT:h_cols]
                        ctx_hi = h[:, k, SLOTS_LAT:SLOTS_LAT + SLOTS_CTX]
                        ctx_both = h[:, k, SLOTS_LAT:SLOTS_LAT + 2 * SLOTS_CTX]
                        for c in range(2):
                            cols = slice(D * kk + BANK * c, D * kk + BANK * (c + 1))
                            hi, lo = w_hi[w][:, cols], w_lo[w][:, cols]
                            for n, (a, b) in enumerate(((lat_hi, hi), (lat_hi, lo), (lat_lo, hi))):
                                last = nc.tensor.matmul(y_sum[c][:], a, b, start=k == 0 and n == 0,
                                                        stop=k == KC - 1 and n == 2)
                            if streams == 2:
                                passes = ((ctx_both, hi, 2), (ctx_hi, lo, 1))
                                if k == KC - 1:
                                    passes = passes[::-1]
                                for n, (a, b, rows) in enumerate(passes):
                                    last = nc.tensor.matmul(y_ctx_sum[0:rows * SLOTS_CTX, BANK * c:BANK * (c + 1)], a, b,
                                                            start=k == 0 and n == 0, stop=k == KC - 1 and n == 1)
                    last.then_inc(down_done, 1)

                turn(0)
                for e, is_last in experts(nc.tensor):
                    gate_up(e)
                    wait(pe, y_ready, e * (2 * streams))
                    down(e, 0)
                    down(e, 1)
                    if not is_last:
                        turn(e + 1)
                    down(e, 2)
                    down(e, 3)

            @blk.scalar
            def _(act):
                def weights_hi(s, e):
                    landed(core, act, first + s, e, EXP_CHUNKS)
                    place_free(act, s, e)
                    nc.scalar.activation(w_hi[s % PLACES][:], core.raw[(first + s) % RING][:], ACT.Copy).then_inc(hi_done, 1)

                def tokens_hi(e):
                    for g in range(turns):
                        bank, (ks, cols) = turn_views(g)
                        act.wait_ge(turned_s, e * turns + (g + 1))
                        nc.scalar.activation(x[:, ks, 0, cols], bank, ACT.Copy).then_inc(x_hi_done, 1)

                def context_part(e):
                    act.wait_ge(down_done, e * 4 + 4)
                    wait(act, y_ready, e * (2 * streams))
                    nc.scalar.activation(ctx_part[:], y_ctx_sum[SLOTS_CTX:2 * SLOTS_CTX, :], ACT.Copy)\
                      .then_inc(ctx_part_done, 1)

                tokens_hi(0)
                for s in range(LEAD):
                    weights_hi(s, 0)
                for e, is_last in experts(nc.scalar):
                    for t in range(EXP_CHUNKS):
                        j = t - 1
                        if t == 0 and streams == 2 and (not isinstance(e, int) or e > 0):
                            context_part(e - 1)
                        if 0 <= j < KC:
                            act.wait_ge(gu_ready, e * KC + (j + 1))
                            wait(act, sum_done, e * KC + (j - 1))
                            nc.scalar.activation(part[j % 2][:], gu_view(j, 1), ACT.Copy).then_inc(part_done, 1)
                        if t + LEAD < EXP_CHUNKS:
                            weights_hi(t + LEAD, e)
                        elif not is_last:
                            weights_hi(t + LEAD - EXP_CHUNKS, e + 1)
                        if 0 <= j < KC:
                            act.wait_ge(sum_done, e * KC + (j + 1))
                            wait(act, prod_done, e * KC + (j - 1))
                            nc.scalar.activation(silu_g[j % 2][:], gate_up_s[j % 2][:, 0, :], ACT.Silu).then_inc(silu_done, 1)
                        if t == 9 and not is_last:
                            tokens_hi(e + 1)
                if streams == 2:
                    context_part(EXPERTS - 1)

            @blk.vector
            def _(dve):
                def weights_lo(s, e):
                    dve.wait_ge(hi_done, e * EXP_CHUNKS + (s + 1))
                    nc.vector.tensor_tensor(w_lo[s % PLACES][:], core.raw[(first + s) % RING][:],
                                            w_hi[s % PLACES][:].bitcast(F32), ALU.subtract).then_inc(core.chunk_done, 1)

                def tokens_lo(e):
                    for g in range(turns):
                        bank, (ks, cols) = turn_views(g)
                        dve.wait_ge(x_hi_done, e * turns + (g + 1))
                        nc.vector.tensor_tensor(x[:, ks, 1, cols], bank, x[:, ks, 0, cols].bitcast(F32), ALU.subtract)\
                          .then_inc(x_ready, 1)

                def product(j, e):
                    dve.wait_ge(silu_done, e * KC + (j + 1))
                    wait(dve, h_ready, e * KC + (j - 1))
                    nc.vector.tensor_tensor(prod[j % 2][:], gate_up_s[j % 2][:, 1, :], silu_g[j % 2][:], ALU.mult)\
                      .then_inc(prod_done, 1)
                    dve.wait_ge(prod_done, e * KC + (j + 1))
                    nc.vector.tensor_copy(h[:, j, 0:slots], prod[j % 2][:]).then_inc(h_hi_done, 1)
                    dve.wait_ge(h_hi_done, e * KC + (j + 1))
                    if streams == 2:
                        nc.vector.tensor_tensor(h[:, j, slots:slots + SLOTS_CTX], prod[j % 2][:, SLOTS_LAT:],
                                                h[:, j, SLOTS_LAT:slots].bitcast(F32), ALU.subtract)
                    nc.vector.tensor_tensor(h[:, j, h_cols - SLOTS_LAT:], prod[j % 2][:, 0:SLOTS_LAT],
                                            h[:, j, 0:SLOTS_LAT].bitcast(F32), ALU.subtract).then_inc(h_ready, 1)

                def results(e):
                    dve.wait_ge(down_done, e * 4 + 4)
                    wait(dve, scattered, e * 16)
                    for c in range(2):
                        cols = slice(BANK * c, BANK * (c + 1))
                        nc.vector.scalar_tensor_tensor(y[:, cols], y_sum[c][:], core.gate_t[:, ds(e, 1)], g2_rows[:, 0, cols],
                                                       ALU.mult, ALU.mult).then_inc(y_ready, 1)
                    if streams == 2:
                        dve.wait_ge(ctx_part_done, e + 1)
                        wait(dve, scattered_ctx, e * 16)
                        for c in range(2):
                            cols = slice(BANK * c, BANK * (c + 1))
                            nc.vector.tensor_tensor(y_ctx[:, cols], y_ctx_sum[0:SLOTS_CTX, cols], ctx_part[:, cols], ALU.add)\
                              .then_inc(ctx_added, 1)
                            dve.wait_ge(ctx_added, e * 2 + (c + 1))
                            nc.vector.scalar_tensor_tensor(y_ctx[:, cols], y_ctx[:, cols],
                                                           core.gate_t[0:SLOTS_CTX, ds(e + 32, 1)],
                                                           g2_rows[0:SLOTS_CTX, 1, cols], ALU.mult, ALU.mult)\
                              .then_inc(y_ready, 1)

                tokens_lo(0)
                for s in range(LEAD):
                    weights_lo(s, 0)
                for e, is_last in experts(nc.vector):
                    for t in range(EXP_CHUNKS):
                        j = t - 1
                        if t == 0 and (not isinstance(e, int) or e > 0):
                            results(e - 1)
                        if 0 <= j < KC:
                            dve.wait_ge(part_done, e * KC + (j + 1))
                            nc.vector.tensor_tensor(gate_up_s[j % 2][:], gu_view(j, 0), part[j % 2][:], ALU.add)\
                              .then_inc(sum_done, 1)
                        if t + LEAD < EXP_CHUNKS:
                            weights_lo(t + LEAD, e)
                        elif not is_last:
                            weights_lo(t + LEAD - EXP_CHUNKS, e + 1)
                        if 0 <= j < KC:
                            product(j, e)
                        if t == 9 and not is_last:
                            tokens_lo(e + 1)
                results(EXPERTS - 1)



def padded_place(ht):
    def into(k, t, stream):
        at = t * P + (OFF_CTX - N_LAT if stream else OFF_LAT)
        return ht[:, k:k + 4, ds(at, P)]
    return into


def pool_stage(core, ht, x, gain_rows):
    nc, io = core.nc, core.io
    tiles = T_LAT + T_CTX
    with ExitStack() as st:
        def sb(n, shape, dt=F32):
            return st.enter_context(nc.sbuf_tensor(f"pool_{n}", shape, dt))

        sums = [sb(f"sums{i}", [P, 2, PADDED]) for i in range(2)]
        weights = sb("weights", [P, 2 * len(WINDOWS), 2 * P])
        edge = sb("edge", [P, len(WINDOWS), 2, PAD])
        edge_mean = sb("edge_mean", [P, 2, 4, PAD])
        change = [sb(f"change{i}", [P, D]) for i in range(2)]
        out = [[st.enter_context(nc.psum_tensor(f"pool_out{i}{n}", [P, BANK], F32)) for n in range(2)] for i in range(2)]
        loaded, step, pooled, product, scaled, added = (
            core.sem(f"pool_{n}") for n in ("loaded", "step", "pooled", "product", "scaled", "added"))
        with core.block() as blk:
            @blk.sync
            def _(sp):
                sp.dma_start(weights[:], io["pool_w"][0].rearrange("g (k p) d -> p (g k) d", p=P)).then_inc(loaded, 16)
                sp.dma_start(edge[:], io["edge"].partition_broadcast(P).rearrange("p (g s c) -> p g s c", g=len(WINDOWS), s=2))\
                  .then_inc(loaded, 16)

            @blk.vector
            def _(dve):
                done = [0]

                def chain(ins):
                    ins.then_inc(step, 1)
                    done[0] += 1
                    dve.wait_ge(step, done[0])

                dve.wait_ge(loaded, 32)
                for g, w in enumerate(WINDOWS):
                    h = ht[:, 2 * g:2 * g + 2, :]
                    src, reach = h, 0
                    for level in range(g + 1):
                        dst = sums[level % 2]
                        if level == 0:
                            chain(nc.vector.tensor_tensor(dst[:, :, 1:PADDED], h[:, :, 1:PADDED], h[:, :, 0:PADDED - 1], ALU.add))
                        else:
                            n = 1 << (level - 1)
                            lo = 2 * n
                            chain(nc.vector.tensor_tensor(dst[:, :, lo:PADDED - lo + 1], src[:, :, lo - n:PADDED - lo + 1 - n],
                                                          src[:, :, lo + n:PADDED - lo + 1 + n], ALU.add))
                        src = dst
                    ends = [OFF_LAT, OFF_LAT + N_LAT - PAD, OFF_CTX, OFF_CTX + N_CTX - PAD]
                    for i, at in enumerate(ends):
                        inv = edge[:, g, i % 2, :].unsqueeze(1).to_broadcast([P, 2, PAD])
                        chain(nc.vector.tensor_tensor(edge_mean[:, :, i, :], src[:, :, at:at + PAD], inv, ALU.mult))
                        chain(nc.vector.tensor_tensor(edge_mean[:, :, i, :], edge_mean[:, :, i, :], h[:, :, at:at + PAD],
                                                      ALU.subtract))
                    for at, n in ((OFF_LAT, N_LAT), (OFF_CTX, N_CTX)):
                        chain(nc.vector.scalar_tensor_tensor(h[:, :, at:at + n], src[:, :, at:at + n], 1.0 / w,
                                                             h[:, :, at:at + n], ALU.mult, ALU.subtract))
                    for i, at in enumerate(ends):
                        last = nc.vector.tensor_copy(h[:, :, at:at + PAD], edge_mean[:, :, i, :])
                        chain(last) if i < 3 else last.then_inc(pooled, 1)
                for t in range(tiles):
                    gain = gain_rows[:, 1 if t >= T_LAT else 0, :]
                    dve.wait_ge(product, t + 1)
                    wait(dve, added, t - 1)
                    for n in range(2):
                        nc.vector.tensor_tensor(change[t % 2][:, BANK * n:BANK * n + BANK], out[t % 2][n][:],
                                                gain[:, BANK * n:BANK * n + BANK], ALU.mult).then_inc(scaled, 1)
                    dve.wait_ge(scaled, 2 * t + 2)
                    nc.vector.tensor_tensor(x[:, t, :], x[:, t, :], change[t % 2][:], ALU.add).then_inc(added, 1)

            @blk.tensor
            def _(pe):
                pe.wait_ge(pooled, len(WINDOWS))
                for t in range(tiles):
                    wait(pe, scaled, 2 * (t - 1))
                    at = t * P + (OFF_CTX - N_LAT if t >= T_LAT else OFF_LAT)
                    for g in range(len(WINDOWS)):
                        for k in range(2):
                            last = nc.tensor.matmul(out[t % 2][g // 2][:, 256 * (g % 2):256 * (g % 2) + 256],
                                                    ht[:, 2 * g + k, at:at + P], weights[:, 2 * g + k, :],
                                                    start=k == 0, stop=k == 1)
                    last.then_inc(product, 1)



def lru_stage(core, t_hi, t_lo, decay):
    nc, io = core.nc, core.io
    first = core.chunks
    core.chunks += KC
    half = KC * P
    unroll = RING
    segments = ((0, BANK), (BANK, BANK), (N_LAT, N_CTX))
    with ExitStack() as st:
        def sb(n, shape, dt=F32):
            return st.enter_context(nc.sbuf_tensor(f"lru_{n}", shape, dt))

        w_hi, w_lo = sb("w_hi", [P, CHUNK], F32R), sb("w_lo", [P, CHUNK], F32R)
        gw = [sb(f"gw{i}", [P, 4, P]) for i in range(2)]
        gw_hi, gw_lo = sb("gw_hi", [P, 4, P], F32R), sb("gw_lo", [P, 4, P], F32R)
        par = sb("par", [P, LRU_COLS + 6])
        x, x_hi, x_lo = sb("x", [P, TOK]), sb("x_hi", [P, TOK], F32R), sb("x_lo", [P, TOK], F32R)
        r = [sb(f"r{i}", [P, TOK]) for i in range(2)]
        gi = [sb(f"i{i}", [P, TOK]) for i in range(2)]
        a = [sb(f"a{i}", [P, TOK]) for i in range(2)]
        q = [sb(f"q{i}", [P, TOK]) for i in range(2)]
        y = sb("y", [P, N_LAT])
        x_sum = st.enter_context(nc.psum_tensor("lru_x_sum", [P, 3 * BANK], F32))
        y_sum = st.enter_context(nc.psum_tensor("lru_y_sum", [P, 2 * BANK], F32))
        g_sum = [st.enter_context(nc.psum_tensor(f"lru_g_sum{i}", [P, BANK], F32)) for i in range(3)]
        (gw_landed0, gw_landed1, hi_done, gw_hi_done, gw_done, par_set, x_ready, y_ready, conv, x_hi_done, x_split,
         y_done, gates, g_done, powers, roots, step, stored, o_ready) = (core.sem(f"lru_{n}") for n in (
             "gw_landed0", "gw_landed1", "hi_done", "gw_hi_done", "gw_done", "par_set", "x_ready", "y_ready", "conv",
             "x_hi_done", "x_split", "y_done", "gates", "g_done", "powers", "roots", "step", "stored", "o_ready"))
        gw_landed = (gw_landed0, gw_landed1)
        CONV = 8
        STEPS = 11

        def blocks(engine):
            for i in range(unroll):
                yield 0, i
            with engine.Fori(1, KC // unroll) as e:
                for i in range(unroll):
                    yield e, i

        w_in = io["lru_w_in"][0].rearrange("(k p) (s b m) -> p s k b m", p=P, s=2, m=P)
        wa = io["lru_wa"][0].rearrange("d b i o -> i d b o")
        wx = io["lru_wx"][0].rearrange("d b i o -> i d b o")

        with core.block() as blk:
            @blk.sync
            def _(sp):
                for e, i in blocks(nc.sync):
                    b = e * unroll + i
                    sp.wait_ge(core.chunk_done, e * unroll + (first + i + 1))
                    sp.dma_start(core.raw[i][:].rearrange("p (s k b m) -> p s k b m", s=2, k=KC, b=1),
                                 w_in[:, :, :, ds(b, 1), :]).then_inc(core.raw_landed[i], 16)
                    wait(sp, gw_done, e * unroll + (i - 1))
                    for s, w in enumerate((wa, wx)):
                        sp.dma_start(gw[i % 2][:, 2 * s:2 * s + 2, :].unsqueeze(2), w[:, :, ds(b, 1), :])\
                          .then_inc(gw_landed[i % 2], 16)

            @blk.tensor
            def _(pe):
                for e, i in blocks(nc.tensor):
                    b = e * unroll + i
                    chunk_done(core, pe, first + i, e, unroll)
                    wait(pe, conv, b * CONV)
                    for n, (at, size) in enumerate(segments):
                        for k in range(KC):
                            for m, (w, t) in enumerate(((w_hi, t_hi), (w_hi, t_lo), (w_lo, t_hi))):
                                last = nc.tensor.matmul(x_sum[:, BANK * n:BANK * n + size], w[:, half + P * k:half + P * k + P],
                                                        t[:, k, at:at + size], start=k == 0 and m == 0,
                                                        stop=k == KC - 1 and m == 2)
                    last.then_inc(x_ready, 1)
                    wait(pe, y_done, b)
                    for n in range(2):
                        for k in range(KC):
                            for m, (w, t) in enumerate(((w_hi, t_hi), (w_hi, t_lo), (w_lo, t_hi))):
                                last = nc.tensor.matmul(y_sum[:, BANK * n:BANK * n + BANK], w[:, P * k:P * k + P],
                                                        t[:, k, BANK * n:BANK * n + BANK], start=k == 0 and m == 0,
                                                        stop=k == KC - 1 and m == 2)
                    last.then_inc(y_ready, 1)
                    pe.wait_ge(gw_done, b + 1)
                    pe.wait_ge(x_split, b + 1)
                    for g in range(4):
                        for n, (at, size) in enumerate(segments):
                            wait(pe, g_done, b * 12 + (3 * g + n - 2))
                            for m, (w, t) in enumerate(((gw_hi, x_hi), (gw_hi, x_lo), (gw_lo, x_hi))):
                                last = nc.tensor.matmul(g_sum[n][:, 0:size], w[:, g, :], t[:, at:at + size],
                                                        start=m == 0, stop=m == 2)
                            last.then_inc(gates, 1)

            @blk.scalar
            def _(act):
                def store(act, b):
                    act.dma_start(core.o_lru.rearrange("(b p) t -> p b t", p=P)[:, ds(b, 1), :],
                                  r[0][:, 0:N_LAT].unsqueeze(1)).then_inc(stored, 16)

                for e, i in blocks(nc.scalar):
                    b = e * unroll + i
                    landed(core, act, first + i, e, unroll)
                    wait(act, y_ready, b)
                    nc.scalar.activation(w_hi[:], core.raw[i][:], ACT.Copy).then_inc(hi_done, 1)
                    act.wait_ge(gw_landed[i % 2], e * 64 + (32 * (i // 2) + 32))
                    wait(act, gates, b * 12)
                    nc.scalar.activation(gw_hi[:], gw[i % 2][:], ACT.Copy).then_inc(gw_hi_done, 1)
                    act.wait_ge(conv, b * CONV + CONV)
                    nc.scalar.activation(x_hi[:], x[:], ACT.Copy).then_inc(x_hi_done, 1)
                    act.wait_ge(y_ready, b + 1)
                    wait(act, o_ready, b)
                    if not isinstance(b, int) or b > 0:
                        store(act, b - 1)
                    nc.scalar.activation(y[:], y_sum[:], ACT.Gelu_apprx_tanh).then_inc(y_done, 1)
                    act.wait_ge(par_set, b * 2 + 2)
                    wait(act, stored, b * 16)
                    for g in range(4):
                        out = (r[0], r[1], gi[0], gi[1])[g]
                        for n, (at, size) in enumerate(segments):
                            act.wait_ge(gates, b * 12 + (3 * g + n + 1))
                            nc.scalar.activation(out[:, at:at + size], g_sum[n][:, 0:size], ACT.Sigmoid,
                                                 bias=par[:, 5 + g:6 + g]).then_inc(g_done, 1)
                    act.wait_ge(g_done, b * 12 + 6)
                    for d in range(2):
                        for m, out in enumerate((a, q, r)):
                            if m == 2:
                                act.wait_ge(powers, b * 6 + (3 * d + 2))
                            nc.scalar.activation(out[d][:], r[d][:], ACT.Tanh if m == 2 else ACT.Exp,
                                                 scale=par[:, LRU_COLS + 3 * d + m:LRU_COLS + 3 * d + m + 1]).then_inc(powers, 1)
                    for d in range(2):
                        act.wait_ge(step, b * STEPS + (5 * d + 2))
                        nc.scalar.activation(q[d][:], q[d][:], ACT.Sqrt).then_inc(roots, 1)
                act.wait_ge(o_ready, KC)
                store(act, KC - 1)
                act.wait_ge(stored, 16 * KC)

            @blk.vector
            def _(dve):
                for e, i in blocks(nc.vector):
                    b = e * unroll + i
                    dve.wait_ge(hi_done, b + 1)
                    nc.vector.tensor_tensor(w_lo[:], core.raw[i][:], w_hi[:].bitcast(F32), ALU.subtract).then_inc(core.chunk_done, 1)
                    dve.wait_ge(gw_hi_done, b + 1)
                    nc.vector.tensor_tensor(gw_lo[:], gw[i % 2][:], gw_hi[:].bitcast(F32), ALU.subtract).then_inc(gw_done, 1)
                    wait(dve, roots, b * 2)
                    nc.vector.tensor_copy(par[:, 0:LRU_COLS], core.vec[:, ds(b * LRU_COLS + V_LRU, LRU_COLS)]).then_inc(par_set, 1)
                    nc.vector.tensor_copy(par[:, LRU_COLS:LRU_COLS + 6], decay[:, ds(b * 6, 6)]).then_inc(par_set, 1)
                    dve.wait_ge(x_ready, b + 1)
                    dve.wait_ge(par_set, b * 2 + 2)
                    seqs = ((0, N_LAT), (N_LAT, N_CTX))
                    for n, (tap, shift) in enumerate(((2, 0), (1, -1), (0, -2), (3, 1))):
                        for s, (at, size) in enumerate(seqs):
                            lo, hi = at + max(0, -shift), at + size - max(0, shift)
                            if n == 0:
                                ins = nc.vector.tensor_scalar(x[:, lo:hi], x_sum[:, lo:hi], par[:, 2:3], par[:, 4:5],
                                                              ALU.mult, ALU.add)
                            else:
                                dve.wait_ge(conv, b * CONV + (2 * n + s - 1))
                                ins = nc.vector.scalar_tensor_tensor(x[:, lo:hi], x_sum[:, lo + shift:hi + shift],
                                                                     par[:, tap:tap + 1], x[:, lo:hi], ALU.mult, ALU.add)
                            ins.then_inc(conv, 1)
                    dve.wait_ge(x_hi_done, b + 1)
                    nc.vector.tensor_tensor(x_lo[:], x[:], x_hi[:].bitcast(F32), ALU.subtract).then_inc(x_split, 1)
                    done = 0
                    for d in range(2):
                        dve.wait_ge(g_done, b * 12 + (9 + 3 * d))
                        nc.vector.tensor_tensor(gi[d][:], gi[d][:], x[:], ALU.mult).then_inc(step, 1)
                        dve.wait_ge(powers, b * 6 + (3 * d + 3))
                        nc.vector.scalar_tensor_tensor(q[d][:], q[d][:], 1.0, r[d][:], ALU.add, ALU.mult).then_inc(step, 1)
                        done += 2
                        dve.wait_ge(roots, b * 2 + (d + 1))
                        dve.wait_ge(step, b * STEPS + (done - 1))
                        nc.vector.tensor_tensor(gi[d][:], gi[d][:], q[d][:], ALU.mult).then_inc(step, 1)
                        done += 1
                        dve.wait_ge(step, b * STEPS + done)
                        turn = slice(None, None, -1) if d else slice(None)
                        c, l = slice(N_LAT, TOK), slice(0, N_LAT)
                        nc.vector.tensor_tensor_scan(r[d][:, c][:, turn], a[d][:, c][:, turn], gi[d][:, c][:, turn], 0.0,
                                                     ALU.mult, ALU.add).then_inc(step, 1)
                        done += 1
                        dve.wait_ge(step, b * STEPS + done)
                        end = N_LAT if d else TOK - 1
                        nc.vector.tensor_tensor_scan(r[d][:, l][:, turn], a[d][:, l][:, turn], gi[d][:, l][:, turn],
                                                     r[d][:, end:end + 1], ALU.mult, ALU.add).then_inc(step, 1)
                        done += 1
                    dve.wait_ge(step, b * STEPS + done)
                    nc.vector.tensor_tensor(r[0][:, l], r[0][:, l], r[1][:, l], ALU.add).then_inc(step, 1)
                    done += 1
                    dve.wait_ge(step, b * STEPS + done)
                    dve.wait_ge(y_done, b + 1)
                    nc.vector.tensor_tensor(r[0][:, l], r[0][:, l], y[:], ALU.mult).then_inc(o_ready, 1)
                    assert done == STEPS


def decay_stage(core, decay):
    nc = core.nc
    terms = 9
    lam = core.vec[:, V_LRU:V_LRU + LRU_COLS * KC].rearrange("p (b c) -> p b c", c=LRU_COLS)[:, :, LRU_COLS - 2:]
    with ExitStack() as st:
        neg, mag, e, s, s2, acc = (st.enter_context(nc.sbuf_tensor(f"decay_{n}", [P, KC, 2], F32))
                                   for n in ("neg", "mag", "e", "s", "s2", "acc"))
        step, exps = core.sem("decay_step"), core.sem("decay_exps")
        with core.block() as blk:
            @blk.vector
            def _(dve):
                done = [0]

                def chain(ins):
                    ins.then_inc(step, 1)
                    done[0] += 1
                    dve.wait_ge(step, done[0])

                chain(nc.vector.tensor_scalar(neg[:], lam, -1.0, None, ALU.mult))
                chain(nc.vector.tensor_tensor(mag[:], lam, neg[:], ALU.max))
                dve.wait_ge(exps, 1)
                chain(nc.vector.tensor_scalar(s2[:], e[:], 2.0, None, ALU.add))
                chain(nc.vector.reciprocal(s2[:], s2[:]))
                chain(nc.vector.tensor_tensor(s[:], e[:], s2[:], ALU.mult))
                chain(nc.vector.tensor_tensor(s2[:], s[:], s[:], ALU.mult))
                chain(nc.vector.memset(acc[:], 1.0 / (2 * terms + 1)))
                for n in reversed(range(terms)):
                    chain(nc.vector.tensor_tensor(acc[:], acc[:], s2[:], ALU.mult))
                    chain(nc.vector.tensor_scalar(acc[:], acc[:], 1.0 / (2 * n + 1), None, ALU.add))
                chain(nc.vector.tensor_tensor(acc[:], acc[:], s[:], ALU.mult))
                chain(nc.vector.tensor_scalar(neg[:], neg[:], 0.0, None, ALU.max))
                chain(nc.vector.scalar_tensor_tensor(acc[:], acc[:], 2.0, neg[:], ALU.mult, ALU.add))
                out = decay[:].rearrange("p (b d m) -> p b d m", d=2, m=3)
                for m, f in enumerate((-8.0, -16.0, 8.0)):
                    chain(nc.vector.tensor_scalar(out[:, :, :, m], acc[:], f, None, ALU.mult))

            @blk.scalar
            def _(act):
                act.wait_ge(step, 2)
                nc.scalar.activation(e[:], mag[:], ACT.Exp, scale=-1.0).then_inc(exps, 1)


def out_stage(core, x, gain_row, load):
    nc, io = core.nc, core.io
    first = core.chunks
    core.chunks += KC
    with ExitStack() as st:
        hi = [st.enter_context(nc.sbuf_tensor(f"out_hi{i}", [P, KC, D], F32R)) for i in range(2)]
        lo = [st.enter_context(nc.sbuf_tensor(f"out_lo{i}", [P, KC, D], F32R)) for i in range(2)]
        change = st.enter_context(nc.sbuf_tensor("out_change", [P, D], F32))
        sums = [[st.enter_context(nc.psum_tensor(f"out_sums{i}{n}", [P, BANK], F32)) for n in range(2)] for i in range(2)]
        x_landed, hi_done, product, scaled, added = (core.sem(f"out_{n}") for n in (
            "x_landed", "hi_done", "product", "scaled", "added"))
        with core.block() as blk:
            @blk.sync
            def _(sp):
                for c in range(KC):
                    src = (io["lru_w_out"][0] if c % 2 else core.o_lru).rearrange("(k p) d -> p k d", p=P)
                    load_chunk(core, sp, first + c, src[:, c // 2 * 2:c // 2 * 2 + 2, :],
                               lambda place: place[:].rearrange("p (k d) -> p k d", k=2))
                for dst, src in load:
                    sp.dma_start(dst, src).then_inc(x_landed, 16)

            @blk.scalar
            def _(act):
                for c in range(KC):
                    landed(core, act, first + c)
                    nc.scalar.activation(hi[c % 2][:, c // 2 * 2:c // 2 * 2 + 2, :],
                                         core.raw[(first + c) % RING][:].rearrange("p (k d) -> p k d", k=2), ACT.Copy)\
                      .then_inc(hi_done, 1)

            @blk.vector
            def _(dve):
                for c in range(KC):
                    dve.wait_ge(hi_done, c + 1)
                    ks = slice(c // 2 * 2, c // 2 * 2 + 2)
                    nc.vector.tensor_tensor(lo[c % 2][:, ks, :], core.raw[(first + c) % RING][:].rearrange("p (k d) -> p k d", k=2),
                                            hi[c % 2][:, ks, :].bitcast(F32), ALU.subtract).then_inc(core.chunk_done, 1)
                dve.wait_ge(x_landed, 16 * len(load))
                for t in range(T_LAT):
                    dve.wait_ge(product, t + 1)
                    wait(dve, added, t)
                    for n in range(2):
                        nc.vector.tensor_tensor(change[:, BANK * n:BANK * n + BANK], sums[t % 2][n][:],
                                                gain_row[:, BANK * n:BANK * n + BANK], ALU.mult).then_inc(scaled, 1)
                    dve.wait_ge(scaled, 2 * t + 2)
                    nc.vector.tensor_tensor(x[:, t, :], x[:, t, :], change[:], ALU.add).then_inc(added, 1)

            @blk.tensor
            def _(pe):
                for t in range(T_LAT):
                    wait(pe, scaled, 2 * (t - 1))
                    for k in range(KC):
                        if t == 0 and k % 2 == 0:
                            chunk_done(core, pe, first + k + 1)
                        for m, (o, w) in enumerate(((hi[0], hi[1]), (hi[0], lo[1]), (lo[0], hi[1]))):
                            for n in range(2):
                                last = nc.tensor.matmul(sums[t % 2][n][:], o[:, k, t * P:t * P + P],
                                                        w[:, k, BANK * n:BANK * n + BANK],
                                                        start=k == 0 and m == 0, stop=k == KC - 1 and m == 2)
                    last.then_inc(product, 1)


def final_stage(core, src, gain_row, dst):
    nc = core.nc
    with ExitStack() as st:
        x = st.enter_context(nc.sbuf_tensor("fin_x", [P, T_LAT, D], F32))
        y = st.enter_context(nc.sbuf_tensor("fin_y", [P, T_LAT, D], F32))
        squares = st.enter_context(nc.sbuf_tensor("fin_squares", [P, D], F32))
        ssq, rstd, eps = (st.enter_context(nc.sbuf_tensor(f"fin_{n}", [P, c], F32)) for n, c in (
            ("ssq", T_LAT), ("rstd", T_LAT), ("eps", 1)))
        x_landed = [core.sem(f"fin_x_landed{t}") for t in range(T_LAT)]
        squared, root, inverse, done, stored, eps_set = (core.sem(f"fin_{n}") for n in (
            "squared", "root", "inverse", "done", "stored", "eps_set"))
        with core.block() as blk:
            @blk.sync
            def _(sp):
                for t in range(T_LAT):
                    sp.dma_start(x[:, t, :], src[t * P:t * P + P, :]).then_inc(x_landed[t], 16)
                for t in range(T_LAT):
                    sp.wait_ge(done, t + 1)
                    sp.dma_start(dst[t * P:t * P + P, :], y[:, t, :]).then_inc(stored, 16)
                sp.wait_ge(stored, 16 * T_LAT)

            @blk.scalar
            def _(act):
                act.wait_ge(eps_set, 1)
                for t in range(T_LAT):
                    act.wait_ge(x_landed[t], 16)
                    wait(act, squared, t)
                    nc.scalar.activation(squares[:], x[:, t, :], ACT.Square, accum_out=ssq[:, t:t + 1]).then_inc(squared, 1)
                    act.wait_ge(squared, t + 1)
                    nc.scalar.activation(ssq[:, t:t + 1], ssq[:, t:t + 1], ACT.Sqrt, bias=eps[:], scale=1.0 / D).then_inc(root, 1)

            @blk.vector
            def _(dve):
                nc.vector.memset(eps[:], EPS).then_inc(eps_set, 1)
                for t in range(T_LAT):
                    dve.wait_ge(root, t + 1)
                    nc.vector.reciprocal(rstd[:, t:t + 1], ssq[:, t:t + 1]).then_inc(inverse, 1)
                    dve.wait_ge(inverse, t + 1)
                    nc.vector.scalar_tensor_tensor(y[:, t, :], x[:, t, :], rstd[:, t:t + 1], gain_row, ALU.mult, ALU.mult)\
                      .then_inc(done, 1)


def program(nc, io, out):
    tokens = "(t p) d -> p t d"
    with ExitStack() as st:
        core = Core(nc, io, st)
        setup(core)
        modulation_stage(core, 0)
        x_in = [io["x"][0], io["ctx"][0]]
        x_dram = [core.x_lat, core.x_ctx]
        spans = [slice(0, T_LAT), slice(T_LAT, T_LAT + T_CTX)]

        with ExitStack() as s0:
            x = s0.enter_context(nc.sbuf_tensor("x0", [P, T_LAT + T_CTX, D], F32))
            rows = s0.enter_context(nc.sbuf_tensor("rows0", [P, 4, D], F32))
            scales = [(rows[:, 2 * s + n, :], core.mod_col(0, 1 - n, s)) for s in range(2) for n in range(2)]
            broadcast_rows(core, "rows0a", scales)
            with ExitStack() as s1:
                ht = s1.enter_context(nc.sbuf_tensor("ht0", [P, KC, PADDED], F32))
                clear_padding(core, ht)
                norm_stage(core, "norm0a", x, rows, T_LAT + T_CTX, into=padded_place(ht),
                           load=[(x[:, spans[s], :], x_in[s].rearrange(tokens, p=P)) for s in range(2)])
                gains = s1.enter_context(nc.sbuf_tensor("pool_gain", [P, 2, KC], F32))
                pool_gains(core, gains)
                broadcast_rows(core, "rows0b", [(rows[:, s, :], gains[:, s, :]) for s in range(2)])
                pool_stage(core, ht, x, rows)
            scales = [(rows[:, 2 * s + n, :], core.mod_col(0, 4 - n, s)) for s in range(2) for n in range(2)]
            broadcast_rows(core, "rows0c", scales)
            feed_forward_choice(core, 0, 2, x, rows, [(x_dram[s].rearrange(tokens, p=P), x[:, spans[s], :]) for s in range(2)])
        with ExitStack() as s0:
            g2 = s0.enter_context(nc.sbuf_tensor("g2_0", [P, 2, D], F32))
            broadcast_rows(core, "rows0d", [(g2[:, s, :], core.mod_col(0, 5, s)) for s in range(2)])
            experts_stage(core, "moe0", 0, 2, g2, core.x_lat, core.x_ctx)

        with ExitStack() as s0:
            t_hi = s0.enter_context(nc.sbuf_tensor("t_hi", [P, KC, TOK], F32R))
            t_lo = s0.enter_context(nc.sbuf_tensor("t_lo", [P, KC, TOK], F32R))
            with ExitStack() as s1:
                x = s1.enter_context(nc.sbuf_tensor("x1a", [P, T_LAT + T_CTX, D], F32))
                rows = s1.enter_context(nc.sbuf_tensor("rows1a", [P, 4, D], F32))
                scales = [(rows[:, 2 * s + n, :], core.mod_col(1, 1 - n, s)) for s in range(2) for n in range(2)]
                broadcast_rows(core, "rows1a", scales)
                norm_stage(core, "norm1a", x, rows, T_LAT + T_CTX, split=(t_hi, t_lo),
                           load=[(x[:, spans[s], :], x_dram[s].rearrange(tokens, p=P)) for s in range(2)])
            decay = s0.enter_context(nc.sbuf_tensor("decay", [P, 6 * KC], F32))
            decay_stage(core, decay)
            lru_stage(core, t_hi, t_lo, decay)
        with ExitStack() as s0:
            x = s0.enter_context(nc.sbuf_tensor("x1b", [P, T_LAT, D], F32))
            rows = s0.enter_context(nc.sbuf_tensor("rows1b", [P, 2, D], F32))
            broadcast_rows(core, "rows1b", [(rows[:, 0, :], core.mod_col(1, 2, 0))])
            out_stage(core, x, rows[:, 0, :], [(x[:], core.x_lat.rearrange(tokens, p=P))])
            broadcast_rows(core, "rows1c", [(rows[:, n, :], core.mod_col(1, 4 - n, 0)) for n in range(2)])
            feed_forward_choice(core, 1, 1, x, rows, [(core.x_fin.rearrange(tokens, p=P), x[:])])
        with ExitStack() as s0:
            g2 = s0.enter_context(nc.sbuf_tensor("g2_1", [P, 1, D], F32))
            broadcast_rows(core, "rows1d", [(g2[:, 0, :], core.mod_col(1, 5, 0))])
            experts_stage(core, "moe1", 1, 1, g2, core.x_fin, None)
        with ExitStack() as s0:
            gain = s0.enter_context(nc.sbuf_tensor("final_gain_row", [P, D], F32))
            broadcast_rows(core, "rows2", [(gain[:], core.vec[:, V_FG:V_FG + KC])])
            final_stage(core, core.x_fin, gain[:], out)


def clear_padding(core, ht):
    nc = core.nc
    cleared = core.sem("padding_cleared")
    with core.block() as blk:
        @blk.vector
        def _(dve):
            gaps = ((0, OFF_LAT), (OFF_LAT + N_LAT, OFF_CTX), (OFF_CTX + N_CTX, PADDED))
            for a, b in gaps:
                nc.vector.memset(ht[:, :, a:b], 0.0).then_inc(cleared, 1)
            dve.wait_ge(cleared, len(gaps))


def pool_gains(core, gains):
    nc = core.nc
    made = core.sem("pool_gains_made")
    with core.block() as blk:
        @blk.vector
        def _(dve):
            for s in range(2):
                nc.vector.tensor_tensor(gains[:, s, :], core.vec[:, V_PS:V_PS + KC], core.mod_col(0, 2, s), ALU.mult)\
                  .then_inc(made, 1)
            dve.wait_ge(made, 2)


def feed_forward_choice(core, block, streams, x, rows, seed):
    nc, io = core.nc, core.io
    with ExitStack() as st:
        w_router = st.enter_context(nc.sbuf_tensor(f"w_router{block}", [P, KC, EXPERTS], F32))
        logits = st.enter_context(nc.psum_tensor(f"logits{block}", [P, BANK], F32))
        norm_stage(core, f"norm{block}b", x, rows, T_LAT + (T_CTX if streams == 2 else 0), router=(w_router, logits),
                   load=[(w_router[:], io["moe_router"][block].rearrange("(k p) e -> p k e", p=P))], seed=seed)
        beside = None
        if block == 0:
            beside = Modulation(core, 1, [st.enter_context(nc.psum_tensor(f"mod1_sums{i}", [P, BANK], F32)) for i in range(2)])
        choice_stage(core, f"choice{block}", logits, streams, beside)


_INS = ("x", "ctx", "vecs", "mod_b", "edge", "mod_w", "pool_w", "lru_w_in", "lru_wa", "lru_wx", "lru_w_out",
        "moe_router", "moe_w_gate", "moe_w_up", "moe_w_down")


def kernel(**inputs):
    import numpy as np
    import concourse.bacc as bacc
    from concourse.bass_utils import run_bass_kernel_spmd

    inputs = {name: np.asarray(a) for name, a in inputs.items()}

    def by_block(name, d=None):
        return inputs[name][0].reshape(-1, KC, P).transpose(1, 0, 2)

    lru = np.concatenate([by_block(n) for n in ("lru_conv_w", "lru_conv_b", "lru_ba", "lru_bx", "lru_lam")], axis=1)
    inputs["vecs"] = np.concatenate([inputs[n].reshape(-1, P) for n in ("c", "c_ctx", "pool_scale", "final_gain")]
                                    + [lru.reshape(-1, P)], axis=0)
    inputs["mod_b"] = inputs["mod_b"].reshape(-1, P)
    edge = np.zeros((len(WINDOWS), 2, PAD), np.float32)
    for g, w in enumerate(WINDOWS):
        for c in range(PAD):
            edge[g, 0, c] = 1.0 / min(w, c + w // 2)
            edge[g, 1, c] = 1.0 / min(w, PAD - c + w // 2)
    inputs["edge"] = edge.reshape(-1)

    nc = bacc.Bacc("TRN2", target_bir_lowering=False, num_devices=1)
    arrays, io = {}, {}
    for name in _INS:
        a = np.ascontiguousarray(inputs[name])
        arrays[f"in_{name}"] = a
        io[name] = nc.dram_tensor(f"in_{name}", a.shape, mybir.dt.from_np(a.dtype), kind="ExternalInput").ap()
    out = nc.dram_tensor("out_x", (1, N_LAT, D), F32, kind="ExternalOutput").ap()
    program(nc, io, out[0])
    result = run_bass_kernel_spmd(nc, [arrays], core_ids=[0])
    return result.results[0]["out_x"]
```

```python
from contextlib import ExitStack, contextmanager

import concourse.bass as bass
from concourse import mybir

P = 128
D = 1024
KC = D // P
N_LAT, N_CTX = 1024, 256
T_LAT, T_CTX = N_LAT // P, N_CTX // P
TOK = N_LAT + N_CTX
EXPERTS = 16
SLOTS_LAT = 2 * N_LAT // EXPERTS
SLOTS_CTX = 2 * N_CTX // EXPERTS
WINDOWS = (2, 4, 8, 16)
EPS = 1e-6
RING = 4
CHUNK = 2048
MOD_BESIDE_POOL = 6
EXP_CHUNKS = 12
LRU_COLS = 11
BANK = 512

PAD = 8
OFF_LAT = PAD
OFF_CTX = OFF_LAT + N_LAT + 2 * PAD
PADDED = OFF_CTX + N_CTX + PAD

F32 = mybir.dt.float32
F32R = mybir.dt.float32r
U32 = mybir.dt.uint32
ACT = mybir.ActivationFunctionType
ALU = mybir.AluOpType
AX = mybir.AxisListType.X
ds = bass.ds

V_C, V_CC, V_PS, V_FG, V_LRU = 0, 8, 16, 24, 32
N_VECS = V_LRU + LRU_COLS * KC


class Core:

    def __init__(self, nc, io, stack):
        self.nc, self.io, self.stack = nc, io, stack
        self.stage_sems, self.stale_sems = [], []
        self.chunks = 0
        def sb(name, shape, dt=F32):
            return stack.enter_context(nc.sbuf_tensor(name, shape, dt))

        def lasting(name):
            return stack.enter_context(nc.semaphore(name))

        self.h_lat = nc.dram_tensor("h_lat", [N_LAT, D], F32).ap()
        self.h_ctx = nc.dram_tensor("h_ctx", [N_CTX, D], F32).ap()
        self.x_lat = nc.dram_tensor("x_lat", [N_LAT, D], F32).ap()
        self.x_ctx = nc.dram_tensor("x_ctx", [N_CTX, D], F32).ap()
        self.x_fin = nc.dram_tensor("x_fin", [N_LAT, D], F32).ap()
        self.o_lru = nc.dram_tensor("o_lru", [D, N_LAT], F32).ap()
        self.raw = [sb(f"raw{i}", [P, CHUNK]) for i in range(RING)]
        self.ident = sb("ident", [P, P])
        self.ones = sb("ones", [P, P])
        self.vec = sb("vec", [P, N_VECS])
        self.mod_bias = sb("mod_bias", [P, 96])
        self.silu_c = sb("silu_c", [P, KC, 2])
        self.mod = [sb(f"mod{i}", [P, 96]) for i in range(2)]
        self.gate_t = sb("gate_t", [P, 48])
        self.index_t = sb("index_t", [P, 48], U32)
        self.unused = sb("unused", [P, 1])
        self.raw_landed = [lasting(f"raw_landed{i}") for i in range(RING)]
        self.rows_made = 0
        self.diag_ready, self.spread_ready, self.row_ready = (lasting(n) for n in ("diag_ready", "spread_ready", "row_ready"))
        self.placed = lasting("placed")
        self.chunk_done = lasting("chunk_done")

    def sem(self, name):
        self.stage_sems.append(self.nc.alloc_semaphore(name=name))
        return self.stage_sems[-1]

    @contextmanager
    def block(self):
        with self.nc.Block() as block:
            @block.gpsimd
            def _(pool):
                for sem in self.stale_sems:
                    pool.sem_clear(sem)
            yield block
        for sem in self.stale_sems:
            self.nc.release_semaphore(sem)
        self.stale_sems, self.stage_sems = self.stage_sems, []

    def mod_col(self, block, part, stream):
        return self.mod[block][:, 16 * part:16 * part + 16].rearrange("p (k s) -> p k s", s=2)[:, :, stream]


def wait(eng, sem, value):
    if isinstance(value, int) and value <= 0:
        return
    eng.wait_ge(sem, value)


def landed(core, eng, first, e=0, per=0):
    eng.wait_ge(core.raw_landed[first % RING], e * (16 * per // RING) + 16 * (first // RING + 1))


def load_chunk(core, sp, first, src, dst=None, e=0, per=0):
    sp.wait_ge(core.chunk_done, e * per + (first + 1))
    place = core.raw[first % RING]
    sp.dma_start(place[:] if dst is None else dst(place), src).then_inc(core.raw_landed[first % RING], 16)


def chunk_done(core, eng, first, e=0, per=0):
    eng.wait_ge(core.chunk_done, e * per + (RING + first + 1))


def pairs(engine, streams):
    yield 0, 0
    with engine.Fori(1, T_LAT // 2) as e:
        yield e, 0
    if streams == 2:
        yield T_LAT // 2, 1


def expert_chunk(io, block, s, e):
    if s < 8:
        w = io["moe_w_up" if s % 2 else "moe_w_gate"][block]
        return w.rearrange("e (k p) f -> p e k f", p=P)[:, ds(e, 1), :, 256 * (s // 2):256 * (s // 2) + 256]
    w = io["moe_w_down"][block]
    return w.rearrange("e (k p) f -> p e k f", p=P)[:, ds(e, 1), 2 * (s - 8):2 * (s - 8) + 2, :]


def load_expert_chunk(core, sp, block, first, s, e=0):
    shape = dict(e=1, k=KC if s < 8 else 2)
    load_chunk(core, sp, first + s, expert_chunk(core.io, block, s, e),
               lambda place: place[:].rearrange("p (e k f) -> p e k f", **shape), e, EXP_CHUNKS)



def setup(core):
    nc, io = core.nc, core.io
    with ExitStack() as st:
        rows = st.enter_context(nc.sbuf_tensor("vec_rows", [N_VECS, P], F32))
        brows = st.enter_context(nc.sbuf_tensor("modb_rows", [96, P], F32))
        turned = st.enter_context(nc.psum_tensor("turned", [P, 2, BANK], F32))
        rows_landed, made, turned_s, vec_ready, silu_ready = (
            core.sem(n) for n in ("rows_landed", "consts_made", "vecs_turned", "vec_ready", "silu_ready"))
        with core.block() as block:
            @block.sync
            def _(sp):
                sp.dma_start(rows[:], io["vecs"]).then_inc(rows_landed, 16)
                sp.dma_start(brows[:], io["mod_b"]).then_inc(rows_landed, 16)

            @block.gpsimd
            def _(pool):
                nc.gpsimd.memset(core.ident[:], 0.0).then_inc(made, 1)
                nc.gpsimd.memset(core.ones[:], 1.0).then_inc(made, 1)
                pool.wait_ge(made, 2)
                nc.gpsimd.affine_select(out=core.ident[:], in_=core.ident[:], compare_op=ALU.not_equal, fill=1.0,
                                        base=0, pattern=[[-1, P]], channel_multiplier=1).then_inc(made, 1)

            @block.tensor
            def _(pe):
                pe.wait_ge(rows_landed, 32)
                pe.wait_ge(made, 3)
                nc.tensor.transpose(turned[:, 0, 0:N_VECS], rows[:], core.ident[0:N_VECS, 0:N_VECS]).then_inc(turned_s, 1)
                nc.tensor.transpose(turned[:, 1, 0:96], brows[:], core.ident[0:96, 0:96]).then_inc(turned_s, 1)

            @block.vector
            def _(dve):
                dve.wait_ge(turned_s, 2)
                nc.vector.tensor_copy(core.vec[:], turned[:, 0, 0:N_VECS]).then_inc(vec_ready, 1)
                nc.vector.tensor_copy(core.mod_bias[:], turned[:, 1, 0:96]).then_inc(vec_ready, 1)

            @block.scalar
            def _(act):
                act.wait_ge(vec_ready, 1)
                nc.scalar.activation(core.silu_c[:, :, 0], core.vec[:, V_C:V_C + KC], ACT.Silu).then_inc(silu_ready, 1)
                nc.scalar.activation(core.silu_c[:, :, 1], core.vec[:, V_CC:V_CC + KC], ACT.Silu).then_inc(silu_ready, 1)


class Modulation:
    BODY = 2

    def __init__(self, core, block, stack, start=0, strips=6 * D // BANK):
        nc = core.nc
        self.core, self.block, self.start, self.STRIPS = core, block, start, strips
        self.first = core.chunks
        core.chunks += 2 * strips
        self.row_banks = [stack.enter_context(nc.psum_tensor(f"mod{block}_{start}_rows{i}", [P, BANK], F32)) for i in range(2)]
        self.col_bank = stack.enter_context(nc.psum_tensor(f"mod{block}_{start}_cols", [P, BANK], F32))
        self.rows = [stack.enter_context(nc.sbuf_tensor(f"mod{block}_{start}_row{i}", [2, BANK], F32)) for i in range(2)]
        self.copied = core.sem(f"mod_copied{block}_{start}")
        self.turned = core.sem(f"mod_turned{block}_{start}")
        self.ready = core.sem(f"mod_ready{block}_{start}")

    def strips(self, engine):
        for i in range(self.BODY):
            yield 0, i
        with engine.Fori(1, self.STRIPS // self.BODY) as e:
            for i in range(self.BODY):
                yield e, i

    def load(self, sp, between=None):
        w = self.core.io["mod_w"][self.block].rearrange("(h k p) (u m) -> p h k u m", p=P, h=2, m=BANK)
        for e, i in self.strips(self.core.nc.sync):
            for h in range(2):
                load_chunk(self.core, sp, self.first + 2 * i + h, w[:, h, :, ds(e * self.BODY + (self.start + i), 1), :],
                           lambda place: place[:].rearrange("p (k u m) -> p k u m", k=KC // 2, u=1), e, 2 * self.BODY)
            if between and isinstance(e, int) and i == self.BODY - 1:
                between()

    def products(self, pe):
        core, nc = self.core, self.core.nc

        def turn(i, count):
            pe.wait_ge(self.copied, count + 1)
            for c in range(BANK // P):
                last = nc.tensor.matmul(self.col_bank[:, ds(count * 8 + 2 * c, 2)], self.rows[i][:, c * P:(c + 1) * P],
                                        core.ident[0:2, 0:2], start=True, stop=True)
            last.then_inc(self.turned, 1)

        for e, i in self.strips(nc.tensor):
            strip = e * self.BODY + i
            wait(pe, self.copied, strip - 1)
            for h in range(2):
                at = self.first + 2 * i + h
                landed(core, pe, at, e, 2 * self.BODY)
                for k in range(KC // 2):
                    last = nc.tensor.matmul(self.row_banks[i][0:2, :], core.silu_c[:, KC // 2 * h + k, :],
                                            core.raw[at % RING][:, BANK * k:BANK * (k + 1)],
                                            start=h == 0 and k == 0, stop=h == 1 and k == KC // 2 - 1)
                last.then_inc(core.chunk_done, 1)
            if not isinstance(e, int) or strip > 0:
                turn(1 - i, strip - 1)
        turn(self.BODY - 1, self.STRIPS - 1)

    def copy_out(self, act):
        nc = self.core.nc
        for e, i in self.strips(nc.scalar):
            chunk_done(self.core, act, self.first + 2 * i + 1, e, 2 * self.BODY)
            wait(act, self.turned, e * self.BODY + (i - 1))
            nc.scalar.activation(self.rows[i][:], self.row_banks[i][0:2, :], ACT.Copy).then_inc(self.copied, 1)

    def finish(self, dve):
        core, nc = self.core, self.core.nc
        dve.wait_ge(self.turned, self.STRIPS)
        at, n = 8 * self.start, 8 * self.STRIPS
        out = core.mod[self.block][:, at:at + n].rearrange("p (c s) -> p c s", s=2)
        bias = core.mod_bias[:, 48 * self.block + at // 2:48 * self.block + (at + n) // 2]
        nc.vector.tensor_tensor(out, self.col_bank[:, 0:n].rearrange("p (c s) -> p c s", s=2),
                                bias.unsqueeze(2).to_broadcast([P, n // 2, 2]), ALU.add).then_inc(self.ready, 1)
        dve.wait_ge(self.ready, 1)
        for part in (1, 4):
            if at <= 16 * part < at + n:
                cols = core.mod[self.block][:, 16 * part:16 * part + 16]
                nc.vector.tensor_scalar(cols, cols, 1.0, None, ALU.add).then_inc(self.ready, 1)


def modulation_stage(core, block, x, load, rstd):
    nc = core.nc
    tiles = x.shape[1]
    with ExitStack() as st:
        mod = Modulation(core, block, st)
        squares = st.enter_context(nc.sbuf_tensor("first_squares", [P, D], F32))
        eps = st.enter_context(nc.sbuf_tensor("first_eps", [P, 1], F32))
        x_landed, squared, root, rstd_ready = (core.sem(f"first_{n}") for n in ("x_landed", "squared", "root", "rstd_ready"))
        with core.block() as blk:
            @blk.sync
            def _(sp):
                def load_x():
                    for dst, src in load:
                        sp.dma_start(dst, src).then_inc(x_landed, 16)
                mod.load(sp, between=load_x)

            @blk.tensor
            def _(pe):
                mod.products(pe)

            @blk.scalar
            def _(act):
                mod.copy_out(act)
                act.wait_ge(squared, tiles + 1)
                nc.scalar.activation(rstd, rstd, ACT.Sqrt, bias=eps[:], scale=1.0 / D).then_inc(root, 1)

            @blk.vector
            def _(dve):
                nc.vector.memset(core.unused[:], 0.0).then_inc(core.chunk_done, RING)
                nc.vector.memset(eps[:], EPS).then_inc(squared, 1)
                dve.wait_ge(x_landed, 16 * len(load))
                for t in range(tiles):
                    dve.wait_ge(squared, t + 1)
                    nc.vector.tensor_tensor_reduce(squares[:], x[:, t, :], x[:, t, :], 1.0, 0.0, ALU.mult, ALU.add,
                                                   accum_out=rstd[:, t:t + 1]).then_inc(squared, 1)
                mod.finish(dve)
                dve.wait_ge(root, 1)
                nc.vector.reciprocal(rstd, rstd).then_inc(rstd_ready, 1)


def broadcast_rows(core, name, wanted):
    nc = core.nc
    with ExitStack() as st:
        diag = [st.enter_context(nc.sbuf_tensor(f"{name}_diag{i}", [P, KC, P], F32)) for i in range(2)]
        spread = [st.enter_context(nc.psum_tensor(f"{name}_spread{i}", [P, 2, BANK], F32)) for i in range(2)]
        diag_ready, spread_ready, row_ready = core.diag_ready, core.spread_ready, core.row_ready
        base = core.rows_made
        core.rows_made += len(wanted)
        with core.block() as blk:
            @blk.vector
            def _(dve):
                for i, (_, col) in enumerate(wanted):
                    wait(dve, spread_ready, base + i - 1 if i > 1 else 0)
                    nc.vector.tensor_tensor(diag[i % 2][:], core.ident[:].unsqueeze(1).to_broadcast([P, KC, P]),
                                            col.unsqueeze(2).to_broadcast([P, KC, P]), ALU.mult).then_inc(diag_ready, 1)

            @blk.tensor
            def _(pe):
                for i in range(len(wanted)):
                    pe.wait_ge(diag_ready, base + i + 1)
                    wait(pe, row_ready, base + i - 1 if i > 1 else 0)
                    for n in range(2):
                        last = nc.tensor.matmul(spread[i % 2][:, n, :], core.ones[:],
                                                diag[i % 2][:, 4 * n:4 * n + 4, :].rearrange("p k m -> p (k m)"),
                                                start=True, stop=True)
                    last.then_inc(spread_ready, 1)

            @blk.scalar
            def _(act):
                for i, (row, _) in enumerate(wanted):
                    act.wait_ge(spread_ready, base + i + 1)
                    nc.scalar.activation(row, spread[i % 2][:].rearrange("p n m -> p (n m)"), ACT.Copy)\
                      .then_inc(row_ready, 1)



def norm_stage(core, name, x, rows, tiles, into=None, split=None, router=None, load=(), extra=(), seed=(), rstd=None):
    nc = core.nc
    streams = 2 if tiles > T_LAT else 1
    known = rstd is not None
    with ExitStack() as st:
        junk = st.enter_context(nc.sbuf_tensor(f"{name}_squares", [P, D], F32))
        ssq = [st.enter_context(nc.sbuf_tensor(f"{name}_ssq{i}", [P, 1], F32)) for i in range(2)]
        inverse = [st.enter_context(nc.sbuf_tensor(f"{name}_inverse{i}", [P, 1], F32)) for i in range(2)]
        eps = st.enter_context(nc.sbuf_tensor(f"{name}_eps", [P, 1], F32))
        h = [st.enter_context(nc.sbuf_tensor(f"{name}_h{i}", [P, D], F32)) for i in range(2)]
        turned = [st.enter_context(nc.psum_tensor(f"{name}_turned{i}", [P, 4, P], F32)) for i in range(4)]
        if router:
            w_router, logits = router
            ht = [st.enter_context(nc.sbuf_tensor(f"{name}_ht{i}", [P, KC, P], F32)) for i in range(2)]
        (first_landed, rest_landed, extra_landed, squared, eps_set, root, rstd_ready, scaled, h_ready, turned_lo, turned_hi,
         out_lo, out_hi) = (core.sem(f"{name}_{n}") for n in (
            "first_landed", "rest_landed", "extra_landed", "squared", "eps_set", "root", "rstd_ready", "scaled", "h_ready",
            "turned_lo", "turned_hi", "out_lo", "out_hi"))
        stored0, stored1, seeded, routed = (
            core.sem(f"{name}_{n}") if router else None for n in ("stored0", "stored1", "seeded", "routed"))
        stored = (stored0, stored1)
        copies = 2 if split else 1
        LAST = (tiles // 2 - 1, streams - 1, 1)

        def steps(engine):
            for e, stream in pairs(engine, streams):
                for i in range(2):
                    if i == 1:
                        before = (e, stream, 0)
                    elif isinstance(e, int) and e == 0:
                        before = None
                    else:
                        before = (e - 1, 0, 1)
                    yield before, (e, stream, i)

        def x_landed(eng, e):
            if isinstance(e, int) and e == 0:
                eng.wait_ge(first_landed, 16)
            else:
                eng.wait_ge(rest_landed, 16 * (len(load) - 1))

        with core.block() as blk:
            @blk.sync
            def _(sp):
                for n, (dst, src) in enumerate(load):
                    sp.dma_start(dst, src).then_inc(rest_landed if n else first_landed, 16)
                for dst, src in extra:
                    sp.dma_start(dst, src).then_inc(extra_landed, 16)
                for dst, src in seed:
                    sp.dma_start(dst, src).then_inc(seeded, 16)
                if router:
                    for e, stream in pairs(nc.sync, streams):
                        out = (core.h_ctx if stream else core.h_lat).rearrange("(t p) d -> p t d", p=P)
                        for i in range(2):
                            sp.wait_ge(h_ready, e * 2 + (i + 1))
                            sp.dma_start(out[:, ds(e * 2 + (i - T_LAT * stream), 1), :], h[i][:].unsqueeze(1))\
                              .then_inc(stored[i], 16)
                    for i in range(2):
                        sp.wait_ge(stored[i], 16 * (tiles // 2))
                if seed:
                    sp.wait_ge(seeded, 16 * len(seed))

            @blk.scalar
            def _(act):
                def root_mean_square(e, i):
                    t = e * 2 + i
                    if load:
                        x_landed(act, e)
                    wait(act, squared, t)
                    wait(act, rstd_ready, e * 2 + (i - 1))
                    nc.scalar.activation(junk[:], x[:, ds(t, 1), :].rearrange("p a d -> p (a d)"), ACT.Square,
                                         accum_out=ssq[i][:]).then_inc(squared, 1)
                    act.wait_ge(squared, t + 1)
                    nc.scalar.activation(ssq[i][:], ssq[i][:], ACT.Sqrt, bias=eps[:], scale=1.0 / D).then_inc(root, 1)

                def copy_lo(e, stream, i):
                    t = e * 2 + i
                    act.wait_ge(turned_lo, e * 2 + (i + 1))
                    if router:
                        wait(act, routed, e * 2 + (i - 1))
                        nc.scalar.activation(ht[i][:, 0:4, :], turned[2 * i][:], ACT.Copy).then_inc(out_lo, 1)
                    elif split:
                        nc.scalar.activation(split[0][:, 0:4, ds(t * P, P)], turned[2 * i][:], ACT.Copy).then_inc(out_lo, 1)
                        act.wait_ge(turned_hi, e * 2 + (i + 1))
                        nc.scalar.activation(split[0][:, 4:8, ds(t * P, P)], turned[2 * i + 1][:], ACT.Copy)\
                          .then_inc(out_lo, 1)
                    else:
                        nc.scalar.activation(into(0, t, stream), turned[2 * i][:], ACT.Copy).then_inc(out_lo, 1)

                if not known:
                    act.wait_ge(eps_set, 1)
                for before, (e, stream, i) in steps(nc.scalar):
                    if not known:
                        root_mean_square(e, i)
                    if before:
                        copy_lo(*before)
                copy_lo(*LAST)

            @blk.vector
            def _(dve):
                def scale(e, stream, i):
                    t = e * 2 + i
                    if not known:
                        dve.wait_ge(root, t + 1)
                        wait(dve, scaled, e * 2 + (i - 1))
                        nc.vector.reciprocal(inverse[i][:], ssq[i][:]).then_inc(rstd_ready, 1)
                        dve.wait_ge(rstd_ready, t + 1)
                    wait(dve, turned_hi, e * 2 + (i - 1))
                    if router:
                        wait(dve, stored[i], e * 16)
                    nc.vector.scalar_tensor_tensor(h[i][:], x[:, ds(t, 1), :].rearrange("p a d -> p (a d)"),
                                                   rstd[:, ds(t, 1)] if known else inverse[i][:], rows[:, 2 * stream, :],
                                                   ALU.mult, ALU.mult).then_inc(scaled, 1)
                    dve.wait_ge(scaled, t + 1)
                    nc.vector.tensor_tensor(h[i][:], h[i][:], rows[:, 2 * stream + 1, :], ALU.add).then_inc(h_ready, 1)

                def copy_hi(e, stream, i):
                    t = e * 2 + i
                    dve.wait_ge(turned_hi, e * 2 + (i + 1))
                    if router:
                        wait(dve, routed, e * 2 + (i - 1))
                        nc.vector.tensor_copy(ht[i][:, 4:8, :], turned[2 * i + 1][:]).then_inc(out_hi, 1)
                    elif split:
                        for n in range(2):
                            dve.wait_ge(out_lo, e * 4 + (2 * i + n + 1))
                            nc.vector.tensor_tensor(split[1][:, 4 * n:4 * n + 4, ds(t * P, P)], turned[2 * i + n][:],
                                                    split[0][:, 4 * n:4 * n + 4, ds(t * P, P)].bitcast(F32),
                                                    ALU.subtract).then_inc(out_hi, 1)
                    else:
                        nc.vector.tensor_copy(into(4, t, stream), turned[2 * i + 1][:]).then_inc(out_hi, 1)

                if not known:
                    nc.vector.memset(eps[:], EPS).then_inc(eps_set, 1)
                for before, this in steps(nc.vector):
                    scale(*this)
                    if before:
                        copy_hi(*before)
                copy_hi(*LAST)

            @blk.tensor
            def _(pe):
                def route(e, stream, i):
                    pe.wait_ge(out_lo, e * 2 + (i + 1))
                    pe.wait_ge(out_hi, e * 2 + (i + 1))
                    for k in range(KC):
                        last = nc.tensor.matmul(logits[:, ds((e * 2 + i) * EXPERTS, EXPERTS)], ht[i][:, k, :],
                                                w_router[:, k, :], start=k == 0, stop=k == KC - 1)
                    last.then_inc(routed, 1)

                if extra:
                    pe.wait_ge(extra_landed, 16 * len(extra))
                for before, (e, stream, i) in steps(nc.tensor):
                    pe.wait_ge(h_ready, e * 2 + (i + 1))
                    wait(pe, out_lo, (e * 2 + (i - 1)) * copies)
                    wait(pe, out_hi, (e * 2 + (i - 1)) * copies)
                    for k in range(KC):
                        last = nc.tensor.transpose(turned[2 * i + k // 4][:, k % 4, :], h[i][:, k * P:(k + 1) * P],
                                                   core.ident[:])
                        if k == 3:
                            last.then_inc(turned_lo, 1)
                    last.then_inc(turned_hi, 1)
                    if router and before:
                        route(*before)
                if router:
                    route(*LAST)



def choice_stage(core, name, block, logits, streams, beside=None):
    nc = core.nc
    tiles = T_LAT + (T_CTX if streams == 2 else 0)
    rounds = SLOTS_LAT // 8
    with ExitStack() as st:
        def sb(n, shape, dt=F32):
            return st.enter_context(nc.sbuf_tensor(f"{name}_{n}", shape, dt))

        top, total, inv = sb("top", [P, tiles]), sb("total", [P, tiles]), sb("inv", [P, tiles])
        aff = sb("aff", [P, tiles, EXPERTS])
        wide = sb("wide", [P, T_LAT, 48])
        pool_of = [sb(f"left{i}", [48, N_LAT]) for i in range(2)]
        best, where, where_f = sb("best", [48, SLOTS_LAT]), sb("where", [48, SLOTS_LAT], U32), sb("where_f", [48, SLOTS_LAT])
        turned = [st.enter_context(nc.psum_tensor(f"{name}_turned{i}", [P, 4, P], F32)) for i in range(2)]
        out = [st.enter_context(nc.psum_tensor(f"{name}_out{i}", [P, BANK], F32)) for i in range(2)]
        step, exps, turned_s, chosen, back = (core.sem(f"{name}_{n}") for n in (
            "step", "exps", "turned_s", "chosen", "back"))
        placed = core.placed
        with core.block() as blk:
            @blk.vector
            def _(dve):
                done = [0]

                def chain(ins):
                    ins.then_inc(step, 1)
                    done[0] += 1
                    dve.wait_ge(step, done[0])

                seen = logits[:, 0:tiles * EXPERTS].rearrange("p (t e) -> p t e", e=EXPERTS)
                nc.vector.memset(wide[:], -1.0)
                chain(nc.vector.tensor_reduce(top[:], seen, AX, ALU.max))
                chain(nc.vector.tensor_tensor(aff[:], seen, top[:].unsqueeze(2).to_broadcast([P, tiles, EXPERTS]),
                                              ALU.subtract))
                dve.wait_ge(exps, 1)
                chain(nc.vector.tensor_reduce(total[:], aff[:], AX, ALU.add))
                chain(nc.vector.reciprocal(inv[:], total[:]))
                ends = [(0, T_LAT, 0)] + ([(T_LAT, tiles, 32)] if streams == 2 else [])
                for a, b, col in ends:
                    chain(nc.vector.tensor_tensor(wide[:, 0:b - a, col:col + EXPERTS], aff[:, a:b, :],
                                                  inv[:, a:b].unsqueeze(2).to_broadcast([P, b - a, EXPERTS]), ALU.mult))
                for n in range(2):
                    dve.wait_ge(turned_s, n + 1)
                    chain(nc.vector.tensor_copy(pool_of[0][:, BANK * n:BANK * n + BANK],
                                                turned[n][0:48].rearrange("p k m -> p (k m)")))
                for r in range(rounds):
                    left, rest = pool_of[r % 2], pool_of[1 - r % 2]
                    eight = best[:, 8 * r:8 * r + 8]
                    chain(nc.vector.max(eight, left[:]))
                    nc.vector.max_index(where[:, 8 * r:8 * r + 8], eight, left[:]).then_inc(chosen, 1)
                    if r < rounds - 1:
                        chain(nc.vector.match_replace(rest[:], eight, left[:], -1.0))
                dve.wait_ge(chosen, rounds)
                nc.vector.tensor_copy(where_f[:], where[:]).then_inc(chosen, 1)
                dve.wait_ge(back, 1)
                nc.vector.tensor_copy(core.gate_t[:], out[0][:, 0:48]).then_inc(placed, 1)
                dve.wait_ge(back, 2)
                nc.vector.tensor_copy(core.index_t[:], out[1][:, 0:48]).then_inc(placed, 1)
                if beside:
                    beside.finish(dve)

            @blk.scalar
            def _(act):
                act.wait_ge(step, 2)
                nc.scalar.activation(aff[:], aff[:], ACT.Exp).then_inc(exps, 1)
                if beside:
                    beside.copy_out(act)

            @blk.tensor
            def _(pe):
                pe.wait_ge(step, 4 + streams)
                for t in range(T_LAT):
                    last = nc.tensor.transpose(turned[t // 4][0:48, t % 4, :], wide[:, t, :], core.ident[:])
                    if t % 4 == 3:
                        last.then_inc(turned_s, 1)
                if beside:
                    beside.products(pe)
                pe.wait_ge(chosen, rounds + 1)
                nc.tensor.transpose(out[0][:, 0:48], best[:], core.ident[0:48, 0:48]).then_inc(back, 1)
                nc.tensor.transpose(out[1][:, 0:48], where_f[:], core.ident[0:48, 0:48]).then_inc(back, 1)

            @blk.sync
            def _(sp):
                if beside:
                    beside.load(sp)
                for s in range(RING):
                    load_expert_chunk(core, sp, block, core.chunks, s)



def experts_stage(core, name, block, streams, g2_rows, x_lat, x_ctx):
    nc, io = core.nc, core.io
    slots = SLOTS_LAT + (SLOTS_CTX if streams == 2 else 0)
    first = core.chunks
    core.chunks += EXPERTS * EXP_CHUNKS
    PLACES, LEAD = 6, 4
    h_cols = SLOTS_LAT + (2 * SLOTS_CTX if streams == 2 else 0) + SLOTS_LAT
    with ExitStack() as st:
        def sb(n, shape, dt=F32):
            return st.enter_context(nc.sbuf_tensor(f"{name}_{n}", shape, dt))

        def psum(n, banks=1):
            return st.enter_context(nc.psum_tensor(f"{name}_{n}", [P, banks * BANK], F32))

        w_hi = [sb(f"w_hi{i}", [P, CHUNK], F32R) for i in range(PLACES)]
        w_lo = [sb(f"w_lo{i}", [P, CHUNK], F32R) for i in range(PLACES)]
        xg, xg_ctx = sb("xg", [P, D]), sb("xg_ctx", [SLOTS_CTX, D])
        x = sb("x", [P, KC, 2, slots], F32R)
        part = [sb(f"part{i}", [P, 2, slots]) for i in range(2)]
        gate_up_s = [sb(f"gate_up{i}", [P, 2, slots]) for i in range(2)]
        silu_g = [sb(f"silu_g{i}", [P, slots]) for i in range(2)]
        prod = [sb(f"prod{i}", [P, slots]) for i in range(2)]
        h = sb("h", [P, KC, h_cols], F32R)
        y, y_ctx, ctx_part = sb("y", [P, D]), sb("y_ctx", [SLOTS_CTX, D]), sb("ctx_part", [SLOTS_CTX, D])
        gu = [psum(f"gu{i}", 2) for i in range(2)]
        y_sum = [psum(f"y_sum{i}") for i in range(2)]
        y_ctx_sum = psum("y_ctx_sum", 2) if streams == 2 else None
        (hi_done, gathered, gathered_ctx, turned_s, x_hi_done, x_ready, gu_ready, part_done, sum_done, silu_done,
         prod_done, h_hi_done, h_ready, down_done, ctx_part_done, ctx_added, y_ready, scattered, scattered_ctx) = (
            core.sem(f"{name}_{n}") for n in (
                "hi_done", "gathered", "gathered_ctx", "turned", "x_hi_done", "x_ready", "gu_ready", "part_done",
                "sum_done", "silu_done", "prod_done", "h_hi_done", "h_ready", "down_done", "ctx_part_done", "ctx_added",
                "y_ready", "scattered", "scattered_ctx"))
        turns = 2 + (streams == 2)

        def experts(engine):
            yield 0, False
            with engine.Fori(1, EXPERTS - 1) as e:
                yield e, False
            yield EXPERTS - 1, True

        def place_free(eng, s, e):
            if s < PLACES:
                before = s + EXP_CHUNKS - PLACES
                if before < 8:
                    wait(eng, gu_ready, e * KC)
                else:
                    wait(eng, down_done, e * 4 + (before - 8 + 1 - 4))
            else:
                eng.wait_ge(gu_ready, e * KC + (2 * ((s - PLACES) // 2) + 2))

        def turn_views(g):
            if g < 2:
                return (gu[0][:, BANK * g:BANK * (g + 1)].rearrange("p (k m) -> p k m", k=4),
                        (slice(4 * g, 4 * g + 4), slice(0, SLOTS_LAT)))
            return (gu[1][:, 0:KC * SLOTS_CTX].rearrange("p (k m) -> p k m", k=KC),
                    (slice(0, KC), slice(SLOTS_LAT, slots)))

        def gu_view(j, n):
            return gu[j % 2][:].rearrange("p (w m) -> p w m", w=2)[:, :, slots * n:slots * (n + 1)]

        with core.block() as blk:
            @blk.sync
            def _(sp):
                for s in range(RING, EXP_CHUNKS):
                    load_expert_chunk(core, sp, block, first, s)
                with nc.sync.Fori(1, EXPERTS) as e:
                    for s in range(EXP_CHUNKS):
                        load_expert_chunk(core, sp, block, first, s, e)

            @blk.gpsimd
            def _(pool):
                rows_of = ((xg, y, core.h_lat, x_lat, gathered, scattered, SLOTS_LAT, 0),
                           (xg_ctx, y_ctx, core.h_ctx, x_ctx, gathered_ctx, scattered_ctx, SLOTS_CTX, 32))[:streams]
                for e in range(-1, EXPERTS):
                    if e + 1 < EXPERTS:
                        wait(pool, turned_s, (e + 1) * turns)
                        for got, _, rows, _, landed_s, _, n, col in rows_of:
                            index = core.index_t[0:n, e + 1 + col:e + 2 + col]
                            nc.gpsimd.indirect_dma_start(got[:], None, rows, bass.IndirectOffsetOnAxis(ap=index, axis=0))\
                              .then_inc(landed_s, 16)
                    if e >= 0:
                        pool.wait_ge(y_ready, (e + 1) * 2 * streams)
                        for _, add, _, to, _, added_s, n, col in rows_of:
                            wait(pool, added_s, e * 16)
                            index = core.index_t[0:n, e + col:e + 1 + col]
                            nc.gpsimd.indirect_dma_start(to, bass.IndirectOffsetOnAxis(ap=index, axis=0), add[:], None,
                                                         compute_op=ALU.add).then_inc(added_s, 16)
                for _, _, _, _, _, added_s, _, _ in rows_of:
                    pool.wait_ge(added_s, 16 * EXPERTS)

            @blk.tensor
            def _(pe):
                def turn(e):
                    pe.wait_ge(gathered, e * 16 + 16)
                    wait(pe, sum_done, e * KC)
                    for g in range(2):
                        if g == 1 and streams == 2:
                            pe.wait_ge(gathered_ctx, e * 16 + 16)
                        for k in range(4):
                            last = nc.tensor.transpose(gu[0][:, BANK * g + k * P:BANK * g + (k + 1) * P],
                                                       xg[:, (4 * g + k) * P:(4 * g + k + 1) * P], core.ident[:])
                        last.then_inc(turned_s, 1)
                    if streams == 2:
                        for k in range(KC):
                            last = nc.tensor.transpose(gu[1][:, k * SLOTS_CTX:(k + 1) * SLOTS_CTX],
                                                       xg_ctx[:, k * P:(k + 1) * P], core.ident[0:SLOTS_CTX, 0:SLOTS_CTX])
                        last.then_inc(turned_s, 1)

                def gate_up(e):
                    pe.wait_ge(x_ready, e * turns + turns)
                    for j in range(KC):
                        if j % 2 == 0:
                            chunk_done(core, pe, first + j + 1, e, EXP_CHUNKS)
                        wait(pe, sum_done, e * KC + (j - 1))
                        for which in range(2):
                            at = (j // 2 * 2 + which) % PLACES
                            out = gu[j % 2][:, BANK * which:BANK * which + 2 * slots]
                            for k in range(KC):
                                col = 256 * k + P * (j % 2)
                                passes = ((w_hi, 2), (w_lo, 1)) if k < KC - 1 else ((w_lo, 1), (w_hi, 2))
                                for n, (w, cols) in enumerate(passes):
                                    last = nc.tensor.matmul(out[:, 0:cols * slots], w[at][:, col:col + P],
                                                            x[:, k, 0:cols, :], start=k == 0 and n == 0,
                                                            stop=k == KC - 1 and n == 1)
                        last.then_inc(gu_ready, 1)

                def down(e, r):
                    chunk_done(core, pe, first + 8 + r, e, EXP_CHUNKS)
                    pe.wait_ge(h_ready, e * KC + (2 * r + 2))
                    w = (8 + r) % PLACES
                    for kk in range(2):
                        k = 2 * r + kk
                        lat_hi, lat_lo = h[:, k, 0:SLOTS_LAT], h[:, k, h_cols - SLOTS_LAT:h_cols]
                        ctx_hi = h[:, k, SLOTS_LAT:SLOTS_LAT + SLOTS_CTX]
                        ctx_both = h[:, k, SLOTS_LAT:SLOTS_LAT + 2 * SLOTS_CTX]
                        for c in range(2):
                            cols = slice(D * kk + BANK * c, D * kk + BANK * (c + 1))
                            hi, lo = w_hi[w][:, cols], w_lo[w][:, cols]
                            for n, (a, b) in enumerate(((lat_hi, hi), (lat_hi, lo), (lat_lo, hi))):
                                last = nc.tensor.matmul(y_sum[c][:], a, b, start=k == 0 and n == 0,
                                                        stop=k == KC - 1 and n == 2)
                            if streams == 2:
                                passes = ((ctx_both, hi, 2), (ctx_hi, lo, 1))
                                if k == KC - 1:
                                    passes = passes[::-1]
                                for n, (a, b, rows) in enumerate(passes):
                                    last = nc.tensor.matmul(y_ctx_sum[0:rows * SLOTS_CTX, BANK * c:BANK * (c + 1)], a, b,
                                                            start=k == 0 and n == 0, stop=k == KC - 1 and n == 1)
                    last.then_inc(down_done, 1)

                turn(0)
                for e, is_last in experts(nc.tensor):
                    gate_up(e)
                    wait(pe, y_ready, e * (2 * streams))
                    down(e, 0)
                    down(e, 1)
                    if not is_last:
                        turn(e + 1)
                    down(e, 2)
                    down(e, 3)

            @blk.scalar
            def _(act):
                def weights_hi(s, e):
                    landed(core, act, first + s, e, EXP_CHUNKS)
                    place_free(act, s, e)
                    nc.scalar.activation(w_hi[s % PLACES][:], core.raw[(first + s) % RING][:], ACT.Copy).then_inc(hi_done, 1)

                def tokens_hi(e):
                    for g in range(turns):
                        bank, (ks, cols) = turn_views(g)
                        act.wait_ge(turned_s, e * turns + (g + 1))
                        nc.scalar.activation(x[:, ks, 0, cols], bank, ACT.Copy).then_inc(x_hi_done, 1)

                def context_part(e):
                    act.wait_ge(down_done, e * 4 + 4)
                    wait(act, y_ready, e * (2 * streams))
                    nc.scalar.activation(ctx_part[:], y_ctx_sum[SLOTS_CTX:2 * SLOTS_CTX, :], ACT.Copy)\
                      .then_inc(ctx_part_done, 1)

                tokens_hi(0)
                for s in range(LEAD):
                    weights_hi(s, 0)
                for e, is_last in experts(nc.scalar):
                    for t in range(EXP_CHUNKS):
                        j = t - 1
                        if t == 0 and streams == 2 and (not isinstance(e, int) or e > 0):
                            context_part(e - 1)
                        if 0 <= j < KC:
                            act.wait_ge(gu_ready, e * KC + (j + 1))
                            wait(act, sum_done, e * KC + (j - 1))
                            nc.scalar.activation(part[j % 2][:], gu_view(j, 1), ACT.Copy).then_inc(part_done, 1)
                        if t + LEAD < EXP_CHUNKS:
                            weights_hi(t + LEAD, e)
                        elif not is_last:
                            weights_hi(t + LEAD - EXP_CHUNKS, e + 1)
                        if 0 <= j < KC:
                            act.wait_ge(sum_done, e * KC + (j + 1))
                            wait(act, prod_done, e * KC + (j - 1))
                            nc.scalar.activation(silu_g[j % 2][:], gate_up_s[j % 2][:, 0, :], ACT.Silu).then_inc(silu_done, 1)
                        if t == 9 and not is_last:
                            tokens_hi(e + 1)
                if streams == 2:
                    context_part(EXPERTS - 1)

            @blk.vector
            def _(dve):
                def weights_lo(s, e):
                    dve.wait_ge(hi_done, e * EXP_CHUNKS + (s + 1))
                    nc.vector.tensor_tensor(w_lo[s % PLACES][:], core.raw[(first + s) % RING][:],
                                            w_hi[s % PLACES][:].bitcast(F32), ALU.subtract).then_inc(core.chunk_done, 1)

                def tokens_lo(e):
                    for g in range(turns):
                        bank, (ks, cols) = turn_views(g)
                        dve.wait_ge(x_hi_done, e * turns + (g + 1))
                        nc.vector.tensor_tensor(x[:, ks, 1, cols], bank, x[:, ks, 0, cols].bitcast(F32), ALU.subtract)\
                          .then_inc(x_ready, 1)

                def product(j, e):
                    dve.wait_ge(silu_done, e * KC + (j + 1))
                    wait(dve, h_ready, e * KC + (j - 1))
                    nc.vector.tensor_tensor(prod[j % 2][:], gate_up_s[j % 2][:, 1, :], silu_g[j % 2][:], ALU.mult)\
                      .then_inc(prod_done, 1)
                    dve.wait_ge(prod_done, e * KC + (j + 1))
                    nc.vector.tensor_copy(h[:, j, 0:slots], prod[j % 2][:]).then_inc(h_hi_done, 1)
                    dve.wait_ge(h_hi_done, e * KC + (j + 1))
                    if streams == 2:
                        nc.vector.tensor_tensor(h[:, j, slots:slots + SLOTS_CTX], prod[j % 2][:, SLOTS_LAT:],
                                                h[:, j, SLOTS_LAT:slots].bitcast(F32), ALU.subtract)
                    nc.vector.tensor_tensor(h[:, j, h_cols - SLOTS_LAT:], prod[j % 2][:, 0:SLOTS_LAT],
                                            h[:, j, 0:SLOTS_LAT].bitcast(F32), ALU.subtract).then_inc(h_ready, 1)

                def results(e):
                    dve.wait_ge(down_done, e * 4 + 4)
                    wait(dve, scattered, e * 16)
                    for c in range(2):
                        cols = slice(BANK * c, BANK * (c + 1))
                        nc.vector.scalar_tensor_tensor(y[:, cols], y_sum[c][:], core.gate_t[:, ds(e, 1)], g2_rows[:, 0, cols],
                                                       ALU.mult, ALU.mult).then_inc(y_ready, 1)
                    if streams == 2:
                        dve.wait_ge(ctx_part_done, e + 1)
                        wait(dve, scattered_ctx, e * 16)
                        for c in range(2):
                            cols = slice(BANK * c, BANK * (c + 1))
                            nc.vector.tensor_tensor(y_ctx[:, cols], y_ctx_sum[0:SLOTS_CTX, cols], ctx_part[:, cols], ALU.add)\
                              .then_inc(ctx_added, 1)
                            dve.wait_ge(ctx_added, e * 2 + (c + 1))
                            nc.vector.scalar_tensor_tensor(y_ctx[:, cols], y_ctx[:, cols],
                                                           core.gate_t[0:SLOTS_CTX, ds(e + 32, 1)],
                                                           g2_rows[0:SLOTS_CTX, 1, cols], ALU.mult, ALU.mult)\
                              .then_inc(y_ready, 1)

                tokens_lo(0)
                for s in range(LEAD):
                    weights_lo(s, 0)
                for e, is_last in experts(nc.vector):
                    for t in range(EXP_CHUNKS):
                        j = t - 1
                        if t == 0 and (not isinstance(e, int) or e > 0):
                            results(e - 1)
                        if 0 <= j < KC:
                            dve.wait_ge(part_done, e * KC + (j + 1))
                            nc.vector.tensor_tensor(gate_up_s[j % 2][:], gu_view(j, 0), part[j % 2][:], ALU.add)\
                              .then_inc(sum_done, 1)
                        if t + LEAD < EXP_CHUNKS:
                            weights_lo(t + LEAD, e)
                        elif not is_last:
                            weights_lo(t + LEAD - EXP_CHUNKS, e + 1)
                        if 0 <= j < KC:
                            product(j, e)
                        if t == 9 and not is_last:
                            tokens_lo(e + 1)
                results(EXPERTS - 1)



def padded_place(ht):
    def into(k, t, stream):
        at = t * P + (OFF_CTX - N_LAT if stream else OFF_LAT)
        return ht[:, k:k + 4, ds(at, P)]
    return into


def pool_stage(core, ht, x, gain_rows):
    nc, io = core.nc, core.io
    tiles = T_LAT + T_CTX
    with ExitStack() as st:
        def sb(n, shape, dt=F32):
            return st.enter_context(nc.sbuf_tensor(f"pool_{n}", shape, dt))

        mod = Modulation(core, 1, st, 0, MOD_BESIDE_POOL)
        sums = [sb(f"sums{i}", [P, 2, PADDED]) for i in range(2)]
        weights = sb("weights", [P, 2 * len(WINDOWS), 2 * P])
        edge = sb("edge", [P, len(WINDOWS), 2, PAD])
        edge_mean = sb("edge_mean", [P, 2, 4, PAD])
        change = [sb(f"change{i}", [P, D]) for i in range(2)]
        out = [[st.enter_context(nc.psum_tensor(f"pool_out{i}{n}", [P, BANK], F32)) for n in range(2)] for i in range(2)]
        loaded, step, pooled, product, scaled, added = (
            core.sem(f"pool_{n}") for n in ("loaded", "step", "pooled", "product", "scaled", "added"))
        with core.block() as blk:
            @blk.sync
            def _(sp):
                sp.dma_start(weights[:], io["pool_w"][0].rearrange("g (k p) d -> p (g k) d", p=P)).then_inc(loaded, 16)
                sp.dma_start(edge[:], io["edge"].partition_broadcast(P).rearrange("p (g s c) -> p g s c", g=len(WINDOWS), s=2))\
                  .then_inc(loaded, 16)
                mod.load(sp)

            @blk.scalar
            def _(act):
                mod.copy_out(act)

            @blk.vector
            def _(dve):
                done = [0]

                def chain(ins):
                    ins.then_inc(step, 1)
                    done[0] += 1
                    dve.wait_ge(step, done[0])

                dve.wait_ge(loaded, 32)
                for g, w in enumerate(WINDOWS):
                    h = ht[:, 2 * g:2 * g + 2, :]
                    src, reach = h, 0
                    for level in range(g + 1):
                        dst = sums[level % 2]
                        if level == 0:
                            chain(nc.vector.tensor_tensor(dst[:, :, 1:PADDED], h[:, :, 1:PADDED], h[:, :, 0:PADDED - 1], ALU.add))
                        else:
                            n = 1 << (level - 1)
                            lo = 2 * n
                            chain(nc.vector.tensor_tensor(dst[:, :, lo:PADDED - lo + 1], src[:, :, lo - n:PADDED - lo + 1 - n],
                                                          src[:, :, lo + n:PADDED - lo + 1 + n], ALU.add))
                        src = dst
                    ends = [OFF_LAT, OFF_LAT + N_LAT - PAD, OFF_CTX, OFF_CTX + N_CTX - PAD]
                    for i, at in enumerate(ends):
                        inv = edge[:, g, i % 2, :].unsqueeze(1).to_broadcast([P, 2, PAD])
                        chain(nc.vector.tensor_tensor(edge_mean[:, :, i, :], src[:, :, at:at + PAD], inv, ALU.mult))
                        chain(nc.vector.tensor_tensor(edge_mean[:, :, i, :], edge_mean[:, :, i, :], h[:, :, at:at + PAD],
                                                      ALU.subtract))
                    for at, n in ((OFF_LAT, N_LAT), (OFF_CTX, N_CTX)):
                        chain(nc.vector.scalar_tensor_tensor(h[:, :, at:at + n], src[:, :, at:at + n], 1.0 / w,
                                                             h[:, :, at:at + n], ALU.mult, ALU.subtract))
                    for i, at in enumerate(ends):
                        last = nc.vector.tensor_copy(h[:, :, at:at + PAD], edge_mean[:, :, i, :])
                        chain(last) if i < 3 else last.then_inc(pooled, 1)
                for t in range(tiles):
                    gain = gain_rows[:, 1 if t >= T_LAT else 0, :]
                    dve.wait_ge(product, t + 1)
                    wait(dve, added, t - 1)
                    for n in range(2):
                        nc.vector.tensor_tensor(change[t % 2][:, BANK * n:BANK * n + BANK], out[t % 2][n][:],
                                                gain[:, BANK * n:BANK * n + BANK], ALU.mult).then_inc(scaled, 1)
                    dve.wait_ge(scaled, 2 * t + 2)
                    nc.vector.tensor_tensor(x[:, t, :], x[:, t, :], change[t % 2][:], ALU.add).then_inc(added, 1)
                mod.finish(dve)

            @blk.tensor
            def _(pe):
                mod.products(pe)
                pe.wait_ge(pooled, len(WINDOWS))
                for t in range(tiles):
                    wait(pe, scaled, 2 * (t - 1))
                    at = t * P + (OFF_CTX - N_LAT if t >= T_LAT else OFF_LAT)
                    for g in range(len(WINDOWS)):
                        for k in range(2):
                            last = nc.tensor.matmul(out[t % 2][g // 2][:, 256 * (g % 2):256 * (g % 2) + 256],
                                                    ht[:, 2 * g + k, at:at + P], weights[:, 2 * g + k, :],
                                                    start=k == 0, stop=k == 1)
                    last.then_inc(product, 1)



def lru_stage(core, t_hi, t_lo, decay):
    nc, io = core.nc, core.io
    first = core.chunks
    core.chunks += KC
    half = KC * P
    unroll = RING
    segments = ((0, BANK), (BANK, BANK), (N_LAT, N_CTX))
    with ExitStack() as st:
        def sb(n, shape, dt=F32):
            return st.enter_context(nc.sbuf_tensor(f"lru_{n}", shape, dt))

        w_hi = [sb(f"w_hi{i}", [P, CHUNK], F32R) for i in range(2)]
        w_lo = sb("w_lo", [P, CHUNK], F32R)
        gw = [sb(f"gw{i}", [P, 4, P]) for i in range(2)]
        gw_hi, gw_lo = sb("gw_hi", [P, 4, P], F32R), sb("gw_lo", [P, 4, P], F32R)
        params = [sb(f"par{i}", [P, LRU_COLS + 6]) for i in range(2)]
        x, x_hi, x_lo = sb("x", [P, TOK]), sb("x_hi", [P, TOK], F32R), sb("x_lo", [P, TOK], F32R)
        r = [sb(f"r{i}", [P, TOK]) for i in range(2)]
        gi = [sb(f"i{i}", [P, TOK]) for i in range(2)]
        a = [sb(f"a{i}", [P, TOK]) for i in range(2)]
        q = [sb(f"q{i}", [P, TOK]) for i in range(2)]
        y = sb("y", [P, N_LAT])
        x_sum = st.enter_context(nc.psum_tensor("lru_x_sum", [P, 3 * BANK], F32))
        y_sum = st.enter_context(nc.psum_tensor("lru_y_sum", [P, 2 * BANK], F32))
        g_sum = [st.enter_context(nc.psum_tensor(f"lru_g_sum{i}", [P, BANK], F32)) for i in range(3)]
        (gw_landed0, gw_landed1, hi_done, gw_hi_done, gw_done, par_set, x_ready, y_ready, first_tap, conv, x_hi_done,
         x_split, y_done, gates, g_done, powers, roots, step, summed, stored, o_ready) = (core.sem(f"lru_{n}") for n in (
             "gw_landed0", "gw_landed1", "hi_done", "gw_hi_done", "gw_done", "par_set", "x_ready", "y_ready",
             "first_tap", "conv", "x_hi_done", "x_split", "y_done", "gates", "g_done", "powers", "roots", "step", "summed", "stored",
             "o_ready"))
        gw_landed = (gw_landed0, gw_landed1)
        CONV = 6
        STEPS = 10

        def blocks(engine):
            for i in range(unroll):
                yield 0, i
            with engine.Fori(1, KC // unroll) as e:
                for i in range(unroll):
                    yield e, i

        def before(e, i):
            return (e, i - 1) if i else (e - 1, unroll - 1)

        def has_before(e, i):
            return not isinstance(e, int) or e * unroll + i > 0

        w_in = io["lru_w_in"][0].rearrange("(k p) (s b m) -> p s k b m", p=P, s=2, m=P)
        wa = io["lru_wa"][0].rearrange("d b i o -> i d b o")
        wx = io["lru_wx"][0].rearrange("d b i o -> i d b o")

        with core.block() as blk:
            @blk.sync
            def _(sp):
                for e, i in blocks(nc.sync):
                    b = e * unroll + i
                    sp.wait_ge(core.chunk_done, e * unroll + (first + i + 1))
                    sp.dma_start(core.raw[i][:].rearrange("p (s k b m) -> p s k b m", s=2, k=KC, b=1),
                                 w_in[:, :, :, ds(b, 1), :]).then_inc(core.raw_landed[i], 16)
                    wait(sp, gw_done, e * unroll + (i - 1))
                    for s, w in enumerate((wa, wx)):
                        sp.dma_start(gw[i % 2][:, 2 * s:2 * s + 2, :].unsqueeze(2), w[:, :, ds(b, 1), :])\
                          .then_inc(gw_landed[i % 2], 16)

            @blk.gpsimd
            def _(pool):
                lat = slice(0, N_LAT)
                with nc.gpsimd.Fori(0, KC) as b:
                    pool.wait_ge(step, b * STEPS + STEPS)
                    nc.gpsimd.tensor_tensor(r[0][:, lat], r[0][:, lat], r[1][:, lat], ALU.add).then_inc(summed, 1)
                    pool.wait_ge(summed, b + 1)
                    pool.wait_ge(y_done, b + 1)
                    nc.gpsimd.tensor_tensor(r[1][:, lat], r[0][:, lat], y[:], ALU.mult).then_inc(o_ready, 1)
                    pool.wait_ge(o_ready, b + 1)
                    pool.dma_start(core.o_lru.rearrange("(b p) t -> p b t", p=P)[:, ds(b, 1), :],
                                   r[1][:, 0:N_LAT].unsqueeze(1)).then_inc(stored, 16)
                pool.wait_ge(stored, 16 * KC)

            @blk.tensor
            def _(pe):
                for e, i in blocks(nc.tensor):
                    b = e * unroll + i
                    w = (w_hi[i % 2], w_lo)
                    chunk_done(core, pe, first + i, e, unroll)
                    wait(pe, conv, b * CONV)
                    for n, (at, size) in enumerate(segments):
                        for k in range(KC):
                            for m, (part, t) in enumerate(((0, t_hi), (0, t_lo), (1, t_hi))):
                                last = nc.tensor.matmul(x_sum[:, BANK * n:BANK * n + size],
                                                        w[part][:, half + P * k:half + P * k + P],
                                                        t[:, k, at:at + size], start=k == 0 and m == 0,
                                                        stop=k == KC - 1 and m == 2)
                    last.then_inc(x_ready, 1)
                    wait(pe, y_done, b)
                    for n in range(2):
                        for k in range(KC):
                            for m, (part, t) in enumerate(((0, t_hi), (0, t_lo), (1, t_hi))):
                                last = nc.tensor.matmul(y_sum[:, BANK * n:BANK * n + BANK], w[part][:, P * k:P * k + P],
                                                        t[:, k, BANK * n:BANK * n + BANK], start=k == 0 and m == 0,
                                                        stop=k == KC - 1 and m == 2)
                    last.then_inc(y_ready, 1)
                    pe.wait_ge(gw_done, b + 1)
                    pe.wait_ge(x_split, b + 1)
                    for g in range(4):
                        for n, (at, size) in enumerate(segments):
                            wait(pe, g_done, b * 12 + (3 * g + n - 2))
                            for m, (gate_w, t) in enumerate(((gw_hi, x_hi), (gw_hi, x_lo), (gw_lo, x_hi))):
                                last = nc.tensor.matmul(g_sum[n][:, 0:size], gate_w[:, g, :], t[:, at:at + size],
                                                        start=m == 0, stop=m == 2)
                            last.then_inc(gates, 1)

            @blk.scalar
            def _(act):
                def weights_hi(e, i):
                    landed(core, act, first + i, e, unroll)
                    wait(act, y_ready, e * unroll + (i - 1))
                    nc.scalar.activation(w_hi[i % 2][:], core.raw[i][:], ACT.Copy).then_inc(hi_done, 1)

                def gate_weights_hi(e, i):
                    act.wait_ge(gw_landed[i % 2], e * 64 + (32 * (i // 2) + 32))
                    wait(act, gates, (e * unroll + i) * 12)
                    nc.scalar.activation(gw_hi[:], gw[i % 2][:], ACT.Copy).then_inc(gw_hi_done, 1)

                def gelu_and_gates(e, i, following=None):
                    b = e * unroll + i
                    par = params[i % 2]
                    act.wait_ge(y_ready, b + 1)
                    wait(act, o_ready, b)
                    nc.scalar.activation(y[:], y_sum[:], ACT.Gelu_apprx_tanh).then_inc(y_done, 1)
                    act.wait_ge(par_set, b * 2 + 2)
                    for g in range(4):
                        out = (r[0], r[1], gi[0], gi[1])[g]
                        if g == 1:
                            wait(act, stored, b * 16)
                        for n, (at, size) in enumerate(segments):
                            act.wait_ge(gates, b * 12 + (3 * g + n + 1))
                            nc.scalar.activation(out[:, at:at + size], g_sum[n][:, 0:size], ACT.Sigmoid,
                                                 bias=par[:, 5 + g:6 + g]).then_inc(g_done, 1)
                    act.wait_ge(g_done, b * 12 + 6)
                    for d, m, out in ((0, 0, a), (0, 1, q), (0, 2, r), (1, 0, a), (1, 1, q), (1, 2, r)):
                        if m == 2:
                            act.wait_ge(powers, b * 6 + (3 * d + 2))
                        nc.scalar.activation(out[d][:], r[d][:], ACT.Tanh if m == 2 else ACT.Exp,
                                             scale=par[:, LRU_COLS + 3 * d + m:LRU_COLS + 3 * d + m + 1]).then_inc(powers, 1)
                    if following is not None:
                        gate_weights_hi(*following)
                    for d in range(2):
                        act.wait_ge(step, b * STEPS + (3 + d))
                        nc.scalar.activation(q[d][:], q[d][:], ACT.Sqrt).then_inc(roots, 1)

                for e, i in blocks(nc.scalar):
                    weights_hi(e, i)
                    if has_before(e, i):
                        gelu_and_gates(*before(e, i), following=(e, i))
                    else:
                        gate_weights_hi(e, i)
                    b = e * unroll + i
                    act.wait_ge(x_ready, b + 1)
                    act.wait_ge(par_set, b * 2 + 2)
                    par = params[i % 2]
                    nc.scalar.activation(x[:], x_sum[:, 0:TOK], ACT.Identity, scale=par[:, 2:3], bias=par[:, 4:5])\
                      .then_inc(first_tap, 1)
                    act.wait_ge(conv, b * CONV + CONV)
                    nc.scalar.activation(x_hi[:], x[:], ACT.Copy).then_inc(x_hi_done, 1)
                gelu_and_gates(KC // unroll - 1, unroll - 1)

            @blk.vector
            def _(dve):
                def gate_weights_lo(e, i):
                    dve.wait_ge(gw_hi_done, e * unroll + (i + 1))
                    nc.vector.tensor_tensor(gw_lo[:], gw[i % 2][:], gw_hi[:].bitcast(F32), ALU.subtract).then_inc(gw_done, 1)

                def states(e, i, following=None):
                    b = e * unroll + i
                    for d in range(2):
                        dve.wait_ge(g_done, b * 12 + (9 + 3 * d))
                        nc.vector.tensor_tensor(gi[d][:], gi[d][:], x[:], ALU.mult).then_inc(step, 1)
                    for d in range(2):
                        dve.wait_ge(powers, b * 6 + (3 * d + 3))
                        nc.vector.scalar_tensor_tensor(q[d][:], q[d][:], 1.0, r[d][:], ALU.add, ALU.mult).then_inc(step, 1)
                    if following is not None:
                        gate_weights_lo(*following)
                    done = 4
                    for d in range(2):
                        dve.wait_ge(roots, b * 2 + (d + 1))
                        dve.wait_ge(step, b * STEPS + (d + 1))
                        nc.vector.tensor_tensor(gi[d][:], gi[d][:], q[d][:], ALU.mult).then_inc(step, 1)
                        done += 1
                        dve.wait_ge(step, b * STEPS + done)
                        turn = slice(None, None, -1) if d else slice(None)
                        c, l = slice(N_LAT, TOK), slice(0, N_LAT)
                        nc.vector.tensor_tensor_scan(r[d][:, c][:, turn], a[d][:, c][:, turn], gi[d][:, c][:, turn], 0.0,
                                                     ALU.mult, ALU.add).then_inc(step, 1)
                        done += 1
                        dve.wait_ge(step, b * STEPS + done)
                        end = N_LAT if d else TOK - 1
                        nc.vector.tensor_tensor_scan(r[d][:, l][:, turn], a[d][:, l][:, turn], gi[d][:, l][:, turn],
                                                     r[d][:, end:end + 1], ALU.mult, ALU.add).then_inc(step, 1)
                        done += 1
                    assert done == STEPS

                for e, i in blocks(nc.vector):
                    b = e * unroll + i
                    par = params[i % 2]
                    wait(dve, roots, e * (2 * unroll) + 2 * (i - 1))
                    nc.vector.tensor_copy(par[:, 0:LRU_COLS], core.vec[:, ds(b * LRU_COLS + V_LRU, LRU_COLS)]).then_inc(par_set, 1)
                    nc.vector.tensor_copy(par[:, LRU_COLS:LRU_COLS + 6], decay[:, ds(b * 6, 6)]).then_inc(par_set, 1)
                    dve.wait_ge(hi_done, b + 1)
                    wait(dve, y_ready, b)
                    nc.vector.tensor_tensor(w_lo[:], core.raw[i][:], w_hi[i % 2][:].bitcast(F32), ALU.subtract)\
                      .then_inc(core.chunk_done, 1)
                    if has_before(e, i):
                        states(*before(e, i), following=(e, i))
                    else:
                        gate_weights_lo(e, i)
                    dve.wait_ge(first_tap, b + 1)
                    seqs = ((0, N_LAT), (N_LAT, N_CTX))
                    for n, (tap, shift) in enumerate(((1, -1), (0, -2), (3, 1))):
                        for s, (at, size) in enumerate(seqs):
                            lo, hi = at + max(0, -shift), at + size - max(0, shift)
                            if n:
                                dve.wait_ge(conv, b * CONV + (2 * n + s - 1))
                            nc.vector.scalar_tensor_tensor(x[:, lo:hi], x_sum[:, lo + shift:hi + shift],
                                                           par[:, tap:tap + 1], x[:, lo:hi], ALU.mult, ALU.add)\
                              .then_inc(conv, 1)
                    dve.wait_ge(x_hi_done, b + 1)
                    nc.vector.tensor_tensor(x_lo[:], x[:], x_hi[:].bitcast(F32), ALU.subtract).then_inc(x_split, 1)
                states(KC // unroll - 1, unroll - 1)


def decay_stage(core, decay):
    nc = core.nc
    terms = 9
    lam = core.vec[:, V_LRU:V_LRU + LRU_COLS * KC].rearrange("p (b c) -> p b c", c=LRU_COLS)[:, :, LRU_COLS - 2:]
    with ExitStack() as st:
        neg, mag, e, s, s2, acc = (st.enter_context(nc.sbuf_tensor(f"decay_{n}", [P, KC, 2], F32))
                                   for n in ("neg", "mag", "e", "s", "s2", "acc"))
        step, exps = core.sem("decay_step"), core.sem("decay_exps")
        with core.block() as blk:
            @blk.vector
            def _(dve):
                done = [0]

                def chain(ins):
                    ins.then_inc(step, 1)
                    done[0] += 1
                    dve.wait_ge(step, done[0])

                chain(nc.vector.tensor_scalar(neg[:], lam, -1.0, None, ALU.mult))
                chain(nc.vector.tensor_tensor(mag[:], lam, neg[:], ALU.max))
                dve.wait_ge(exps, 1)
                chain(nc.vector.tensor_scalar(s2[:], e[:], 2.0, None, ALU.add))
                chain(nc.vector.reciprocal(s2[:], s2[:]))
                chain(nc.vector.tensor_tensor(s[:], e[:], s2[:], ALU.mult))
                chain(nc.vector.tensor_tensor(s2[:], s[:], s[:], ALU.mult))
                chain(nc.vector.memset(acc[:], 1.0 / (2 * terms + 1)))
                for n in reversed(range(terms)):
                    chain(nc.vector.tensor_tensor(acc[:], acc[:], s2[:], ALU.mult))
                    chain(nc.vector.tensor_scalar(acc[:], acc[:], 1.0 / (2 * n + 1), None, ALU.add))
                chain(nc.vector.tensor_tensor(acc[:], acc[:], s[:], ALU.mult))
                chain(nc.vector.tensor_scalar(neg[:], neg[:], 0.0, None, ALU.max))
                chain(nc.vector.scalar_tensor_tensor(acc[:], acc[:], 2.0, neg[:], ALU.mult, ALU.add))
                out = decay[:].rearrange("p (b d m) -> p b d m", d=2, m=3)
                for m, f in enumerate((-8.0, -16.0, 8.0)):
                    chain(nc.vector.tensor_scalar(out[:, :, :, m], acc[:], f, None, ALU.mult))

            @blk.scalar
            def _(act):
                act.wait_ge(step, 2)
                nc.scalar.activation(e[:], mag[:], ACT.Exp, scale=-1.0).then_inc(exps, 1)


def out_stage(core, x, gain_row, load):
    nc, io = core.nc, core.io
    first = core.chunks
    core.chunks += KC
    with ExitStack() as st:
        hi = [st.enter_context(nc.sbuf_tensor(f"out_hi{i}", [P, KC, D], F32R)) for i in range(2)]
        lo = [st.enter_context(nc.sbuf_tensor(f"out_lo{i}", [P, KC, D], F32R)) for i in range(2)]
        change = st.enter_context(nc.sbuf_tensor("out_change", [P, D], F32))
        sums = [[st.enter_context(nc.psum_tensor(f"out_sums{i}{n}", [P, BANK], F32)) for n in range(2)] for i in range(2)]
        x_landed, hi_done, product, scaled, added = (core.sem(f"out_{n}") for n in (
            "x_landed", "hi_done", "product", "scaled", "added"))
        with core.block() as blk:
            @blk.sync
            def _(sp):
                for c in range(KC):
                    src = (io["lru_w_out"][0] if c % 2 else core.o_lru).rearrange("(k p) d -> p k d", p=P)
                    load_chunk(core, sp, first + c, src[:, c // 2 * 2:c // 2 * 2 + 2, :],
                               lambda place: place[:].rearrange("p (k d) -> p k d", k=2))
                for dst, src in load:
                    sp.dma_start(dst, src).then_inc(x_landed, 16)

            @blk.scalar
            def _(act):
                for c in range(KC):
                    landed(core, act, first + c)
                    nc.scalar.activation(hi[c % 2][:, c // 2 * 2:c // 2 * 2 + 2, :],
                                         core.raw[(first + c) % RING][:].rearrange("p (k d) -> p k d", k=2), ACT.Copy)\
                      .then_inc(hi_done, 1)

            @blk.vector
            def _(dve):
                for c in range(KC):
                    dve.wait_ge(hi_done, c + 1)
                    ks = slice(c // 2 * 2, c // 2 * 2 + 2)
                    nc.vector.tensor_tensor(lo[c % 2][:, ks, :], core.raw[(first + c) % RING][:].rearrange("p (k d) -> p k d", k=2),
                                            hi[c % 2][:, ks, :].bitcast(F32), ALU.subtract).then_inc(core.chunk_done, 1)
                dve.wait_ge(x_landed, 16 * len(load))
                for t in range(T_LAT):
                    dve.wait_ge(product, t + 1)
                    wait(dve, added, t)
                    for n in range(2):
                        nc.vector.tensor_tensor(change[:, BANK * n:BANK * n + BANK], sums[t % 2][n][:],
                                                gain_row[:, BANK * n:BANK * n + BANK], ALU.mult).then_inc(scaled, 1)
                    dve.wait_ge(scaled, 2 * t + 2)
                    nc.vector.tensor_tensor(x[:, t, :], x[:, t, :], change[:], ALU.add).then_inc(added, 1)

            @blk.tensor
            def _(pe):
                for t in range(T_LAT):
                    wait(pe, scaled, 2 * (t - 1))
                    for k in range(KC):
                        if t == 0 and k % 2 == 0:
                            chunk_done(core, pe, first + k + 1)
                        for m, (o, w) in enumerate(((hi[0], hi[1]), (hi[0], lo[1]), (lo[0], hi[1]))):
                            for n in range(2):
                                last = nc.tensor.matmul(sums[t % 2][n][:], o[:, k, t * P:t * P + P],
                                                        w[:, k, BANK * n:BANK * n + BANK],
                                                        start=k == 0 and m == 0, stop=k == KC - 1 and m == 2)
                    last.then_inc(product, 1)


def final_stage(core, src, gain_row, dst):
    nc = core.nc
    with ExitStack() as st:
        x = st.enter_context(nc.sbuf_tensor("fin_x", [P, T_LAT, D], F32))
        y = st.enter_context(nc.sbuf_tensor("fin_y", [P, T_LAT, D], F32))
        squares = st.enter_context(nc.sbuf_tensor("fin_squares", [P, D], F32))
        ssq, rstd, eps = (st.enter_context(nc.sbuf_tensor(f"fin_{n}", [P, c], F32)) for n, c in (
            ("ssq", T_LAT), ("rstd", T_LAT), ("eps", 1)))
        x_landed = [core.sem(f"fin_x_landed{t}") for t in range(T_LAT)]
        squared, root, inverse, done, stored, eps_set = (core.sem(f"fin_{n}") for n in (
            "squared", "root", "inverse", "done", "stored", "eps_set"))
        with core.block() as blk:
            @blk.sync
            def _(sp):
                for t in range(T_LAT):
                    sp.dma_start(x[:, t, :], src[t * P:t * P + P, :]).then_inc(x_landed[t], 16)
                for t in range(T_LAT):
                    sp.wait_ge(done, t + 1)
                    sp.dma_start(dst[t * P:t * P + P, :], y[:, t, :]).then_inc(stored, 16)
                sp.wait_ge(stored, 16 * T_LAT)

            @blk.scalar
            def _(act):
                act.wait_ge(eps_set, 1)
                for t in range(T_LAT):
                    act.wait_ge(x_landed[t], 16)
                    wait(act, squared, t)
                    nc.scalar.activation(squares[:], x[:, t, :], ACT.Square, accum_out=ssq[:, t:t + 1]).then_inc(squared, 1)
                    act.wait_ge(squared, t + 1)
                    nc.scalar.activation(ssq[:, t:t + 1], ssq[:, t:t + 1], ACT.Sqrt, bias=eps[:], scale=1.0 / D).then_inc(root, 1)

            @blk.vector
            def _(dve):
                nc.vector.memset(eps[:], EPS).then_inc(eps_set, 1)
                for t in range(T_LAT):
                    dve.wait_ge(root, t + 1)
                    nc.vector.reciprocal(rstd[:, t:t + 1], ssq[:, t:t + 1]).then_inc(inverse, 1)
                    dve.wait_ge(inverse, t + 1)
                    nc.vector.scalar_tensor_tensor(y[:, t, :], x[:, t, :], rstd[:, t:t + 1], gain_row, ALU.mult, ALU.mult)\
                      .then_inc(done, 1)


def program(nc, io, out):
    tokens = "(t p) d -> p t d"
    with ExitStack() as st:
        core = Core(nc, io, st)
        setup(core)
        x_in = [io["x"][0], io["ctx"][0]]
        x_dram = [core.x_lat, core.x_ctx]
        spans = [slice(0, T_LAT), slice(T_LAT, T_LAT + T_CTX)]

        with ExitStack() as s0:
            x = s0.enter_context(nc.sbuf_tensor("x0", [P, T_LAT + T_CTX, D], F32))
            rstd = s0.enter_context(nc.sbuf_tensor("rstd0", [P, T_LAT + T_CTX], F32))
            modulation_stage(core, 0, x, [(x[:, spans[s], :], x_in[s].rearrange(tokens, p=P)) for s in range(2)], rstd[:])
            rows = s0.enter_context(nc.sbuf_tensor("rows0", [P, 4, D], F32))
            scales = [(rows[:, 2 * s + n, :], core.mod_col(0, 1 - n, s)) for s in range(2) for n in range(2)]
            broadcast_rows(core, "rows0a", scales)
            with ExitStack() as s1:
                ht = s1.enter_context(nc.sbuf_tensor("ht0", [P, KC, PADDED], F32))
                clear_padding(core, ht)
                norm_stage(core, "norm0a", x, rows, T_LAT + T_CTX, into=padded_place(ht), rstd=rstd)
                gains = s1.enter_context(nc.sbuf_tensor("pool_gain", [P, 2, KC], F32))
                pool_gains(core, gains)
                broadcast_rows(core, "rows0b", [(rows[:, s, :], gains[:, s, :]) for s in range(2)])
                pool_stage(core, ht, x, rows)
            scales = [(rows[:, 2 * s + n, :], core.mod_col(0, 4 - n, s)) for s in range(2) for n in range(2)]
            broadcast_rows(core, "rows0c", scales)
            feed_forward_choice(core, 0, 2, x, rows, [(x_dram[s].rearrange(tokens, p=P), x[:, spans[s], :]) for s in range(2)])
        with ExitStack() as s0:
            g2 = s0.enter_context(nc.sbuf_tensor("g2_0", [P, 2, D], F32))
            broadcast_rows(core, "rows0d", [(g2[:, s, :], core.mod_col(0, 5, s)) for s in range(2)])
            experts_stage(core, "moe0", 0, 2, g2, core.x_lat, core.x_ctx)

        with ExitStack() as s0:
            t_hi = s0.enter_context(nc.sbuf_tensor("t_hi", [P, KC, TOK], F32R))
            t_lo = s0.enter_context(nc.sbuf_tensor("t_lo", [P, KC, TOK], F32R))
            with ExitStack() as s1:
                x = s1.enter_context(nc.sbuf_tensor("x1a", [P, T_LAT + T_CTX, D], F32))
                rows = s1.enter_context(nc.sbuf_tensor("rows1a", [P, 4, D], F32))
                scales = [(rows[:, 2 * s + n, :], core.mod_col(1, 1 - n, s)) for s in range(2) for n in range(2)]
                broadcast_rows(core, "rows1a", scales)
                norm_stage(core, "norm1a", x, rows, T_LAT + T_CTX, split=(t_hi, t_lo),
                           load=tile_pairs(x, x_dram[0].rearrange(tokens, p=P))
                           + [(x[:, spans[1], :], x_dram[1].rearrange(tokens, p=P))])
            decay = s0.enter_context(nc.sbuf_tensor("decay", [P, 6 * KC], F32))
            decay_stage(core, decay)
            lru_stage(core, t_hi, t_lo, decay)
        with ExitStack() as s0:
            x = s0.enter_context(nc.sbuf_tensor("x1b", [P, T_LAT, D], F32))
            rows = s0.enter_context(nc.sbuf_tensor("rows1b", [P, 2, D], F32))
            broadcast_rows(core, "rows1b", [(rows[:, 0, :], core.mod_col(1, 2, 0))])
            out_stage(core, x, rows[:, 0, :], [(x[:], core.x_lat.rearrange(tokens, p=P))])
            broadcast_rows(core, "rows1c", [(rows[:, n, :], core.mod_col(1, 4 - n, 0)) for n in range(2)])
            feed_forward_choice(core, 1, 1, x, rows, [(core.x_fin.rearrange(tokens, p=P), x[:])])
        with ExitStack() as s0:
            g2 = s0.enter_context(nc.sbuf_tensor("g2_1", [P, 1, D], F32))
            broadcast_rows(core, "rows1d", [(g2[:, 0, :], core.mod_col(1, 5, 0))])
            experts_stage(core, "moe1", 1, 1, g2, core.x_fin, None)
        with ExitStack() as s0:
            gain = s0.enter_context(nc.sbuf_tensor("final_gain_row", [P, D], F32))
            broadcast_rows(core, "rows2", [(gain[:], core.vec[:, V_FG:V_FG + KC])])
            final_stage(core, core.x_fin, gain[:], out)


def tile_pairs(x, src):
    return [(x[:, 0:2, :], src[:, 0:2, :]), (x[:, 2:T_LAT, :], src[:, 2:T_LAT, :])]


def clear_padding(core, ht):
    nc = core.nc
    cleared = core.sem("padding_cleared")
    with core.block() as blk:
        @blk.vector
        def _(dve):
            gaps = ((0, OFF_LAT), (OFF_LAT + N_LAT, OFF_CTX), (OFF_CTX + N_CTX, PADDED))
            for a, b in gaps:
                nc.vector.memset(ht[:, :, a:b], 0.0).then_inc(cleared, 1)
            dve.wait_ge(cleared, len(gaps))


def pool_gains(core, gains):
    nc = core.nc
    made = core.sem("pool_gains_made")
    with core.block() as blk:
        @blk.vector
        def _(dve):
            for s in range(2):
                nc.vector.tensor_tensor(gains[:, s, :], core.vec[:, V_PS:V_PS + KC], core.mod_col(0, 2, s), ALU.mult)\
                  .then_inc(made, 1)
            dve.wait_ge(made, 2)


def feed_forward_choice(core, block, streams, x, rows, seed):
    nc, io = core.nc, core.io
    with ExitStack() as st:
        w_router = st.enter_context(nc.sbuf_tensor(f"w_router{block}", [P, KC, EXPERTS], F32))
        logits = st.enter_context(nc.psum_tensor(f"logits{block}", [P, BANK], F32))
        norm_stage(core, f"norm{block}b", x, rows, T_LAT + (T_CTX if streams == 2 else 0), router=(w_router, logits),
                   extra=[(w_router[:], io["moe_router"][block].rearrange("(k p) e -> p k e", p=P))], seed=seed)
        beside = None
        if block == 0:
            beside = Modulation(core, 1, st, MOD_BESIDE_POOL, 6 * D // BANK - MOD_BESIDE_POOL)
        choice_stage(core, f"choice{block}", block, logits, streams, beside)


_INS = ("x", "ctx", "vecs", "mod_b", "edge", "mod_w", "pool_w", "lru_w_in", "lru_wa", "lru_wx", "lru_w_out",
        "moe_router", "moe_w_gate", "moe_w_up", "moe_w_down")


def kernel(**inputs):
    import numpy as np
    import concourse.bacc as bacc
    from concourse.bass_utils import run_bass_kernel_spmd

    inputs = {name: np.asarray(a) for name, a in inputs.items()}

    def by_block(name, d=None):
        return inputs[name][0].reshape(-1, KC, P).transpose(1, 0, 2)

    lru = np.concatenate([by_block(n) for n in ("lru_conv_w", "lru_conv_b", "lru_ba", "lru_bx", "lru_lam")], axis=1)
    inputs["vecs"] = np.concatenate([inputs[n].reshape(-1, P) for n in ("c", "c_ctx", "pool_scale", "final_gain")]
                                    + [lru.reshape(-1, P)], axis=0)
    inputs["mod_b"] = inputs["mod_b"].reshape(-1, P)
    edge = np.zeros((len(WINDOWS), 2, PAD), np.float32)
    for g, w in enumerate(WINDOWS):
        for c in range(PAD):
            edge[g, 0, c] = 1.0 / min(w, c + w // 2)
            edge[g, 1, c] = 1.0 / min(w, PAD - c + w // 2)
    inputs["edge"] = edge.reshape(-1)

    nc = bacc.Bacc("TRN2", target_bir_lowering=False, num_devices=1)
    arrays, io = {}, {}
    for name in _INS:
        a = np.ascontiguousarray(inputs[name])
        arrays[f"in_{name}"] = a
        io[name] = nc.dram_tensor(f"in_{name}", a.shape, mybir.dt.from_np(a.dtype), kind="ExternalInput").ap()
    out = nc.dram_tensor("out_x", (1, N_LAT, D), F32, kind="ExternalOutput").ap()
    program(nc, io, out[0])
    result = run_bass_kernel_spmd(nc, [arrays], core_ids=[0])
    return result.results[0]["out_x"]
```

```python
from contextlib import ExitStack, contextmanager

import concourse.bass as bass
from concourse import mybir

P = 128
D = 1024
KC = D // P
N_LAT, N_CTX = 1024, 256
T_LAT, T_CTX = N_LAT // P, N_CTX // P
TOK = N_LAT + N_CTX
EXPERTS = 16
SLOTS_LAT = 2 * N_LAT // EXPERTS
SLOTS_CTX = 2 * N_CTX // EXPERTS
WINDOWS = (2, 4, 8, 16)
EPS = 1e-6
RING = 4
CHUNK = 2048
MOD_BESIDE_POOL = 4
EXP_CHUNKS = 12
LRU_COLS = 11
BANK = 512

PAD = 8
OFF_LAT = PAD
OFF_CTX = OFF_LAT + N_LAT + 2 * PAD
PADDED = OFF_CTX + N_CTX + PAD

F32 = mybir.dt.float32
F32R = mybir.dt.float32r
U32 = mybir.dt.uint32
ACT = mybir.ActivationFunctionType
ALU = mybir.AluOpType
AX = mybir.AxisListType.X
ds = bass.ds

V_C, V_CC, V_PS, V_FG, V_LRU = 0, 8, 16, 24, 32
N_VECS = V_LRU + LRU_COLS * KC


class Core:

    def __init__(self, nc, io, stack):
        self.nc, self.io, self.stack = nc, io, stack
        self.stage_sems, self.stale_sems = [], []
        self.chunks = 0
        def sb(name, shape, dt=F32):
            return stack.enter_context(nc.sbuf_tensor(name, shape, dt))

        def lasting(name):
            return stack.enter_context(nc.semaphore(name))

        self.h_lat = nc.dram_tensor("h_lat", [N_LAT, D], F32).ap()
        self.h_ctx = nc.dram_tensor("h_ctx", [N_CTX, D], F32).ap()
        self.x_lat = nc.dram_tensor("x_lat", [N_LAT, D], F32).ap()
        self.x_ctx = nc.dram_tensor("x_ctx", [N_CTX, D], F32).ap()
        self.x_fin = nc.dram_tensor("x_fin", [N_LAT, D], F32).ap()
        self.o_lru = nc.dram_tensor("o_lru", [D, N_LAT], F32).ap()
        self.raw = [sb(f"raw{i}", [P, CHUNK]) for i in range(RING)]
        self.ident = sb("ident", [P, P])
        self.ones = sb("ones", [P, P])
        self.vec = sb("vec", [P, N_VECS])
        self.mod_bias = sb("mod_bias", [P, 96])
        self.silu_c = sb("silu_c", [P, KC, 2])
        self.decay = sb("decay", [P, 4 * KC])
        self.mod = [sb(f"mod{i}", [P, 96]) for i in range(2)]
        self.gate_t = sb("gate_t", [P, 48])
        self.index_t = sb("index_t", [P, 48], U32)
        self.unused = sb("unused", [P, 1])
        self.raw_landed = [lasting(f"raw_landed{i}") for i in range(RING)]
        self.rows_made = 0
        self.diag_ready, self.spread_ready, self.row_ready = (lasting(n) for n in ("diag_ready", "spread_ready", "row_ready"))
        self.x_landed, self.lru_stored = lasting("x_landed"), lasting("lru_stored")
        self.placed = lasting("placed")
        self.chunk_done = lasting("chunk_done")

    def sem(self, name):
        self.stage_sems.append(self.nc.alloc_semaphore(name=name))
        return self.stage_sems[-1]

    @contextmanager
    def block(self):
        with self.nc.Block() as block:
            @block.gpsimd
            def _(pool):
                for sem in self.stale_sems:
                    pool.sem_clear(sem)
            yield block
        for sem in self.stale_sems:
            self.nc.release_semaphore(sem)
        self.stale_sems, self.stage_sems = self.stage_sems, []

    def mod_col(self, block, part, stream):
        return self.mod[block][:, 16 * part:16 * part + 16].rearrange("p (k s) -> p k s", s=2)[:, :, stream]


def wait(eng, sem, value):
    if isinstance(value, int) and value <= 0:
        return
    eng.wait_ge(sem, value)


def landed(core, eng, first, e=0, per=0):
    eng.wait_ge(core.raw_landed[first % RING], e * (16 * per // RING) + 16 * (first // RING + 1))


def load_chunk(core, sp, first, src, dst=None, e=0, per=0):
    sp.wait_ge(core.chunk_done, e * per + (first + 1))
    place = core.raw[first % RING]
    sp.dma_start(place[:] if dst is None else dst(place), src).then_inc(core.raw_landed[first % RING], 16)


def chunk_done(core, eng, first, e=0, per=0):
    eng.wait_ge(core.chunk_done, e * per + (RING + first + 1))


def pairs(engine, streams):
    yield 0, 0
    with engine.Fori(1, T_LAT // 2) as e:
        yield e, 0
    if streams == 2:
        yield T_LAT // 2, 1


def expert_chunk(io, block, s, e):
    if s < 8:
        w = io["moe_w_up" if s % 2 else "moe_w_gate"][block]
        return w.rearrange("e (k p) f -> p e k f", p=P)[:, ds(e, 1), :, 256 * (s // 2):256 * (s // 2) + 256]
    w = io["moe_w_down"][block]
    return w.rearrange("e (k p) f -> p e k f", p=P)[:, ds(e, 1), 2 * (s - 8):2 * (s - 8) + 2, :]


def load_expert_chunk(core, sp, block, first, s, e=0):
    shape = dict(e=1, k=KC if s < 8 else 2)
    load_chunk(core, sp, first + s, expert_chunk(core.io, block, s, e),
               lambda place: place[:].rearrange("p (e k f) -> p e k f", **shape), e, EXP_CHUNKS)



def setup(core):
    nc, io = core.nc, core.io
    with ExitStack() as st:
        rows = st.enter_context(nc.sbuf_tensor("vec_rows", [N_VECS, P], F32))
        brows = st.enter_context(nc.sbuf_tensor("modb_rows", [96, P], F32))
        turned = st.enter_context(nc.psum_tensor("turned", [P, 2, BANK], F32))
        rows_landed, made, turned_s, vec_ready, silu_ready = (
            core.sem(n) for n in ("rows_landed", "consts_made", "vecs_turned", "vec_ready", "silu_ready"))
        with core.block() as block:
            @block.sync
            def _(sp):
                sp.dma_start(rows[:], io["vecs"]).then_inc(rows_landed, 16)
                sp.dma_start(brows[:], io["mod_b"]).then_inc(rows_landed, 16)

            @block.gpsimd
            def _(pool):
                nc.gpsimd.memset(core.ident[:], 0.0).then_inc(made, 1)
                nc.gpsimd.memset(core.ones[:], 1.0).then_inc(made, 1)
                pool.wait_ge(made, 2)
                nc.gpsimd.affine_select(out=core.ident[:], in_=core.ident[:], compare_op=ALU.not_equal, fill=1.0,
                                        base=0, pattern=[[-1, P]], channel_multiplier=1).then_inc(made, 1)

            @block.tensor
            def _(pe):
                pe.wait_ge(rows_landed, 32)
                pe.wait_ge(made, 3)
                nc.tensor.transpose(turned[:, 0, 0:N_VECS], rows[:], core.ident[0:N_VECS, 0:N_VECS]).then_inc(turned_s, 1)
                nc.tensor.transpose(turned[:, 1, 0:96], brows[:], core.ident[0:96, 0:96]).then_inc(turned_s, 1)

            @block.vector
            def _(dve):
                dve.wait_ge(turned_s, 2)
                nc.vector.tensor_copy(core.vec[:], turned[:, 0, 0:N_VECS]).then_inc(vec_ready, 1)
                nc.vector.tensor_copy(core.mod_bias[:], turned[:, 1, 0:96]).then_inc(vec_ready, 1)

            @block.scalar
            def _(act):
                act.wait_ge(vec_ready, 1)
                nc.scalar.activation(core.silu_c[:, :, 0], core.vec[:, V_C:V_C + KC], ACT.Silu).then_inc(silu_ready, 1)
                nc.scalar.activation(core.silu_c[:, :, 1], core.vec[:, V_CC:V_CC + KC], ACT.Silu).then_inc(silu_ready, 1)


class Modulation:
    BODY = 2

    def __init__(self, core, block, stack, start=0, strips=6 * D // BANK):
        nc = core.nc
        self.core, self.block, self.start, self.n_strips = core, block, start, strips
        self.first = core.chunks
        core.chunks += 2 * strips
        self.row_banks = [stack.enter_context(nc.psum_tensor(f"mod{block}_{start}_rows{i}", [P, BANK], F32)) for i in range(2)]
        self.col_bank = stack.enter_context(nc.psum_tensor(f"mod{block}_{start}_cols", [P, BANK], F32))
        self.rows = [stack.enter_context(nc.sbuf_tensor(f"mod{block}_{start}_row{i}", [2, BANK], F32)) for i in range(2)]
        self.copied = core.sem(f"mod_copied{block}_{start}")
        self.turned = core.sem(f"mod_turned{block}_{start}")
        self.ready = core.sem(f"mod_ready{block}_{start}")

    def strips(self, engine):
        for i in range(self.BODY):
            yield 0, i
        with engine.Fori(1, self.n_strips // self.BODY) as e:
            for i in range(self.BODY):
                yield e, i

    def load(self, sp):
        w = self.core.io["mod_w"][self.block].rearrange("(h k p) (u m) -> p h k u m", p=P, h=2, m=BANK)
        for e, i in self.strips(self.core.nc.sync):
            for h in range(2):
                load_chunk(self.core, sp, self.first + 2 * i + h, w[:, h, :, ds(e * self.BODY + (self.start + i), 1), :],
                           lambda place: place[:].rearrange("p (k u m) -> p k u m", k=KC // 2, u=1), e, 2 * self.BODY)

    def products(self, pe):
        core, nc = self.core, self.core.nc

        def turn(i, count):
            pe.wait_ge(self.copied, count + 1)
            for c in range(BANK // P):
                last = nc.tensor.matmul(self.col_bank[:, ds(count * 8 + 2 * c, 2)], self.rows[i][:, c * P:(c + 1) * P],
                                        core.ident[0:2, 0:2], start=True, stop=True)
            last.then_inc(self.turned, 1)

        for e, i in self.strips(nc.tensor):
            strip = e * self.BODY + i
            wait(pe, self.copied, strip - 1)
            for h in range(2):
                at = self.first + 2 * i + h
                landed(core, pe, at, e, 2 * self.BODY)
                for k in range(KC // 2):
                    last = nc.tensor.matmul(self.row_banks[i][0:2, :], core.silu_c[:, KC // 2 * h + k, :],
                                            core.raw[at % RING][:, BANK * k:BANK * (k + 1)],
                                            start=h == 0 and k == 0, stop=h == 1 and k == KC // 2 - 1)
                last.then_inc(core.chunk_done, 1)
            if not isinstance(e, int) or strip > 0:
                turn(1 - i, strip - 1)
        turn(self.BODY - 1, self.n_strips - 1)

    def copy_out(self, act):
        nc = self.core.nc
        for e, i in self.strips(nc.scalar):
            chunk_done(self.core, act, self.first + 2 * i + 1, e, 2 * self.BODY)
            wait(act, self.turned, e * self.BODY + (i - 1))
            nc.scalar.activation(self.rows[i][:], self.row_banks[i][0:2, :], ACT.Copy).then_inc(self.copied, 1)

    def finish(self, dve):
        core, nc = self.core, self.core.nc
        dve.wait_ge(self.turned, self.n_strips)
        at, n = 8 * self.start, 8 * self.n_strips
        out = core.mod[self.block][:, at:at + n].rearrange("p (c s) -> p c s", s=2)
        bias = core.mod_bias[:, 48 * self.block + at // 2:48 * self.block + (at + n) // 2]
        nc.vector.tensor_tensor(out, self.col_bank[:, 0:n].rearrange("p (c s) -> p c s", s=2),
                                bias.unsqueeze(2).to_broadcast([P, n // 2, 2]), ALU.add).then_inc(self.ready, 1)
        dve.wait_ge(self.ready, 1)
        for part in (1, 4):
            if at <= 16 * part < at + n:
                cols = core.mod[self.block][:, 16 * part:16 * part + 16]
                nc.vector.tensor_scalar(cols, cols, 1.0, None, ALU.add).then_inc(self.ready, 1)


class Decay:

    def __init__(self, core, stack):
        self.core = core
        self.neg, self.mag, self.e, self.s, self.s2, self.acc = (
            stack.enter_context(core.nc.sbuf_tensor(f"decay_{n}", [P, KC, 2], F32))
            for n in ("neg", "mag", "e", "s", "s2", "acc"))
        self.step, self.exps = core.sem("decay_step"), core.sem("decay_exps")

    def on_vector(self, dve):
        nc = self.core.nc
        neg, mag, e, s, s2, acc = self.neg, self.mag, self.e, self.s, self.s2, self.acc
        terms = 9
        lam = self.core.vec[:, V_LRU:V_LRU + LRU_COLS * KC].rearrange("p (b c) -> p b c", c=LRU_COLS)[:, :, LRU_COLS - 2:]
        done = [0]

        def chain(ins):
            ins.then_inc(self.step, 1)
            done[0] += 1
            dve.wait_ge(self.step, done[0])

        chain(nc.vector.tensor_scalar(neg[:], lam, -1.0, None, ALU.mult))
        chain(nc.vector.tensor_tensor(mag[:], lam, neg[:], ALU.max))
        dve.wait_ge(self.exps, 1)
        chain(nc.vector.tensor_scalar(s2[:], e[:], 2.0, None, ALU.add))
        chain(nc.vector.reciprocal(s2[:], s2[:]))
        chain(nc.vector.tensor_tensor(s[:], e[:], s2[:], ALU.mult))
        chain(nc.vector.tensor_tensor(s2[:], s[:], s[:], ALU.mult))
        chain(nc.vector.memset(acc[:], 1.0 / (2 * terms + 1)))
        for n in reversed(range(terms)):
            chain(nc.vector.tensor_tensor(acc[:], acc[:], s2[:], ALU.mult))
            chain(nc.vector.tensor_scalar(acc[:], acc[:], 1.0 / (2 * n + 1), None, ALU.add))
        chain(nc.vector.tensor_tensor(acc[:], acc[:], s[:], ALU.mult))
        chain(nc.vector.tensor_scalar(neg[:], neg[:], 0.0, None, ALU.max))
        chain(nc.vector.scalar_tensor_tensor(acc[:], acc[:], 2.0, neg[:], ALU.mult, ALU.add))
        out = self.core.decay[:].rearrange("p (b d m) -> p b d m", d=2, m=2)
        for m, f in enumerate((-8.0, 8.0)):
            chain(nc.vector.tensor_scalar(out[:, :, :, m], acc[:], f, None, ALU.mult))

    def on_scalar(self, act):
        act.wait_ge(self.step, 2)
        self.core.nc.scalar.activation(self.e[:], self.mag[:], ACT.Exp, scale=-1.0).then_inc(self.exps, 1)


def modulation_stage(core, block, x, load, rstd):
    nc = core.nc
    tiles = x.shape[1]
    with ExitStack() as st:
        mod = Modulation(core, block, st)
        decay = Decay(core, st)
        squares = st.enter_context(nc.sbuf_tensor("first_squares", [P, D], F32))
        eps = st.enter_context(nc.sbuf_tensor("first_eps", [P, 1], F32))
        squared, root, rstd_ready = (core.sem(f"first_{n}") for n in ("squared", "root", "rstd_ready"))
        x_landed = core.x_landed
        with core.block() as blk:
            @blk.sync
            def _(sp):
                mod.load(sp)

            @blk.gpsimd
            def _(pool):
                for at, (count, src) in zip((0, T_LAT), load):
                    with nc.gpsimd.Fori(0, count) as t:
                        pool.wait_ge(core.chunk_done, t * 2 + (RING + mod.first + 2 * at + 1))
                        pool.dma_start(x[:, ds(t + at, 1), :], src[:, ds(t, 1), :]).then_inc(x_landed, 16)

            @blk.tensor
            def _(pe):
                mod.products(pe)

            @blk.scalar
            def _(act):
                decay.on_scalar(act)
                mod.copy_out(act)
                act.wait_ge(squared, tiles + 1)
                nc.scalar.activation(rstd, rstd, ACT.Sqrt, bias=eps[:], scale=1.0 / D).then_inc(root, 1)

            @blk.vector
            def _(dve):
                nc.vector.memset(core.unused[:], 0.0).then_inc(core.chunk_done, RING)
                nc.vector.memset(eps[:], EPS).then_inc(squared, 1)
                decay.on_vector(dve)
                dve.wait_ge(x_landed, 16 * tiles)
                for t in range(tiles):
                    dve.wait_ge(squared, t + 1)
                    nc.vector.tensor_tensor_reduce(squares[:], x[:, t, :], x[:, t, :], 1.0, 0.0, ALU.mult, ALU.add,
                                                   accum_out=rstd[:, t:t + 1]).then_inc(squared, 1)
                mod.finish(dve)
                dve.wait_ge(root, 1)
                nc.vector.reciprocal(rstd, rstd).then_inc(rstd_ready, 1)


def broadcast_rows(core, name, wanted):
    nc = core.nc
    with ExitStack() as st:
        diag = [st.enter_context(nc.sbuf_tensor(f"{name}_diag{i}", [P, KC, P], F32)) for i in range(2)]
        spread = [st.enter_context(nc.psum_tensor(f"{name}_spread{i}", [P, 2, BANK], F32)) for i in range(2)]
        diag_ready, spread_ready, row_ready = core.diag_ready, core.spread_ready, core.row_ready
        base = core.rows_made
        core.rows_made += len(wanted)
        with core.block() as blk:
            @blk.vector
            def _(dve):
                for i, (_, col) in enumerate(wanted):
                    wait(dve, spread_ready, base + i - 1 if i > 1 else 0)
                    nc.vector.tensor_tensor(diag[i % 2][:], core.ident[:].unsqueeze(1).to_broadcast([P, KC, P]),
                                            col.unsqueeze(2).to_broadcast([P, KC, P]), ALU.mult).then_inc(diag_ready, 1)

            @blk.tensor
            def _(pe):
                for i in range(len(wanted)):
                    pe.wait_ge(diag_ready, base + i + 1)
                    wait(pe, row_ready, base + i - 1 if i > 1 else 0)
                    for n in range(2):
                        last = nc.tensor.matmul(spread[i % 2][:, n, :], core.ones[:],
                                                diag[i % 2][:, 4 * n:4 * n + 4, :].rearrange("p k m -> p (k m)"),
                                                start=True, stop=True)
                    last.then_inc(spread_ready, 1)

            @blk.scalar
            def _(act):
                for i, (row, _) in enumerate(wanted):
                    act.wait_ge(spread_ready, base + i + 1)
                    nc.scalar.activation(row, spread[i % 2][:].rearrange("p n m -> p (n m)"), ACT.Copy)\
                      .then_inc(row_ready, 1)



def norm_stage(core, name, x, rows, tiles, into=None, split=None, router=None, load=(), extra=(), seed=(), rstd=None,
               prefetch=None, columns=None):
    nc = core.nc
    streams = 2 if tiles > T_LAT else 1
    known = rstd is not None
    with ExitStack() as st:
        junk = st.enter_context(nc.sbuf_tensor(f"{name}_squares", [P, D], F32))
        ssq = [st.enter_context(nc.sbuf_tensor(f"{name}_ssq{i}", [P, 1], F32)) for i in range(2)]
        inverse = [st.enter_context(nc.sbuf_tensor(f"{name}_inverse{i}", [P, 1], F32)) for i in range(2)]
        eps = st.enter_context(nc.sbuf_tensor(f"{name}_eps", [P, 1], F32))
        h = [st.enter_context(nc.sbuf_tensor(f"{name}_h{i}", [P, D], F32)) for i in range(2)]
        turned = [st.enter_context(nc.psum_tensor(f"{name}_turned{i}", [P, 4, P], F32)) for i in range(4)]
        if router:
            w_router, logits = router
            ht = [st.enter_context(nc.sbuf_tensor(f"{name}_ht{i}", [P, KC, P], F32)) for i in range(2)]
            by_expert = st.enter_context(nc.sbuf_tensor(f"{name}_by_expert", [EXPERTS, tiles * P], F32))
            by_expert_sum = st.enter_context(nc.psum_tensor(f"{name}_by_expert_sum", [P, 3 * BANK], F32))
            by_expert_ready = core.sem(f"{name}_by_expert_ready")
        (first_landed, rest_landed, extra_landed, squared, eps_set, root, rstd_ready, scaled, h_ready, turned_lo, turned_hi,
         out_lo, out_hi) = (core.sem(f"{name}_{n}") for n in (
            "first_landed", "rest_landed", "extra_landed", "squared", "eps_set", "root", "rstd_ready", "scaled", "h_ready",
            "turned_lo", "turned_hi", "out_lo", "out_hi"))
        stored0, stored1, seeded, routed = (
            core.sem(f"{name}_{n}") if router else None for n in ("stored0", "stored1", "seeded", "routed"))
        stored = (stored0, stored1)
        if split:
            whole = [st.enter_context(nc.sbuf_tensor(f"{name}_whole{i}", [P, KC, P], F32)) for i in range(2)]
            split_hi, split_lo = core.sem(f"{name}_split_hi"), core.sem(f"{name}_split_lo")
        LAST = (tiles // 2 - 1, streams - 1, 1)

        def steps(engine):
            for e, stream in pairs(engine, streams):
                for i in range(2):
                    if i == 1:
                        before = (e, stream, 0)
                    elif isinstance(e, int) and e == 0:
                        before = None
                    else:
                        before = (e - 1, 0, 1)
                    yield before, (e, stream, i)

        def x_landed(eng, e):
            if isinstance(e, int) and e == 0:
                eng.wait_ge(first_landed, 16)
            else:
                eng.wait_ge(rest_landed, 16 * (len(load) - 1))

        with core.block() as blk:
            @blk.sync
            def _(sp):
                for n, (dst, src) in enumerate(load):
                    sp.dma_start(dst, src).then_inc(rest_landed if n else first_landed, 16)
                for dst, src in extra:
                    sp.dma_start(dst, src).then_inc(extra_landed, 16)
                if prefetch:
                    prefetch(sp)
                if router:
                    for e, stream in pairs(nc.sync, streams):
                        out = (core.h_ctx if stream else core.h_lat).rearrange("(t p) d -> p t d", p=P)
                        for i in range(2):
                            sp.wait_ge(h_ready, e * 2 + (i + 1))
                            sp.dma_start(out[:, ds(e * 2 + (i - T_LAT * stream), 1), :], h[i][:].unsqueeze(1))\
                              .then_inc(stored[i], 16)
                        sp.dma_start(seed[stream][:, ds(e * 2 - T_LAT * stream, 2), :], x[:, ds(e * 2, 2), :]).then_inc(seeded, 16)
                    for i in range(2):
                        sp.wait_ge(stored[i], 16 * (tiles // 2))
                    sp.wait_ge(seeded, 16 * (tiles // 2))

            @blk.scalar
            def _(act):
                def root_mean_square(e, i):
                    t = e * 2 + i
                    if load:
                        x_landed(act, e)
                    wait(act, squared, t)
                    wait(act, rstd_ready, e * 2 + (i - 1))
                    nc.scalar.activation(junk[:], x[:, ds(t, 1), :].rearrange("p a d -> p (a d)"), ACT.Square,
                                         accum_out=ssq[i][:]).then_inc(squared, 1)
                    act.wait_ge(squared, t + 1)
                    nc.scalar.activation(ssq[i][:], ssq[i][:], ACT.Sqrt, bias=eps[:], scale=1.0 / D).then_inc(root, 1)

                def modulated(out, bank, stream, k0):
                    scales, shifts = columns(stream)
                    for k in range(4):
                        last = nc.scalar.activation(out[:, k, :], bank[:, k, :], ACT.Identity,
                                                    scale=scales[:, k0 + k:k0 + k + 1], bias=shifts[:, k0 + k:k0 + k + 1])
                    return last

                def copy_lo(e, stream, i):
                    t = e * 2 + i
                    act.wait_ge(turned_lo, e * 2 + (i + 1))
                    if router:
                        wait(act, routed, e * 2 + (i - 1))
                        nc.scalar.activation(ht[i][:, 0:4, :], turned[2 * i][:], ACT.Copy).then_inc(out_lo, 1)
                    elif split:
                        wait(act, split_lo, e * 2 + (i - 1))
                        modulated(whole[i][:, 0:4, :], turned[2 * i][:], stream, 0).then_inc(out_lo, 1)
                        act.wait_ge(out_lo, e * 2 + (i + 1))
                        act.wait_ge(out_hi, e * 2 + (i + 1))
                        nc.scalar.activation(split[0][:, :, ds(t * P, P)], whole[i][:], ACT.Copy).then_inc(split_hi, 1)
                    else:
                        modulated(into(0, t, stream), turned[2 * i][:], stream, 0).then_inc(out_lo, 1)

                if not known:
                    act.wait_ge(eps_set, 1)
                for before, (e, stream, i) in steps(nc.scalar):
                    if not known:
                        root_mean_square(e, i)
                    if before:
                        copy_lo(*before)
                copy_lo(*LAST)
                if router:
                    act.wait_ge(routed, tiles)
                    nc.scalar.activation(by_expert[:], by_expert_sum[0:EXPERTS, 0:tiles * P], ACT.Copy).then_inc(by_expert_ready, 1)

            @blk.vector
            def _(dve):
                def modulated(out, bank, stream, k0):
                    scales, shifts = columns(stream)
                    for k in range(4):
                        last = nc.vector.tensor_scalar(out[:, k, :], bank[:, k, :], scales[:, k0 + k:k0 + k + 1],
                                                       shifts[:, k0 + k:k0 + k + 1], ALU.mult, ALU.add)
                    return last

                def scale(e, stream, i):
                    t = e * 2 + i
                    if not known:
                        dve.wait_ge(root, t + 1)
                        wait(dve, h_ready, e * 2 + (i - 1))
                        nc.vector.reciprocal(inverse[i][:], ssq[i][:]).then_inc(rstd_ready, 1)
                        dve.wait_ge(rstd_ready, t + 1)
                    wait(dve, turned_hi, e * 2 + (i - 1))
                    if router:
                        wait(dve, stored[i], e * 16)
                    x_tile, per_token = x[:, ds(t, 1), :].rearrange("p a d -> p (a d)"), rstd[:, ds(t, 1)] if known else inverse[i][:]
                    if columns:
                        nc.vector.tensor_scalar(h[i][:], x_tile, per_token, None, ALU.mult).then_inc(h_ready, 1)
                        return
                    nc.vector.scalar_tensor_tensor(h[i][:], x_tile, per_token, rows[:, 2 * stream, :],
                                                   ALU.mult, ALU.mult).then_inc(scaled, 1)
                    dve.wait_ge(scaled, t + 1)
                    nc.vector.tensor_tensor(h[i][:], h[i][:], rows[:, 2 * stream + 1, :], ALU.add).then_inc(h_ready, 1)

                def copy_hi(e, stream, i):
                    t = e * 2 + i
                    dve.wait_ge(turned_hi, e * 2 + (i + 1))
                    if router:
                        wait(dve, routed, e * 2 + (i - 1))
                        nc.vector.tensor_copy(ht[i][:, 4:8, :], turned[2 * i + 1][:]).then_inc(out_hi, 1)
                    elif split:
                        modulated(whole[i][:, 4:8, :], turned[2 * i + 1][:], stream, 4).then_inc(out_hi, 1)
                        dve.wait_ge(split_hi, t + 1)
                        nc.vector.tensor_tensor(split[1][:, :, ds(t * P, P)], whole[i][:],
                                                split[0][:, :, ds(t * P, P)].bitcast(F32), ALU.subtract).then_inc(split_lo, 1)
                    else:
                        modulated(into(4, t, stream), turned[2 * i + 1][:], stream, 4).then_inc(out_hi, 1)

                if not known:
                    nc.vector.memset(eps[:], EPS).then_inc(eps_set, 1)
                for before, this in steps(nc.vector):
                    scale(*this)
                    if before:
                        copy_hi(*before)
                copy_hi(*LAST)

            @blk.tensor
            def _(pe):
                def route(e, stream, i):
                    pe.wait_ge(out_lo, e * 2 + (i + 1))
                    pe.wait_ge(out_hi, e * 2 + (i + 1))
                    for k in range(KC):
                        last = nc.tensor.matmul(by_expert_sum[0:EXPERTS, ds((e * 2 + i) * P, P)], w_router[:, k, :],
                                                ht[i][:, k, :], start=k == 0, stop=k == KC - 1)
                    last.then_inc(routed, 1)

                if extra:
                    pe.wait_ge(extra_landed, 16 * len(extra))
                for before, (e, stream, i) in steps(nc.tensor):
                    pe.wait_ge(h_ready, e * 2 + (i + 1))
                    wait(pe, out_lo, e * 2 + (i - 1))
                    wait(pe, out_hi, e * 2 + (i - 1))
                    for k in range(KC):
                        last = nc.tensor.transpose(turned[2 * i + k // 4][:, k % 4, :], h[i][:, k * P:(k + 1) * P],
                                                   core.ident[:])
                        if k == 3:
                            last.then_inc(turned_lo, 1)
                    last.then_inc(turned_hi, 1)
                    if router and before:
                        route(*before)
                if router:
                    route(*LAST)
                    pe.wait_ge(by_expert_ready, 1)
                    for t in range(tiles):
                        nc.tensor.transpose(logits[:, t * EXPERTS:(t + 1) * EXPERTS], by_expert[:, t * P:(t + 1) * P],
                                            core.ident[0:EXPERTS, 0:EXPERTS])



def choice_stage(core, name, block, logits, streams, beside=None):
    nc = core.nc
    tiles = T_LAT + (T_CTX if streams == 2 else 0)
    rounds = SLOTS_LAT // 8
    with ExitStack() as st:
        def sb(n, shape, dt=F32):
            return st.enter_context(nc.sbuf_tensor(f"{name}_{n}", shape, dt))

        top, total, inv = sb("top", [P, tiles]), sb("total", [P, tiles]), sb("inv", [P, tiles])
        aff = sb("aff", [P, tiles, EXPERTS])
        wide = sb("wide", [P, T_LAT, 48])
        pool_of = [sb(f"left{i}", [48, N_LAT]) for i in range(2)]
        best, where, where_f = sb("best", [48, SLOTS_LAT]), sb("where", [48, SLOTS_LAT], U32), sb("where_f", [48, SLOTS_LAT])
        turned = [st.enter_context(nc.psum_tensor(f"{name}_turned{i}", [P, 4, P], F32)) for i in range(2)]
        out = [st.enter_context(nc.psum_tensor(f"{name}_out{i}", [P, BANK], F32)) for i in range(2)]
        step, exps, turned_s, chosen, back = (core.sem(f"{name}_{n}") for n in (
            "step", "exps", "turned_s", "chosen", "back"))
        placed = core.placed
        with core.block() as blk:
            @blk.vector
            def _(dve):
                done = [0]

                def chain(ins):
                    ins.then_inc(step, 1)
                    done[0] += 1
                    dve.wait_ge(step, done[0])

                seen = logits[:, 0:tiles * EXPERTS].rearrange("p (t e) -> p t e", e=EXPERTS)
                nc.vector.memset(wide[:], -1.0)
                chain(nc.vector.tensor_reduce(top[:], seen, AX, ALU.max))
                chain(nc.vector.tensor_tensor(aff[:], seen, top[:].unsqueeze(2).to_broadcast([P, tiles, EXPERTS]),
                                              ALU.subtract))
                dve.wait_ge(exps, 1)
                chain(nc.vector.tensor_reduce(total[:], aff[:], AX, ALU.add))
                chain(nc.vector.reciprocal(inv[:], total[:]))
                ends = [(0, T_LAT, 0)] + ([(T_LAT, tiles, 32)] if streams == 2 else [])
                for a, b, col in ends:
                    chain(nc.vector.tensor_tensor(wide[:, 0:b - a, col:col + EXPERTS], aff[:, a:b, :],
                                                  inv[:, a:b].unsqueeze(2).to_broadcast([P, b - a, EXPERTS]), ALU.mult))
                for n in range(2):
                    dve.wait_ge(turned_s, n + 1)
                    chain(nc.vector.tensor_copy(pool_of[0][:, BANK * n:BANK * n + BANK],
                                                turned[n][0:48].rearrange("p k m -> p (k m)")))
                for r in range(rounds):
                    left, rest = pool_of[r % 2], pool_of[1 - r % 2]
                    eight = best[:, 8 * r:8 * r + 8]
                    chain(nc.vector.max(eight, left[:]))
                    nc.vector.max_index(where[:, 8 * r:8 * r + 8], eight, left[:]).then_inc(chosen, 1)
                    if r < rounds - 1:
                        chain(nc.vector.match_replace(rest[:], eight, left[:], -1.0))
                dve.wait_ge(chosen, rounds)
                nc.vector.tensor_copy(where_f[:], where[:]).then_inc(chosen, 1)
                dve.wait_ge(back, 1)
                nc.vector.tensor_copy(core.gate_t[:], out[0][:, 0:48]).then_inc(placed, 1)
                dve.wait_ge(back, 2)
                nc.vector.tensor_copy(core.index_t[:], out[1][:, 0:48]).then_inc(placed, 1)
                if beside:
                    beside.finish(dve)

            @blk.scalar
            def _(act):
                act.wait_ge(step, 2)
                nc.scalar.activation(aff[:], aff[:], ACT.Exp).then_inc(exps, 1)
                if beside:
                    beside.copy_out(act)

            @blk.tensor
            def _(pe):
                pe.wait_ge(step, 4 + streams)
                for t in range(T_LAT):
                    last = nc.tensor.transpose(turned[t // 4][0:48, t % 4, :], wide[:, t, :], core.ident[:])
                    if t % 4 == 3:
                        last.then_inc(turned_s, 1)
                if beside:
                    beside.products(pe)
                pe.wait_ge(chosen, rounds + 1)
                nc.tensor.transpose(out[0][:, 0:48], best[:], core.ident[0:48, 0:48]).then_inc(back, 1)
                nc.tensor.transpose(out[1][:, 0:48], where_f[:], core.ident[0:48, 0:48]).then_inc(back, 1)

            @blk.sync
            def _(sp):
                if beside:
                    beside.load(sp)
                for s in range(RING):
                    load_expert_chunk(core, sp, block, core.chunks, s)



def experts_stage(core, name, block, streams, g2_rows, x_lat, x_ctx):
    nc, io = core.nc, core.io
    slots = SLOTS_LAT + (SLOTS_CTX if streams == 2 else 0)
    first = core.chunks
    core.chunks += EXPERTS * EXP_CHUNKS
    PLACES, LEAD = 6, 4
    h_cols = SLOTS_LAT + (2 * SLOTS_CTX if streams == 2 else 0) + SLOTS_LAT
    with ExitStack() as st:
        def sb(n, shape, dt=F32):
            return st.enter_context(nc.sbuf_tensor(f"{name}_{n}", shape, dt))

        def psum(n, banks=1):
            return st.enter_context(nc.psum_tensor(f"{name}_{n}", [P, banks * BANK], F32))

        w_hi = [sb(f"w_hi{i}", [P, CHUNK], F32R) for i in range(PLACES)]
        w_lo = [sb(f"w_lo{i}", [P, CHUNK], F32R) for i in range(PLACES)]
        xg, xg_ctx = sb("xg", [P, D]), sb("xg_ctx", [SLOTS_CTX, D])
        x = sb("x", [P, KC, 2, slots], F32R)
        part = [sb(f"part{i}", [P, 2, slots]) for i in range(2)]
        gate_up_s = [sb(f"gate_up{i}", [P, 2, slots]) for i in range(2)]
        silu_g = [sb(f"silu_g{i}", [P, slots]) for i in range(2)]
        prod = [sb(f"prod{i}", [P, slots]) for i in range(2)]
        h = sb("h", [P, KC, h_cols], F32R)
        y, y_ctx, ctx_part = sb("y", [P, D]), sb("y_ctx", [SLOTS_CTX, D]), sb("ctx_part", [SLOTS_CTX, D])
        gu = [psum(f"gu{i}", 2) for i in range(2)]
        y_sum = [psum(f"y_sum{i}") for i in range(2)]
        y_ctx_sum = psum("y_ctx_sum", 2) if streams == 2 else None
        (hi_done, gathered, gathered_ctx, turned_s, x_hi_done, x_ready, gu_ready, part_done, sum_done, silu_done,
         prod_done, h_hi_done, h_ready, down_done, ctx_part_done, ctx_added, y_ready, scattered, scattered_ctx) = (
            core.sem(f"{name}_{n}") for n in (
                "hi_done", "gathered", "gathered_ctx", "turned", "x_hi_done", "x_ready", "gu_ready", "part_done",
                "sum_done", "silu_done", "prod_done", "h_hi_done", "h_ready", "down_done", "ctx_part_done", "ctx_added",
                "y_ready", "scattered", "scattered_ctx"))
        turns = 2 + (streams == 2)

        def experts(engine):
            yield 0, False
            with engine.Fori(1, EXPERTS - 1) as e:
                yield e, False
            yield EXPERTS - 1, True

        def place_free(eng, s, e):
            if s < PLACES:
                before = s + EXP_CHUNKS - PLACES
                if before < 8:
                    wait(eng, gu_ready, e * KC)
                else:
                    wait(eng, down_done, e * 4 + (before - 8 + 1 - 4))
            else:
                eng.wait_ge(gu_ready, e * KC + (2 * ((s - PLACES) // 2) + 2))

        def turn_views(g):
            if g < 2:
                return (gu[0][:, BANK * g:BANK * (g + 1)].rearrange("p (k m) -> p k m", k=4),
                        (slice(4 * g, 4 * g + 4), slice(0, SLOTS_LAT)))
            return (gu[1][:, 0:KC * SLOTS_CTX].rearrange("p (k m) -> p k m", k=KC),
                    (slice(0, KC), slice(SLOTS_LAT, slots)))

        def gu_view(j, n):
            return gu[j % 2][:].rearrange("p (w m) -> p w m", w=2)[:, :, slots * n:slots * (n + 1)]

        with core.block() as blk:
            @blk.sync
            def _(sp):
                for s in range(RING, EXP_CHUNKS):
                    load_expert_chunk(core, sp, block, first, s)
                with nc.sync.Fori(1, EXPERTS) as e:
                    for s in range(EXP_CHUNKS):
                        load_expert_chunk(core, sp, block, first, s, e)

            @blk.gpsimd
            def _(pool):
                rows_of = ((xg, y, core.h_lat, x_lat, gathered, scattered, SLOTS_LAT, 0),
                           (xg_ctx, y_ctx, core.h_ctx, x_ctx, gathered_ctx, scattered_ctx, SLOTS_CTX, 32))[:streams]
                for e in range(-1, EXPERTS):
                    if e + 1 < EXPERTS:
                        wait(pool, turned_s, (e + 1) * turns)
                        for got, _, rows, _, landed_s, _, n, col in rows_of:
                            index = core.index_t[0:n, e + 1 + col:e + 2 + col]
                            nc.gpsimd.indirect_dma_start(got[:], None, rows, bass.IndirectOffsetOnAxis(ap=index, axis=0))\
                              .then_inc(landed_s, 16)
                    if e >= 0:
                        pool.wait_ge(y_ready, (e + 1) * 2 * streams)
                        for _, add, _, to, _, added_s, n, col in rows_of:
                            wait(pool, added_s, e * 16)
                            index = core.index_t[0:n, e + col:e + 1 + col]
                            nc.gpsimd.indirect_dma_start(to, bass.IndirectOffsetOnAxis(ap=index, axis=0), add[:], None,
                                                         compute_op=ALU.add).then_inc(added_s, 16)
                for _, _, _, _, _, added_s, _, _ in rows_of:
                    pool.wait_ge(added_s, 16 * EXPERTS)

            @blk.tensor
            def _(pe):
                def turn(e):
                    pe.wait_ge(gathered, e * 16 + 16)
                    wait(pe, sum_done, e * KC)
                    for g in range(2):
                        if g == 1 and streams == 2:
                            pe.wait_ge(gathered_ctx, e * 16 + 16)
                        for k in range(4):
                            last = nc.tensor.transpose(gu[0][:, BANK * g + k * P:BANK * g + (k + 1) * P],
                                                       xg[:, (4 * g + k) * P:(4 * g + k + 1) * P], core.ident[:])
                        last.then_inc(turned_s, 1)
                    if streams == 2:
                        for k in range(KC):
                            last = nc.tensor.transpose(gu[1][:, k * SLOTS_CTX:(k + 1) * SLOTS_CTX],
                                                       xg_ctx[:, k * P:(k + 1) * P], core.ident[0:SLOTS_CTX, 0:SLOTS_CTX])
                        last.then_inc(turned_s, 1)

                def gate_up(e):
                    pe.wait_ge(x_ready, e * turns + turns)
                    for j in range(KC):
                        if j % 2 == 0:
                            chunk_done(core, pe, first + j + 1, e, EXP_CHUNKS)
                        wait(pe, sum_done, e * KC + (j - 1))
                        for which in range(2):
                            at = (j // 2 * 2 + which) % PLACES
                            out = gu[j % 2][:, BANK * which:BANK * which + 2 * slots]
                            for k in range(KC):
                                col = 256 * k + P * (j % 2)
                                passes = ((w_hi, 2), (w_lo, 1)) if k < KC - 1 else ((w_lo, 1), (w_hi, 2))
                                for n, (w, cols) in enumerate(passes):
                                    last = nc.tensor.matmul(out[:, 0:cols * slots], w[at][:, col:col + P],
                                                            x[:, k, 0:cols, :], start=k == 0 and n == 0,
                                                            stop=k == KC - 1 and n == 1)
                        last.then_inc(gu_ready, 1)

                def down(e, r):
                    chunk_done(core, pe, first + 8 + r, e, EXP_CHUNKS)
                    pe.wait_ge(h_ready, e * KC + (2 * r + 2))
                    w = (8 + r) % PLACES
                    for kk in range(2):
                        k = 2 * r + kk
                        lat_hi, lat_lo = h[:, k, 0:SLOTS_LAT], h[:, k, h_cols - SLOTS_LAT:h_cols]
                        ctx_hi = h[:, k, SLOTS_LAT:SLOTS_LAT + SLOTS_CTX]
                        ctx_both = h[:, k, SLOTS_LAT:SLOTS_LAT + 2 * SLOTS_CTX]
                        for c in range(2):
                            cols = slice(D * kk + BANK * c, D * kk + BANK * (c + 1))
                            hi, lo = w_hi[w][:, cols], w_lo[w][:, cols]
                            for n, (a, b) in enumerate(((lat_hi, hi), (lat_hi, lo), (lat_lo, hi))):
                                last = nc.tensor.matmul(y_sum[c][:], a, b, start=k == 0 and n == 0,
                                                        stop=k == KC - 1 and n == 2)
                            if streams == 2:
                                passes = ((ctx_both, hi, 2), (ctx_hi, lo, 1))
                                if k == KC - 1:
                                    passes = passes[::-1]
                                for n, (a, b, rows) in enumerate(passes):
                                    last = nc.tensor.matmul(y_ctx_sum[0:rows * SLOTS_CTX, BANK * c:BANK * (c + 1)], a, b,
                                                            start=k == 0 and n == 0, stop=k == KC - 1 and n == 1)
                    last.then_inc(down_done, 1)

                turn(0)
                for e, is_last in experts(nc.tensor):
                    gate_up(e)
                    wait(pe, y_ready, e * (2 * streams))
                    down(e, 0)
                    down(e, 1)
                    if not is_last:
                        turn(e + 1)
                    down(e, 2)
                    down(e, 3)

            @blk.scalar
            def _(act):
                def weights_hi(s, e):
                    landed(core, act, first + s, e, EXP_CHUNKS)
                    place_free(act, s, e)
                    nc.scalar.activation(w_hi[s % PLACES][:], core.raw[(first + s) % RING][:], ACT.Copy).then_inc(hi_done, 1)

                def tokens_hi(e):
                    for g in range(turns):
                        bank, (ks, cols) = turn_views(g)
                        act.wait_ge(turned_s, e * turns + (g + 1))
                        nc.scalar.activation(x[:, ks, 0, cols], bank, ACT.Copy).then_inc(x_hi_done, 1)

                def context_part(e):
                    act.wait_ge(down_done, e * 4 + 4)
                    wait(act, y_ready, e * (2 * streams))
                    nc.scalar.activation(ctx_part[:], y_ctx_sum[SLOTS_CTX:2 * SLOTS_CTX, :], ACT.Copy)\
                      .then_inc(ctx_part_done, 1)

                for s in range(LEAD):
                    if s == LEAD - 1:
                        tokens_hi(0)
                    weights_hi(s, 0)
                for e, is_last in experts(nc.scalar):
                    for t in range(EXP_CHUNKS):
                        j = t - 1
                        if t == 0 and streams == 2 and (not isinstance(e, int) or e > 0):
                            context_part(e - 1)
                        if 0 <= j < KC:
                            act.wait_ge(gu_ready, e * KC + (j + 1))
                            wait(act, sum_done, e * KC + (j - 1))
                            nc.scalar.activation(part[j % 2][:], gu_view(j, 1), ACT.Copy).then_inc(part_done, 1)
                        if t + LEAD < EXP_CHUNKS:
                            weights_hi(t + LEAD, e)
                        elif not is_last:
                            weights_hi(t + LEAD - EXP_CHUNKS, e + 1)
                        if 0 <= j < KC:
                            act.wait_ge(sum_done, e * KC + (j + 1))
                            wait(act, prod_done, e * KC + (j - 1))
                            nc.scalar.activation(silu_g[j % 2][:], gate_up_s[j % 2][:, 0, :], ACT.Silu).then_inc(silu_done, 1)
                        if t == 9 and not is_last:
                            tokens_hi(e + 1)
                if streams == 2:
                    context_part(EXPERTS - 1)

            @blk.vector
            def _(dve):
                def weights_lo(s, e):
                    dve.wait_ge(hi_done, e * EXP_CHUNKS + (s + 1))
                    nc.vector.tensor_tensor(w_lo[s % PLACES][:], core.raw[(first + s) % RING][:],
                                            w_hi[s % PLACES][:].bitcast(F32), ALU.subtract).then_inc(core.chunk_done, 1)

                def tokens_lo(e):
                    for g in range(turns):
                        bank, (ks, cols) = turn_views(g)
                        dve.wait_ge(x_hi_done, e * turns + (g + 1))
                        nc.vector.tensor_tensor(x[:, ks, 1, cols], bank, x[:, ks, 0, cols].bitcast(F32), ALU.subtract)\
                          .then_inc(x_ready, 1)

                def product(j, e):
                    dve.wait_ge(silu_done, e * KC + (j + 1))
                    wait(dve, h_ready, e * KC + (j - 1))
                    nc.vector.tensor_tensor(prod[j % 2][:], gate_up_s[j % 2][:, 1, :], silu_g[j % 2][:], ALU.mult)\
                      .then_inc(prod_done, 1)
                    dve.wait_ge(prod_done, e * KC + (j + 1))
                    nc.vector.tensor_copy(h[:, j, 0:slots], prod[j % 2][:]).then_inc(h_hi_done, 1)
                    dve.wait_ge(h_hi_done, e * KC + (j + 1))
                    if streams == 2:
                        nc.vector.tensor_tensor(h[:, j, slots:slots + SLOTS_CTX], prod[j % 2][:, SLOTS_LAT:],
                                                h[:, j, SLOTS_LAT:slots].bitcast(F32), ALU.subtract)
                    nc.vector.tensor_tensor(h[:, j, h_cols - SLOTS_LAT:], prod[j % 2][:, 0:SLOTS_LAT],
                                            h[:, j, 0:SLOTS_LAT].bitcast(F32), ALU.subtract).then_inc(h_ready, 1)

                def results(e):
                    dve.wait_ge(down_done, e * 4 + 4)
                    wait(dve, scattered, e * 16)
                    for c in range(2):
                        cols = slice(BANK * c, BANK * (c + 1))
                        nc.vector.scalar_tensor_tensor(y[:, cols], y_sum[c][:], core.gate_t[:, ds(e, 1)], g2_rows[:, 0, cols],
                                                       ALU.mult, ALU.mult).then_inc(y_ready, 1)
                    if streams == 2:
                        dve.wait_ge(ctx_part_done, e + 1)
                        wait(dve, scattered_ctx, e * 16)
                        for c in range(2):
                            cols = slice(BANK * c, BANK * (c + 1))
                            nc.vector.tensor_tensor(y_ctx[:, cols], y_ctx_sum[0:SLOTS_CTX, cols], ctx_part[:, cols], ALU.add)\
                              .then_inc(ctx_added, 1)
                            dve.wait_ge(ctx_added, e * 2 + (c + 1))
                            nc.vector.scalar_tensor_tensor(y_ctx[:, cols], y_ctx[:, cols],
                                                           core.gate_t[0:SLOTS_CTX, ds(e + 32, 1)],
                                                           g2_rows[0:SLOTS_CTX, 1, cols], ALU.mult, ALU.mult)\
                              .then_inc(y_ready, 1)

                for s in range(LEAD):
                    if s == LEAD - 1:
                        tokens_lo(0)
                    weights_lo(s, 0)
                for e, is_last in experts(nc.vector):
                    for t in range(EXP_CHUNKS):
                        j = t - 1
                        if t == 0 and (not isinstance(e, int) or e > 0):
                            results(e - 1)
                        if 0 <= j < KC:
                            dve.wait_ge(part_done, e * KC + (j + 1))
                            nc.vector.tensor_tensor(gate_up_s[j % 2][:], gu_view(j, 0), part[j % 2][:], ALU.add)\
                              .then_inc(sum_done, 1)
                        if t + LEAD < EXP_CHUNKS:
                            weights_lo(t + LEAD, e)
                        elif not is_last:
                            weights_lo(t + LEAD - EXP_CHUNKS, e + 1)
                        if 0 <= j < KC:
                            product(j, e)
                        if t == 9 and not is_last:
                            tokens_lo(e + 1)
                results(EXPERTS - 1)



def padded_place(ht):
    def into(k, t, stream):
        at = t * P + (OFF_CTX - N_LAT if stream else OFF_LAT)
        return ht[:, k:k + 4, ds(at, P)]
    return into


def pool_stage(core, ht, x, gain_rows):
    nc, io = core.nc, core.io
    tiles = T_LAT + T_CTX
    with ExitStack() as st:
        def sb(n, shape, dt=F32):
            return st.enter_context(nc.sbuf_tensor(f"pool_{n}", shape, dt))

        mod = Modulation(core, 1, st, 0, MOD_BESIDE_POOL)
        sums = [sb(f"sums{i}", [P, 2, PADDED]) for i in range(2)]
        weights = sb("weights", [P, 2 * len(WINDOWS), 2 * P])
        edge = sb("edge", [P, len(WINDOWS), 2, PAD])
        edge_mean = sb("edge_mean", [P, 2, 4, PAD])
        scaled = [sb(f"scaled{s}", [P, 2 * len(WINDOWS), 2 * P]) for s in range(2)]
        out = [st.enter_context(nc.psum_tensor(f"pool_out{i}", [P, 2, 2 * P], F32)) for i in range(4)]
        edge_loaded, loaded, step, pooled, product, weights_ready, added = (
            core.sem(f"pool_{n}") for n in ("edge_loaded", "loaded", "step", "pooled", "product", "weights_ready", "added"))
        n_pairs = tiles // 2
        units = [(g, pair) for g in range(len(WINDOWS)) for pair in range(n_pairs)]
        with core.block() as blk:
            @blk.sync
            def _(sp):
                sp.dma_start(edge[:], io["edge"].partition_broadcast(P).rearrange("p (g s c) -> p g s c", g=len(WINDOWS), s=2))\
                  .then_inc(edge_loaded, 16)
                sp.dma_start(weights[:], io["pool_w"][0].rearrange("g (k p) d -> p (g k) d", p=P)).then_inc(loaded, 16)
                mod.load(sp)

            @blk.scalar
            def _(act):
                mod.copy_out(act)

            @blk.vector
            def _(dve):
                done = [0]

                def chain(ins):
                    ins.then_inc(step, 1)
                    done[0] += 1
                    dve.wait_ge(step, done[0])

                def add_products(g):
                    for u, (_, pair) in list(enumerate(units))[g * n_pairs:(g + 1) * n_pairs]:
                        dve.wait_ge(product, u + 1)
                        xs = x[:, 2 * pair:2 * pair + 2, 2 * P * g:2 * P * (g + 1)]
                        nc.vector.tensor_tensor(xs, xs, out[u % 4][:], ALU.add).then_inc(added, 1)

                for g, w in enumerate(WINDOWS):
                    if g == len(WINDOWS) - 1:
                        add_products(0)
                    h = ht[:, 2 * g:2 * g + 2, :]
                    src, reach = h, 0
                    for level in range(g + 1):
                        dst = sums[level % 2]
                        if level == 0:
                            chain(nc.vector.tensor_tensor(dst[:, :, 1:PADDED], h[:, :, 1:PADDED], h[:, :, 0:PADDED - 1], ALU.add))
                        else:
                            n = 1 << (level - 1)
                            lo = 2 * n
                            chain(nc.vector.tensor_tensor(dst[:, :, lo:PADDED - lo + 1], src[:, :, lo - n:PADDED - lo + 1 - n],
                                                          src[:, :, lo + n:PADDED - lo + 1 + n], ALU.add))
                        src = dst
                        if g == len(WINDOWS) - 1 and level == 2:
                            add_products(1)
                    if g == 0:
                        dve.wait_ge(edge_loaded, 16)
                    ends = [OFF_LAT, OFF_LAT + N_LAT - PAD, OFF_CTX, OFF_CTX + N_CTX - PAD]
                    for i, at in enumerate(ends):
                        inv = edge[:, g, i % 2, :].unsqueeze(1).to_broadcast([P, 2, PAD])
                        chain(nc.vector.tensor_tensor(edge_mean[:, :, i, :], src[:, :, at:at + PAD], inv, ALU.mult))
                        chain(nc.vector.tensor_tensor(edge_mean[:, :, i, :], edge_mean[:, :, i, :], h[:, :, at:at + PAD],
                                                      ALU.subtract))
                    for at, n in ((OFF_LAT, N_LAT), (OFF_CTX, N_CTX)):
                        chain(nc.vector.scalar_tensor_tensor(h[:, :, at:at + n], src[:, :, at:at + n], 1.0 / w,
                                                             h[:, :, at:at + n], ALU.mult, ALU.subtract))
                    for i, at in enumerate(ends):
                        last = nc.vector.tensor_copy(h[:, :, at:at + PAD], edge_mean[:, :, i, :])
                        chain(last) if i < 3 else last.then_inc(pooled, 1)
                for g in range(2, len(WINDOWS)):
                    add_products(g)
                mod.finish(dve)

            @blk.tensor
            def _(pe):
                mod.products(pe)
                pe.wait_ge(weights_ready, 2)
                for u, (g, pair) in enumerate(units):
                    pe.wait_ge(pooled, g + 1)
                    wait(pe, added, u - 3)
                    stream = 1 if 2 * pair >= T_LAT else 0
                    for i in range(2):
                        at = (2 * pair + i) * P + (OFF_CTX - N_LAT if stream else OFF_LAT)
                        for k in range(2):
                            last = nc.tensor.matmul(out[u % 4][:, i, :], ht[:, 2 * g + k, at:at + P],
                                                    scaled[stream][:, 2 * g + k, :], start=k == 0, stop=k == 1)
                    last.then_inc(product, 1)

            @blk.gpsimd
            def _(pool):
                pool.wait_ge(loaded, 16)
                for s in range(2):
                    gain = gain_rows[:, s, :].rearrange("p (g d) -> p g d", g=len(WINDOWS)).unsqueeze(2)
                    nc.gpsimd.tensor_tensor(scaled[s][:].rearrange("p (g k) d -> p g k d", k=2),
                                            weights[:].rearrange("p (g k) d -> p g k d", k=2),
                                            gain.to_broadcast([P, len(WINDOWS), 2, 2 * P]), ALU.mult).then_inc(weights_ready, 1)



def load_lru_chunk(core, sp, first, e, i):
    w_in = core.io["lru_w_in"][0].rearrange("(k p) (s b m) -> p s k b m", p=P, s=2, m=P)
    sp.wait_ge(core.chunk_done, e * RING + (first + i + 1))
    sp.dma_start(core.raw[(first + i) % RING][:].rearrange("p (s k b m) -> p s k b m", s=2, k=KC, b=1),
                 w_in[:, :, :, ds(e * RING + i, 1), :]).then_inc(core.raw_landed[(first + i) % RING], 16)


def load_out_chunk(core, sp, first, c):
    src = (core.io["lru_w_out"][0] if c < KC // 2 else core.o_lru).rearrange("(k p) d -> p k d", p=P)
    k = 2 * (c % (KC // 2))
    load_chunk(core, sp, first + c, src[:, k:k + 2, :], lambda place: place[:].rearrange("p (k d) -> p k d", k=2))


def lru_stage(core, t_hi, t_lo, decay):
    nc, io = core.nc, core.io
    first = core.chunks
    core.chunks += KC
    half = KC * P
    unroll = RING
    segments = ((0, BANK), (BANK, BANK), (N_LAT, N_CTX))
    with ExitStack() as st:
        def sb(n, shape, dt=F32):
            return st.enter_context(nc.sbuf_tensor(f"lru_{n}", shape, dt))

        w_hi = [sb(f"w_hi{i}", [P, CHUNK], F32R) for i in range(2)]
        w_lo = sb("w_lo", [P, CHUNK], F32R)
        gw = [sb(f"gw{i}", [P, 4, P]) for i in range(2)]
        gw_hi, gw_lo = sb("gw_hi", [P, 4, P], F32R), sb("gw_lo", [P, 4, P], F32R)
        params = [sb(f"par{i}", [P, LRU_COLS + 4]) for i in range(2)]
        x, x_hi, x_lo = sb("x", [P, TOK]), sb("x_hi", [P, TOK], F32R), sb("x_lo", [P, TOK], F32R)
        r = [sb(f"r{i}", [P, TOK]) for i in range(2)]
        gi = [sb(f"i{i}", [P, TOK]) for i in range(2)]
        a = [sb(f"a{i}", [P, TOK]) for i in range(2)]
        q = [sb(f"q{i}", [P, TOK]) for i in range(2)]
        y = sb("y", [P, N_LAT])
        x_sum = st.enter_context(nc.psum_tensor("lru_x_sum", [P, 3 * BANK], F32))
        y_sum = st.enter_context(nc.psum_tensor("lru_y_sum", [P, 2 * BANK], F32))
        g_sum = [st.enter_context(nc.psum_tensor(f"lru_g_sum{i}", [P, BANK], F32)) for i in range(3)]
        (gw_landed0, gw_landed1, hi_done, gw_hi_done, gw_done, par_set, x_ready, y_ready, first_tap, conv, x_hi_done,
         x_split, y_done, gates, g_done, powers, roots, step, summed, o_ready) = (core.sem(f"lru_{n}") for n in (
             "gw_landed0", "gw_landed1", "hi_done", "gw_hi_done", "gw_done", "par_set", "x_ready", "y_ready",
             "first_tap", "conv", "x_hi_done", "x_split", "y_done", "gates", "g_done", "powers", "roots", "step", "summed",
             "o_ready"))
        gw_landed = (gw_landed0, gw_landed1)
        stored = core.lru_stored
        CONV = 6
        STEPS = 12

        def blocks(engine):
            for i in range(unroll):
                yield 0, i
            with engine.Fori(1, KC // unroll) as e:
                for i in range(unroll):
                    yield e, i

        def before(e, i):
            return (e, i - 1) if i else (e - 1, unroll - 1)

        def has_before(e, i):
            return not isinstance(e, int) or e * unroll + i > 0

        wa = io["lru_wa"][0].rearrange("d b i o -> i d b o")
        wx = io["lru_wx"][0].rearrange("d b i o -> i d b o")

        with core.block() as blk:
            @blk.sync
            def _(sp):
                for e, i in blocks(nc.sync):
                    b = e * unroll + i
                    if not isinstance(e, int) or e > 0:
                        load_lru_chunk(core, sp, first, e, i)
                    wait(sp, gw_done, e * unroll + (i - 1))
                    for s, w in enumerate((wa, wx)):
                        sp.dma_start(gw[i % 2][:, 2 * s:2 * s + 2, :].unsqueeze(2), w[:, :, ds(b, 1), :])\
                          .then_inc(gw_landed[i % 2], 16)
                for c in range(KC // 2):
                    load_out_chunk(core, sp, core.chunks, c)

            @blk.gpsimd
            def _(pool):
                lat = slice(0, N_LAT)
                with nc.gpsimd.Fori(0, KC) as b:
                    pool.wait_ge(step, b * STEPS + STEPS)
                    nc.gpsimd.tensor_tensor(r[0][:, lat], r[0][:, lat], r[1][:, lat], ALU.add).then_inc(summed, 1)
                    pool.wait_ge(summed, b + 1)
                    pool.wait_ge(y_done, b + 1)
                    nc.gpsimd.tensor_tensor(r[1][:, lat], r[0][:, lat], y[:], ALU.mult).then_inc(o_ready, 1)
                    pool.wait_ge(o_ready, b + 1)
                    pool.dma_start(core.o_lru.rearrange("(b p) t -> p b t", p=P)[:, ds(b, 1), :],
                                   r[1][:, 0:N_LAT].unsqueeze(1)).then_inc(stored, 16)
                pool.wait_ge(stored, 16 * KC)

            @blk.tensor
            def _(pe):
                for e, i in blocks(nc.tensor):
                    b = e * unroll + i
                    w = (w_hi[i % 2], w_lo)
                    chunk_done(core, pe, first + i, e, unroll)
                    wait(pe, conv, b * CONV)
                    for n, (at, size) in enumerate(segments):
                        for k in range(KC):
                            for m, (part, t) in enumerate(((0, t_hi), (0, t_lo), (1, t_hi))):
                                last = nc.tensor.matmul(x_sum[:, BANK * n:BANK * n + size],
                                                        w[part][:, half + P * k:half + P * k + P],
                                                        t[:, k, at:at + size], start=k == 0 and m == 0,
                                                        stop=k == KC - 1 and m == 2)
                    last.then_inc(x_ready, 1)
                    wait(pe, y_done, b)
                    for n in range(2):
                        for k in range(KC):
                            for m, (part, t) in enumerate(((0, t_hi), (0, t_lo), (1, t_hi))):
                                last = nc.tensor.matmul(y_sum[:, BANK * n:BANK * n + BANK], w[part][:, P * k:P * k + P],
                                                        t[:, k, BANK * n:BANK * n + BANK], start=k == 0 and m == 0,
                                                        stop=k == KC - 1 and m == 2)
                    last.then_inc(y_ready, 1)
                    pe.wait_ge(gw_done, b + 1)
                    pe.wait_ge(x_split, b + 1)
                    for g in range(4):
                        for n, (at, size) in enumerate(segments):
                            wait(pe, g_done, b * 12 + (3 * g + n - 2))
                            for m, (gate_w, t) in enumerate(((gw_hi, x_hi), (gw_hi, x_lo), (gw_lo, x_hi))):
                                last = nc.tensor.matmul(g_sum[n][:, 0:size], gate_w[:, g, :], t[:, at:at + size],
                                                        start=m == 0, stop=m == 2)
                            last.then_inc(gates, 1)

            @blk.scalar
            def _(act):
                def weights_hi(e, i):
                    landed(core, act, first + i, e, unroll)
                    wait(act, y_ready, e * unroll + (i - 1))
                    nc.scalar.activation(w_hi[i % 2][:], core.raw[i][:], ACT.Copy).then_inc(hi_done, 1)

                def gate_weights_hi(e, i):
                    act.wait_ge(gw_landed[i % 2], e * 64 + (32 * (i // 2) + 32))
                    wait(act, gates, (e * unroll + i) * 12)
                    nc.scalar.activation(gw_hi[:], gw[i % 2][:], ACT.Copy).then_inc(gw_hi_done, 1)

                def gates_and_roots(e, i):
                    b = e * unroll + i
                    par = params[i % 2]
                    act.wait_ge(conv, b * CONV + CONV)
                    nc.scalar.activation(x_hi[:], x[:], ACT.Copy).then_inc(x_hi_done, 1)
                    act.wait_ge(y_ready, b + 1)
                    wait(act, o_ready, b)
                    nc.scalar.activation(y[:], y_sum[:], ACT.Gelu_apprx_tanh).then_inc(y_done, 1)
                    act.wait_ge(par_set, b * 2 + 2)
                    for g in range(4):
                        out = (r[0], r[1], gi[0], gi[1])[g]
                        if g == 1:
                            wait(act, stored, b * 16)
                        for n, (at, size) in enumerate(segments):
                            act.wait_ge(gates, b * 12 + (3 * g + n + 1))
                            nc.scalar.activation(out[:, at:at + size], g_sum[n][:, 0:size], ACT.Sigmoid,
                                                 bias=par[:, 5 + g:6 + g]).then_inc(g_done, 1)
                    act.wait_ge(g_done, b * 12 + 6)
                    for d in range(2):
                        nc.scalar.activation(a[d][:], r[d][:], ACT.Exp,
                                             scale=par[:, LRU_COLS + 2 * d:LRU_COLS + 2 * d + 1]).then_inc(powers, 1)
                        act.wait_ge(powers, b * 4 + (2 * d + 1))
                        nc.scalar.activation(r[d][:], r[d][:], ACT.Tanh,
                                             scale=par[:, LRU_COLS + 2 * d + 1:LRU_COLS + 2 * d + 2]).then_inc(powers, 1)
                    for d in range(2):
                        act.wait_ge(step, b * STEPS + (4 + 2 * d))
                        nc.scalar.activation(q[d][:], q[d][:], ACT.Sqrt).then_inc(roots, 1)

                for e, i in blocks(nc.scalar):
                    weights_hi(e, i)
                    if has_before(e, i):
                        gates_and_roots(*before(e, i))
                    b = e * unroll + i
                    act.wait_ge(x_ready, b + 1)
                    act.wait_ge(par_set, b * 2 + 2)
                    par = params[i % 2]
                    nc.scalar.activation(x[:], x_sum[:, 0:TOK], ACT.Identity, scale=par[:, 2:3], bias=par[:, 4:5])\
                      .then_inc(first_tap, 1)
                    gate_weights_hi(e, i)
                gates_and_roots(KC // unroll - 1, unroll - 1)

            @blk.vector
            def _(dve):
                def gate_weights_lo(e, i):
                    dve.wait_ge(gw_hi_done, e * unroll + (i + 1))
                    nc.vector.tensor_tensor(gw_lo[:], gw[i % 2][:], gw_hi[:].bitcast(F32), ALU.subtract).then_inc(gw_done, 1)

                def states(e, i):
                    b = e * unroll + i
                    for d in range(2):
                        dve.wait_ge(g_done, b * 12 + (9 + 3 * d))
                        nc.vector.tensor_tensor(gi[d][:], gi[d][:], x[:], ALU.mult).then_inc(step, 1)
                    for d in range(2):
                        dve.wait_ge(powers, b * 4 + (2 * d + 1))
                        nc.vector.tensor_tensor(q[d][:], a[d][:], a[d][:], ALU.mult).then_inc(step, 1)
                        dve.wait_ge(powers, b * 4 + (2 * d + 2))
                        dve.wait_ge(step, b * STEPS + (3 + 2 * d))
                        nc.vector.scalar_tensor_tensor(q[d][:], q[d][:], 1.0, r[d][:], ALU.add, ALU.mult).then_inc(step, 1)
                    done = 6
                    for d in range(2):
                        dve.wait_ge(roots, b * 2 + (d + 1))
                        dve.wait_ge(step, b * STEPS + (d + 1))
                        nc.vector.tensor_tensor(gi[d][:], gi[d][:], q[d][:], ALU.mult).then_inc(step, 1)
                        done += 1
                        dve.wait_ge(step, b * STEPS + done)
                        turn = slice(None, None, -1) if d else slice(None)
                        c, l = slice(N_LAT, TOK), slice(0, N_LAT)
                        nc.vector.tensor_tensor_scan(r[d][:, c][:, turn], a[d][:, c][:, turn], gi[d][:, c][:, turn], 0.0,
                                                     ALU.mult, ALU.add).then_inc(step, 1)
                        done += 1
                        dve.wait_ge(step, b * STEPS + done)
                        end = N_LAT if d else TOK - 1
                        nc.vector.tensor_tensor_scan(r[d][:, l][:, turn], a[d][:, l][:, turn], gi[d][:, l][:, turn],
                                                     r[d][:, end:end + 1], ALU.mult, ALU.add).then_inc(step, 1)
                        done += 1
                    assert done == STEPS

                for e, i in blocks(nc.vector):
                    b = e * unroll + i
                    par = params[i % 2]
                    wait(dve, roots, e * (2 * unroll) + 2 * (i - 1))
                    nc.vector.tensor_copy(par[:, 0:LRU_COLS], core.vec[:, ds(b * LRU_COLS + V_LRU, LRU_COLS)]).then_inc(par_set, 1)
                    nc.vector.tensor_copy(par[:, LRU_COLS:LRU_COLS + 4], decay[:, ds(b * 4, 4)]).then_inc(par_set, 1)
                    dve.wait_ge(hi_done, b + 1)
                    wait(dve, y_ready, b)
                    nc.vector.tensor_tensor(w_lo[:], core.raw[i][:], w_hi[i % 2][:].bitcast(F32), ALU.subtract)\
                      .then_inc(core.chunk_done, 1)
                    if has_before(e, i):
                        states(*before(e, i))
                    dve.wait_ge(first_tap, b + 1)
                    seqs = ((0, N_LAT), (N_LAT, N_CTX))
                    for n, (tap, shift) in enumerate(((1, -1), (0, -2), (3, 1))):
                        for s, (at, size) in enumerate(seqs):
                            lo, hi = at + max(0, -shift), at + size - max(0, shift)
                            if n:
                                dve.wait_ge(conv, b * CONV + (2 * n + s - 1))
                            nc.vector.scalar_tensor_tensor(x[:, lo:hi], x_sum[:, lo + shift:hi + shift],
                                                           par[:, tap:tap + 1], x[:, lo:hi], ALU.mult, ALU.add)\
                              .then_inc(conv, 1)
                    gate_weights_lo(e, i)
                    dve.wait_ge(x_hi_done, b + 1)
                    nc.vector.tensor_tensor(x_lo[:], x[:], x_hi[:].bitcast(F32), ALU.subtract).then_inc(x_split, 1)
                states(KC // unroll - 1, unroll - 1)


def out_stage(core, x, gain_row, load):
    nc, io = core.nc, core.io
    first = core.chunks
    core.chunks += KC
    with ExitStack() as st:
        hi = [st.enter_context(nc.sbuf_tensor(f"out_hi{i}", [P, KC, D], F32R)) for i in range(2)]
        lo = [st.enter_context(nc.sbuf_tensor(f"out_lo{i}", [P, KC, D], F32R)) for i in range(2)]
        change = st.enter_context(nc.sbuf_tensor("out_change", [P, D], F32))
        sums = [[st.enter_context(nc.psum_tensor(f"out_sums{i}{n}", [P, BANK], F32)) for n in range(2)] for i in range(2)]
        x_landed, hi_done, product, scaled, added = (core.sem(f"out_{n}") for n in (
            "x_landed", "hi_done", "product", "scaled", "added"))
        with core.block() as blk:
            @blk.sync
            def _(sp):
                for c in range(KC // 2, KC):
                    load_out_chunk(core, sp, first, c)
                for dst, src in load:
                    sp.dma_start(dst, src).then_inc(x_landed, 16)

            @blk.scalar
            def _(act):
                for c in range(KC):
                    landed(core, act, first + c)
                    which, k = 1 - c // (KC // 2), 2 * (c % (KC // 2))
                    nc.scalar.activation(hi[which][:, k:k + 2, :],
                                         core.raw[(first + c) % RING][:].rearrange("p (k d) -> p k d", k=2), ACT.Copy)\
                      .then_inc(hi_done, 1)

            @blk.vector
            def _(dve):
                for c in range(KC):
                    dve.wait_ge(hi_done, c + 1)
                    which, k = 1 - c // (KC // 2), 2 * (c % (KC // 2))
                    nc.vector.tensor_tensor(lo[which][:, k:k + 2, :], core.raw[(first + c) % RING][:].rearrange("p (k d) -> p k d", k=2),
                                            hi[which][:, k:k + 2, :].bitcast(F32), ALU.subtract).then_inc(core.chunk_done, 1)
                dve.wait_ge(x_landed, 16 * len(load))
                for t in range(T_LAT):
                    dve.wait_ge(product, t + 1)
                    wait(dve, added, t)
                    for n in range(2):
                        nc.vector.tensor_tensor(change[:, BANK * n:BANK * n + BANK], sums[t % 2][n][:],
                                                gain_row[:, BANK * n:BANK * n + BANK], ALU.mult).then_inc(scaled, 1)
                    dve.wait_ge(scaled, 2 * t + 2)
                    nc.vector.tensor_tensor(x[:, t, :], x[:, t, :], change[:], ALU.add).then_inc(added, 1)

            @blk.tensor
            def _(pe):
                for t in range(T_LAT):
                    wait(pe, scaled, 2 * (t - 1))
                    for k in range(KC):
                        if t == 0 and k % 2 == 0:
                            chunk_done(core, pe, first + KC // 2 + k // 2)
                        for m, (o, w) in enumerate(((hi[0], hi[1]), (hi[0], lo[1]), (lo[0], hi[1]))):
                            for n in range(2):
                                last = nc.tensor.matmul(sums[t % 2][n][:], o[:, k, t * P:t * P + P],
                                                        w[:, k, BANK * n:BANK * n + BANK],
                                                        start=k == 0 and m == 0, stop=k == KC - 1 and m == 2)
                    last.then_inc(product, 1)


def final_stage(core, src, gain_row, dst):
    nc = core.nc
    with ExitStack() as st:
        x = st.enter_context(nc.sbuf_tensor("fin_x", [P, T_LAT, D], F32))
        y = st.enter_context(nc.sbuf_tensor("fin_y", [P, T_LAT, D], F32))
        squares = st.enter_context(nc.sbuf_tensor("fin_squares", [P, D], F32))
        ssq, rstd, eps = (st.enter_context(nc.sbuf_tensor(f"fin_{n}", [P, c], F32)) for n, c in (
            ("ssq", T_LAT), ("rstd", T_LAT), ("eps", 1)))
        x_landed = [core.sem(f"fin_x_landed{t}") for t in range(T_LAT)]
        squared, root, inverse, done, stored, eps_set = (core.sem(f"fin_{n}") for n in (
            "squared", "root", "inverse", "done", "stored", "eps_set"))
        with core.block() as blk:
            @blk.sync
            def _(sp):
                for t in range(T_LAT):
                    sp.dma_start(x[:, t, :], src[t * P:t * P + P, :]).then_inc(x_landed[t], 16)
                for t in range(T_LAT):
                    sp.wait_ge(done, t + 1)
                    sp.dma_start(dst[t * P:t * P + P, :], y[:, t, :]).then_inc(stored, 16)
                sp.wait_ge(stored, 16 * T_LAT)

            @blk.scalar
            def _(act):
                act.wait_ge(eps_set, 1)
                for t in range(T_LAT):
                    act.wait_ge(x_landed[t], 16)
                    wait(act, squared, t)
                    nc.scalar.activation(squares[:], x[:, t, :], ACT.Square, accum_out=ssq[:, t:t + 1]).then_inc(squared, 1)
                    act.wait_ge(squared, t + 1)
                    nc.scalar.activation(ssq[:, t:t + 1], ssq[:, t:t + 1], ACT.Sqrt, bias=eps[:], scale=1.0 / D).then_inc(root, 1)

            @blk.vector
            def _(dve):
                nc.vector.memset(eps[:], EPS).then_inc(eps_set, 1)
                for t in range(T_LAT):
                    dve.wait_ge(root, t + 1)
                    nc.vector.reciprocal(rstd[:, t:t + 1], ssq[:, t:t + 1]).then_inc(inverse, 1)
                    dve.wait_ge(inverse, t + 1)
                    nc.vector.scalar_tensor_tensor(y[:, t, :], x[:, t, :], rstd[:, t:t + 1], gain_row, ALU.mult, ALU.mult)\
                      .then_inc(done, 1)


def program(nc, io, out):
    tokens = "(t p) d -> p t d"
    with ExitStack() as st:
        core = Core(nc, io, st)
        setup(core)
        x_in = [io["x"][0], io["ctx"][0]]
        x_dram = [core.x_lat, core.x_ctx]
        spans = [slice(0, T_LAT), slice(T_LAT, T_LAT + T_CTX)]

        s_g2 = ExitStack()
        g2 = s_g2.enter_context(nc.sbuf_tensor("g2_0", [P, 2, D], F32))
        with ExitStack() as s0:
            x = s0.enter_context(nc.sbuf_tensor("x0", [P, T_LAT + T_CTX, D], F32))
            rstd = s0.enter_context(nc.sbuf_tensor("rstd0", [P, T_LAT + T_CTX], F32))
            modulation_stage(core, 0, x, [(n, x_in[s].rearrange(tokens, p=P)) for s, n in enumerate((T_LAT, T_CTX))], rstd[:])
            rows = s0.enter_context(nc.sbuf_tensor("rows0", [P, 4, D], F32))
            with ExitStack() as s1:
                ht = s1.enter_context(nc.sbuf_tensor("ht0", [P, KC, PADDED], F32))
                clear_padding(core, ht)
                norm_stage(core, "norm0a", x, None, T_LAT + T_CTX, into=padded_place(ht), rstd=rstd,
                           columns=lambda s: (core.mod_col(0, 1, s), core.mod_col(0, 0, s)))
                gains = s1.enter_context(nc.sbuf_tensor("pool_gain", [P, 2, KC], F32))
                pool_gains(core, gains)
                broadcast_rows(core, "rows0b", [(rows[:, s, :], gains[:, s, :]) for s in range(2)])
                pool_stage(core, ht, x, rows)
            scales = [(rows[:, 2 * s + n, :], core.mod_col(0, 4 - n, s)) for s in range(2) for n in range(2)]
            broadcast_rows(core, "rows0c", scales + [(g2[:, s, :], core.mod_col(0, 5, s)) for s in range(2)])
            feed_forward_choice(core, 0, 2, x, rows, [x_dram[s].rearrange(tokens, p=P) for s in range(2)])
        experts_stage(core, "moe0", 0, 2, g2, core.x_lat, core.x_ctx)
        s_g2.close()

        with ExitStack() as s0:
            t_hi = s0.enter_context(nc.sbuf_tensor("t_hi", [P, KC, TOK], F32R))
            t_lo = s0.enter_context(nc.sbuf_tensor("t_lo", [P, KC, TOK], F32R))
            with ExitStack() as s1:
                x = s1.enter_context(nc.sbuf_tensor("x1a", [P, T_LAT + T_CTX, D], F32))
                norm_stage(core, "norm1a", x, None, T_LAT + T_CTX, split=(t_hi, t_lo),
                           columns=lambda s: (core.mod_col(1, 1, s), core.mod_col(1, 0, s)),
                           load=tile_pairs(x, x_dram[0].rearrange(tokens, p=P))
                           + [(x[:, spans[1], :], x_dram[1].rearrange(tokens, p=P))],
                           prefetch=lambda sp: [load_lru_chunk(core, sp, core.chunks, 0, i) for i in range(RING)])
            lru_stage(core, t_hi, t_lo, core.decay)
        with ExitStack() as s_rows:
            gain = s_rows.enter_context(nc.sbuf_tensor("gain_row", [P, D], F32))
            g2 = s_rows.enter_context(nc.sbuf_tensor("g2_1", [P, 1, D], F32))
            with ExitStack() as s0:
                x = s0.enter_context(nc.sbuf_tensor("x1b", [P, T_LAT, D], F32))
                broadcast_rows(core, "rows1b", [(gain[:], core.mod_col(1, 2, 0))])
                out_stage(core, x, gain[:], [(x[:], core.x_lat.rearrange(tokens, p=P))])
                rows = s0.enter_context(nc.sbuf_tensor("rows1b", [P, 2, D], F32))
                broadcast_rows(core, "rows1c", [(rows[:, n, :], core.mod_col(1, 4 - n, 0)) for n in range(2)]
                               + [(g2[:, 0, :], core.mod_col(1, 5, 0)), (gain[:], core.vec[:, V_FG:V_FG + KC])])
                feed_forward_choice(core, 1, 1, x, rows, [core.x_fin.rearrange(tokens, p=P)])
            experts_stage(core, "moe1", 1, 1, g2, core.x_fin, None)
            final_stage(core, core.x_fin, gain[:], out)


def tile_pairs(x, src):
    return [(x[:, 0:2, :], src[:, 0:2, :]), (x[:, 2:T_LAT, :], src[:, 2:T_LAT, :])]


def clear_padding(core, ht):
    nc = core.nc
    cleared = core.sem("padding_cleared")
    with core.block() as blk:
        @blk.vector
        def _(dve):
            gaps = ((0, OFF_LAT), (OFF_LAT + N_LAT, OFF_CTX), (OFF_CTX + N_CTX, PADDED))
            for a, b in gaps:
                nc.vector.memset(ht[:, :, a:b], 0.0).then_inc(cleared, 1)
            dve.wait_ge(cleared, len(gaps))


def pool_gains(core, gains):
    nc = core.nc
    made = core.sem("pool_gains_made")
    with core.block() as blk:
        @blk.vector
        def _(dve):
            for s in range(2):
                nc.vector.tensor_tensor(gains[:, s, :], core.vec[:, V_PS:V_PS + KC], core.mod_col(0, 2, s), ALU.mult)\
                  .then_inc(made, 1)
            dve.wait_ge(made, 2)


def feed_forward_choice(core, block, streams, x, rows, seed):
    nc, io = core.nc, core.io
    with ExitStack() as st:
        w_router = st.enter_context(nc.sbuf_tensor(f"w_router{block}", [P, KC, EXPERTS], F32))
        logits = st.enter_context(nc.psum_tensor(f"logits{block}", [P, BANK], F32))
        norm_stage(core, f"norm{block}b", x, rows, T_LAT + (T_CTX if streams == 2 else 0), router=(w_router, logits),
                   extra=[(w_router[:], io["moe_router"][block].rearrange("(k p) e -> p k e", p=P))], seed=seed)
        beside = None
        if block == 0:
            beside = Modulation(core, 1, st, MOD_BESIDE_POOL, 6 * D // BANK - MOD_BESIDE_POOL)
        choice_stage(core, f"choice{block}", block, logits, streams, beside)


_INS = ("x", "ctx", "vecs", "mod_b", "edge", "mod_w", "pool_w", "lru_w_in", "lru_wa", "lru_wx", "lru_w_out",
        "moe_router", "moe_w_gate", "moe_w_up", "moe_w_down")


def kernel(**inputs):
    import numpy as np
    import concourse.bacc as bacc
    from concourse.bass_utils import run_bass_kernel_spmd

    inputs = {name: np.asarray(a) for name, a in inputs.items()}

    def by_block(name, d=None):
        return inputs[name][0].reshape(-1, KC, P).transpose(1, 0, 2)

    lru = np.concatenate([by_block(n) for n in ("lru_conv_w", "lru_conv_b", "lru_ba", "lru_bx", "lru_lam")], axis=1)
    inputs["vecs"] = np.concatenate([inputs[n].reshape(-1, P) for n in ("c", "c_ctx", "pool_scale", "final_gain")]
                                    + [lru.reshape(-1, P)], axis=0)
    inputs["mod_b"] = inputs["mod_b"].reshape(-1, P)
    edge = np.zeros((len(WINDOWS), 2, PAD), np.float32)
    for g, w in enumerate(WINDOWS):
        for c in range(PAD):
            edge[g, 0, c] = 1.0 / min(w, c + w // 2)
            edge[g, 1, c] = 1.0 / min(w, PAD - c + w // 2)
    inputs["edge"] = edge.reshape(-1)

    nc = bacc.Bacc("TRN2", target_bir_lowering=False, num_devices=1)
    arrays, io = {}, {}
    for name in _INS:
        a = np.ascontiguousarray(inputs[name])
        arrays[f"in_{name}"] = a
        io[name] = nc.dram_tensor(f"in_{name}", a.shape, mybir.dt.from_np(a.dtype), kind="ExternalInput").ap()
    out = nc.dram_tensor("out_x", (1, N_LAT, D), F32, kind="ExternalOutput").ap()
    program(nc, io, out[0])
    result = run_bass_kernel_spmd(nc, [arrays], core_ids=[0])
    return result.results[0]["out_x"]
```
